# Optimizing a Trainium2 kernel written in Bass

```python
import math
import jax
import jax.numpy as jnp
from jax import lax
import numpy as np

D_MODEL = 1024
BATCH = 1
SEQ = 1024
DEPTH = 1

GRID_W = 64
CTX_LEN = 256
EPS = 1e-6
ROPE_THETA = 10000.0
Q_BLOCK = 128

BRANCH_WIDTH = D_MODEL // 2
N_BRANCH = 3
DA_HEADS = 4
DA_V_DIM = BRANCH_WIDTH // DA_HEADS
DA_QK_DIM = DA_V_DIM // 2
POOL_WINDOWS = (2, 4, 8, 16)
POOL_GROUPS = 4
POOL_GROUP = BRANCH_WIDTH // POOL_GROUPS
WA_HEAD_DIM = 64
WA_HEADS = BRANCH_WIDTH // WA_HEAD_DIM
WA_KV_HEADS = 2
WA_GROUP = WA_HEADS // WA_KV_HEADS
WA_WINDOW = 128
WA_BLOCK = 128
D_FF = ((8 * D_MODEL + 3 * 256 - 1) // (3 * 256)) * 256
IN_SPLITS = (
    DA_HEADS * 2 * DA_QK_DIM,
    DA_HEADS * 2 * DA_QK_DIM,
    DA_HEADS * DA_V_DIM,
    BRANCH_WIDTH,
    WA_HEADS * WA_HEAD_DIM,
    WA_KV_HEADS * WA_HEAD_DIM,
    WA_KV_HEADS * WA_HEAD_DIM,
    N_BRANCH * D_MODEL,
)
IN_WIDTH = (3 * DA_HEADS * 2 * DA_QK_DIM - DA_HEADS * 2 * DA_QK_DIM + DA_HEADS * DA_V_DIM
            + BRANCH_WIDTH + WA_HEADS * WA_HEAD_DIM + 2 * WA_KV_HEADS * WA_HEAD_DIM
            + N_BRANCH * D_MODEL)

kernel_name = 'hybrid_diffattn_pool_swa_adaln_block'

def rms_norm(x, g):
    xf = x.astype(jnp.float32)
    y = xf * lax.rsqrt(jnp.mean(xf * xf, axis=-1, keepdims=True) + EPS)
    return (y * g.astype(jnp.float32)).astype(x.dtype)

def modulate(x, g, shift, scale):
    return rms_norm(x, g) * (1 + scale) + shift

def axial_rope_tables(n, dim):
    rows = n // GRID_W
    row = jnp.repeat(jnp.arange(rows, dtype=jnp.float32), GRID_W)
    col = jnp.tile(jnp.arange(GRID_W, dtype=jnp.float32), rows)
    n_freq = dim // 4
    inv = ROPE_THETA ** (-jnp.arange(n_freq, dtype=jnp.float32) / n_freq)
    ang = jnp.concatenate([row[:, None] * inv, col[:, None] * inv], axis=-1)
    return jnp.cos(ang), jnp.sin(ang)

def apply_rope(x, cos, sin):
    shp = (cos.shape[0],) + (1,) * (x.ndim - 3) + (cos.shape[1],)
    cs = cos.reshape(shp).astype(x.dtype)
    sn = sin.reshape(shp).astype(x.dtype)
    x1 = x[..., 0::2]
    x2 = x[..., 1::2]
    return jnp.stack([x1 * cs - x2 * sn, x1 * sn + x2 * cs], axis=-1).reshape(x.shape)

def split_mixer_inputs(z):
    b, n = z.shape[:2]
    parts = []
    start = 0
    for w in IN_SPLITS:
        parts.append(z[..., start:start + w])
        start += w
    qa, ka, va, u, qw, kw, vw, gates = parts
    return (qa.reshape(b, n, DA_HEADS, 2, DA_QK_DIM),
            ka.reshape(b, n, DA_HEADS, 2, DA_QK_DIM),
            va.reshape(b, n, DA_HEADS, DA_V_DIM),
            u,
            qw.reshape(b, n, WA_HEADS, WA_HEAD_DIM),
            kw.reshape(b, n, WA_KV_HEADS, WA_HEAD_DIM),
            vw.reshape(b, n, WA_KV_HEADS, WA_HEAD_DIM),
            gates)

def diff_attention(q, k, v, lam, g_sub, lam_init):
    b, nq = q.shape[:2]
    nb = nq // Q_BLOCK
    qb = q.reshape((b, nb, Q_BLOCK) + q.shape[2:]).swapaxes(0, 1)
    scale = DA_QK_DIM ** -0.5

    def one(qblk):
        s = jnp.einsum('bqhsd,bkhsd->bhsqk', qblk, k).astype(jnp.float32) * scale
        p = jax.nn.softmax(s, axis=-1)
        a = p[:, :, 0] - lam * p[:, :, 1]
        return jnp.einsum('bhqk,bkhe->bqhe', a.astype(v.dtype), v)

    o = lax.map(one, qb).swapaxes(0, 1).reshape(b, nq, DA_HEADS, DA_V_DIM)
    o = rms_norm(o, g_sub) * (1 - lam_init)
    return o.reshape(b, nq, DA_HEADS * DA_V_DIM)

def multiscale_pool(u, w_pool, pool_scale):
    b, n, _ = u.shape
    uf = u.reshape(b, n, POOL_GROUPS, POOL_GROUP).astype(jnp.float32)
    csum = jnp.concatenate([jnp.zeros((b, 1, POOL_GROUPS, POOL_GROUP), jnp.float32),
                            lax.cumsum(uf, axis=1)], axis=1)
    w = jnp.array(POOL_WINDOWS, dtype=jnp.int32)
    t = jnp.arange(n, dtype=jnp.int32)[:, None]
    lo = jnp.clip(t - w // 2, 0, n)
    hi = jnp.clip(t + w - w // 2, 0, n)
    grp = jnp.arange(POOL_GROUPS)[None, :]
    wsum = csum[:, hi, grp] - csum[:, lo, grp]
    count = (hi - lo).astype(jnp.float32)[..., None]
    pooled = (wsum / count - uf).astype(u.dtype)
    y = jnp.einsum('bngc,gcd->bngd', pooled, w_pool).reshape(b, n, BRANCH_WIDTH)
    return y * pool_scale

def sink_softmax(s, sink):
    sk = sink.astype(jnp.float32)[:, :, None, None]
    m = jnp.maximum(jnp.max(s, axis=-1, keepdims=True), sk)
    e = jnp.exp(s - m)
    return e / (jnp.sum(e, axis=-1, keepdims=True) + jnp.exp(sk - m))

def window_sink_attention(q, k, v, kc, vc, sink):
    b, n = q.shape[:2]
    nb = n // WA_BLOCK
    pad = ((0, 0), (WA_BLOCK, WA_BLOCK), (0, 0), (0, 0))
    kp = jnp.pad(k, pad)
    vp = jnp.pad(v, pad)
    qb = q.reshape(b, nb, WA_BLOCK, WA_KV_HEADS, WA_GROUP, WA_HEAD_DIM).swapaxes(0, 1)
    sink_g = sink.reshape(WA_KV_HEADS, WA_GROUP)
    scale = WA_HEAD_DIM ** -0.5
    band = 3 * WA_BLOCK
    rel = jnp.arange(band)[None, :] - WA_BLOCK - jnp.arange(WA_BLOCK)[:, None]
    band_ok = jnp.abs(rel) <= WA_WINDOW

    def one(args):
        i, qblk = args
        kb = lax.dynamic_slice_in_dim(kp, i * WA_BLOCK, band, axis=1)
        vb = lax.dynamic_slice_in_dim(vp, i * WA_BLOCK, band, axis=1)
        kpos = (i - 1) * WA_BLOCK + jnp.arange(band)
        ok = band_ok & ((kpos >= 0) & (kpos < n))[None, :]
        s_band = jnp.einsum('bqkgd,bjkd->bkgqj', qblk, kb).astype(jnp.float32) * scale
        s_band = jnp.where(ok, s_band, -jnp.inf)
        s_ctx = jnp.einsum('bqkgd,bjkd->bkgqj', qblk, kc).astype(jnp.float32) * scale
        p = sink_softmax(jnp.concatenate([s_band, s_ctx], axis=-1), sink_g)
        vv = jnp.concatenate([vb, vc], axis=1)
        return jnp.einsum('bkgqj,bjkd->bqkgd', p.astype(v.dtype), vv)

    o = lax.map(one, (jnp.arange(nb, dtype=jnp.int32), qb))
    return o.swapaxes(0, 1).reshape(b, n, WA_HEADS * WA_HEAD_DIM)

def context_sink_attention(q, k, v, sink):
    b, n = q.shape[:2]
    qg = q.reshape(b, n, WA_KV_HEADS, WA_GROUP, WA_HEAD_DIM)
    s = jnp.einsum('bqkgd,bjkd->bkgqj', qg, k).astype(jnp.float32) * WA_HEAD_DIM ** -0.5
    p = sink_softmax(s, sink.reshape(WA_KV_HEADS, WA_GROUP))
    o = jnp.einsum('bkgqj,bjkd->bqkgd', p.astype(v.dtype), v)
    return o.reshape(b, n, WA_HEADS * WA_HEAD_DIM)

def merge_branches(ya, yb, yc, gates, w_branch, w_out):
    b, n = gates.shape[:2]
    g = jax.nn.sigmoid(gates.reshape(b, n, N_BRANCH, D_MODEL))
    m = (g[:, :, 0] * (ya @ w_branch[0]) + g[:, :, 1] * (yb @ w_branch[1])
         + g[:, :, 2] * (yc @ w_branch[2]))
    return m @ w_out

def swiglu(h, w_in, w_out):
    gate, up = jnp.split(h @ w_in, 2, axis=-1)
    return (jax.nn.silu(gate) * up) @ w_out

def setup_inputs(seed: int = 0) -> dict:
    key = jax.random.key(seed)
    ks = jax.random.split(key, 17)

    def nrm(k, shape, s):
        return jax.random.normal(k, shape, jnp.float32) * s

    return {
        'x': nrm(ks[0], (BATCH, SEQ, D_MODEL), 1.0),
        'c': nrm(ks[1], (BATCH, D_MODEL), 1.0),
        'ctx': nrm(ks[2], (BATCH, CTX_LEN, D_MODEL), 1.0),
        'c_ctx': nrm(ks[3], (D_MODEL,), 1.0),
        'w_ada': nrm(ks[4], (DEPTH, D_MODEL, 6 * D_MODEL), 0.5 * D_MODEL ** -0.5),
        'b_ada': nrm(ks[5], (DEPTH, 6 * D_MODEL), 0.02),
        'norm_g': 1.0 + nrm(ks[6], (DEPTH, 4, D_MODEL), 0.02),
        'w_in': nrm(ks[7], (DEPTH, D_MODEL, IN_WIDTH), D_MODEL ** -0.5),
        'da_lambda': nrm(ks[8], (DEPTH, 4, DA_QK_DIM), 0.1),
        'da_subln_g': 1.0 + nrm(ks[9], (DEPTH, DA_V_DIM), 0.02),
        'pool_w': nrm(ks[10], (DEPTH, POOL_GROUPS, POOL_GROUP, POOL_GROUP), POOL_GROUP ** -0.5),
        'pool_scale': 1.0 + nrm(ks[11], (DEPTH, BRANCH_WIDTH), 0.02),
        'wa_sink': nrm(ks[12], (DEPTH, WA_HEADS), 0.5),
        'w_branch': nrm(ks[13], (DEPTH, N_BRANCH, BRANCH_WIDTH, D_MODEL), BRANCH_WIDTH ** -0.5),
        'w_out': nrm(ks[14], (DEPTH, D_MODEL, D_MODEL), D_MODEL ** -0.5),
        'w_ffn_in': nrm(ks[15], (DEPTH, D_MODEL, 2 * D_FF), D_MODEL ** -0.5),
        'w_ffn_out': nrm(ks[16], (DEPTH, D_FF, D_MODEL), D_FF ** -0.5),
    }

def reference(x, c, ctx, c_ctx, w_ada, b_ada, norm_g, w_in, da_lambda, da_subln_g,
              pool_w, pool_scale, wa_sink, w_branch, w_out, w_ffn_in, w_ffn_out):
    n = x.shape[1]
    cos_a, sin_a = axial_rope_tables(n, DA_QK_DIM)
    cos_w, sin_w = axial_rope_tables(n, WA_HEAD_DIM)
    xc = ctx
    for l in range(DEPTH):
        mod_x = jnp.split((jax.nn.silu(c) @ w_ada[l] + b_ada[l])[:, None, :], 6, axis=-1)
        mod_c = jnp.split((jax.nn.silu(c_ctx) @ w_ada[l] + b_ada[l])[None, None, :], 6, axis=-1)
        lam_init = 0.8 - 0.6 * math.exp(-0.3 * l)
        lp = da_lambda[l].astype(jnp.float32)
        lam = jnp.exp(jnp.sum(lp[0] * lp[1])) - jnp.exp(jnp.sum(lp[2] * lp[3])) + lam_init

        hc = modulate(xc, norm_g[l, 0], mod_c[0], mod_c[1])
        qac, kac, vac, uc, qwc, kwc, vwc, gatec = split_mixer_inputs(hc @ w_in[l])

        h = modulate(x, norm_g[l, 0], mod_x[0], mod_x[1])
        qa, ka, va, u, qw, kw, vw, gate = split_mixer_inputs(h @ w_in[l])
        qa = apply_rope(qa, cos_a, sin_a)
        ka = apply_rope(ka, cos_a, sin_a)
        qw = apply_rope(qw, cos_w, sin_w)
        kw = apply_rope(kw, cos_w, sin_w)
        ya = diff_attention(qa, jnp.concatenate([ka, kac], axis=1),
                            jnp.concatenate([va, vac], axis=1), lam, da_subln_g[l], lam_init)
        yb = multiscale_pool(u, pool_w[l], pool_scale[l])
        yc = window_sink_attention(qw, kw, vw, kwc, vwc, wa_sink[l])
        mix = merge_branches(ya, yb, yc, gate, w_branch[l], w_out[l])
        x = x + mod_x[2] * rms_norm(mix, norm_g[l, 1])
        h2 = modulate(x, norm_g[l, 2], mod_x[3], mod_x[4])
        x = x + mod_x[5] * rms_norm(swiglu(h2, w_ffn_in[l], w_ffn_out[l]), norm_g[l, 3])

        if l < DEPTH - 1:
            yac = diff_attention(qac, kac, vac, lam, da_subln_g[l], lam_init)
            ybc = multiscale_pool(uc, pool_w[l], pool_scale[l])
            ycc = context_sink_attention(qwc, kwc, vwc, wa_sink[l])
            mixc = merge_branches(yac, ybc, ycc, gatec, w_branch[l], w_out[l])
            xc = xc + mod_c[2] * rms_norm(mixc, norm_g[l, 1])
            h2c = modulate(xc, norm_g[l, 2], mod_c[3], mod_c[4])
            xc = xc + mod_c[5] * rms_norm(swiglu(h2c, w_ffn_in[l], w_ffn_out[l]), norm_g[l, 3])
    return x


_drawn_inputs = setup_inputs


def setup_inputs(seed=0):
    import zlib

    import numpy as np

    out = dict(_drawn_inputs(seed))
    spreads = {}
    factors = {'norm_g': 4.145, 'da_lambda': 5.024, 'da_subln_g': 8.0, 'pool_scale': 8.0, 'wa_sink': 8.0}
    for name, (base, spread) in spreads.items():
        noise = np.random.default_rng([zlib.crc32(name.encode()), seed]).standard_normal(out[name].shape)
        drawn = base * np.exp(spread * noise) if base else spread * noise
        out[name] = jnp.asarray(drawn.astype(out[name].dtype))
    for name, factor in factors.items():
        out[name] = (out[name] * factor).astype(out[name].dtype)
    return out
```

```python
import math
from contextlib import ExitStack

import numpy as np

import concourse.bass as bass
from concourse import mybir

F32 = mybir.dt.float32
F32R = mybir.dt.float32r
ALU = mybir.AluOpType
ACT = mybir.ActivationFunctionType
AX = mybir.AxisListType

P = 128
D = 1024
SEQ = 1024
CTX = 256
TOK = SEQ + CTX
KC = D // P
TL = SEQ // P
TT = TOK // P
HALF = 512
NH = SEQ // HALF
GRID_W = 64
EPS = 1e-6
ROPE_THETA = 10000.0
HD = 64
DA_HEADS = 4
DA_V = 128
WA_HEADS = 8
WA_KV = 2
WA_GROUP = WA_HEADS // WA_KV
BW = 512
BC = BW // P
POOL_WINDOWS = (2, 4, 8, 16)
D_FF = ((8 * D + 3 * 256 - 1) // (3 * 256)) * 256
FC = D_FF // P
LAM_INIT = 0.8 - 0.6 * math.exp(-0.3 * 0)
SCALE = HD ** -0.5
MASKED = -1e30
GW = 3 * P
UNITS = 6


def parts_product(pe, out, stat, mov, first, last):
    (sh, sl), (mh, ml) = stat, mov
    pe.matmul(out, sh, mh, start=first, stop=False)
    pe.matmul(out, sh, ml, start=False, stop=False)
    return pe.matmul(out, sl, mh, start=False, stop=last)


class Chain:

    def __init__(self, eng, sem, base=0):
        self.eng, self.sem, self.base, self.n = eng, sem, base, 0

    def did(self, ins):
        ins.then_inc(self.sem, 1)
        self.n += 1

    def settle(self):
        self.eng.wait_ge(self.sem, self.base + self.n)

    def link(self, ins):
        self.did(ins)
        self.settle()


def prepare(nc, sem, banks, io, keep):
    h_hi, h_lo, ident, neg_lam, sub_g = keep["h_hi"], keep["h_lo"], keep["ident"], keep["neg_lam"], keep["sub_g"]
    ADA = 4
    UN = [(c, k) for c in range(3) for k in range(KC)]
    with ExitStack() as ctx:
        sb = lambda n, s, d=F32: ctx.enter_context(nc.sbuf_tensor(n, s, d))
        xt = sb("xt", [P, TT, D])
        ada = [sb(f"ada{j}", [P, KC, HALF]) for j in range(ADA)]
        junk = sb("junk", [P, D])
        full = sb("full", [P, 2, HALF])
        cond = sb("cond", [P, 2, KC])
        econd = sb("econd", [P, 2, KC])
        silu = sb("silu", [P, KC, 2])
        ada_b = sb("ada_b", [P, 48])
        norm_g = sb("norm_g", [P, 4, KC])
        mod = sb("mod", [P, 2 * KC, 2])
        A = sb("A", [P, KC, 2])
        lamv = sb("lamv", [P, 4, HD])
        lamp = sb("lamp", [P, 2, HD])
        lamd = sb("lamd", [P, 4])
        ss = sb("ss", [P, TT])
        rs = sb("rs", [P, TT])
        small_in, x_in = sem("pr_small_in"), [sem(f"pr_x_in{j}") for j in range(3)]
        ada_in = [sem(f"pr_ada_in{j}") for j in range(ADA)]
        e_ready, silu_ready, ada_done, ab_ready = sem("pr_e"), sem("pr_silu"), sem("pr_ada_done"), sem("pr_ab")
        sq_done, mean_ready, rs_ready, xn_ready = sem("pr_sq"), sem("pr_mean"), sem("pr_rs"), sem("pr_xn")
        turned, full_ready, h_ready, dve, act_own = sem("pr_turned"), sem("pr_full"), sem("pr_h"), sem("pr_dve"), sem("pr_act")
        lam_dots, lam_exp = sem("pr_lam_dots"), sem("pr_lam_exp")
        CH = [range(0, 4), range(4, 8), range(8, 10)]

        block = ctx.enter_context(nc.Block())

        @block.sync
        def _(sp):
            for dst, src in ((cond, io["cT"]), (ada_b, io["b_adaT"]), (norm_g, io["norm_gT"]), (ident, io["ident"]),
                             (sub_g, io["sub_g"])):
                sp.dma_start(dst[:], src).then_inc(small_in, 16)
            sp.dma_start(lamv[:].rearrange("p a b -> p (a b)"),
                         io["da_lambda"].to_broadcast([P, 4 * HD])).then_inc(small_in, 16)
            xv = io["x"].rearrange("(t p) d -> p t d", p=P)
            cv = io["ctx"].rearrange("(t p) d -> p t d", p=P)
            av = io["w_ada"].rearrange("(k p) n -> p k n", p=P)
            sp.dma_start(xt[:, 0:4, :], xv[:, 0:4, :]).then_inc(x_in[0], 16)
            for j in range(ADA):
                sp.dma_start(ada[j][:], av[:, :, j * HALF:(j + 1) * HALF]).then_inc(ada_in[j], 16)
                if j == 1:
                    sp.dma_start(xt[:, 4:8, :], xv[:, 4:8, :]).then_inc(x_in[1], 16)
                    sp.dma_start(xt[:, 8:10, :], cv).then_inc(x_in[2], 16)

        @block.tensor
        def _(pe):
            pe.wait_ge(silu_ready, 1)
            for j in range(ADA):
                pe.wait_ge(ada_in[j], 16)
                for b in range(4):
                    n = 4 * j + b
                    for k in range(KC):
                        mm = pe.matmul(banks[7][:, 2 * n:2 * n + 2], ada[j][:, k, b * P:(b + 1) * P], silu[:, k, :],
                                       start=(k == 0), stop=(k == KC - 1))
            mm.then_inc(ada_done, 1)
            for u, (c, k) in enumerate(UN):
                pe.wait_ge(xn_ready, [4, 8, 10][c])
                if u >= 4:
                    pe.wait_ge(full_ready, u - 3)
                for j, t in enumerate(CH[c]):
                    mm = pe.transpose(banks[u % 4][:, j * P:(j + 1) * P], xt[:, t, k * P:(k + 1) * P], ident[:])
                mm.then_inc(turned, 1)

        @block.scalar
        def _(act):
            act.wait_ge(small_in, 96)
            act.activation(econd[:], cond[:], ACT.Exp, scale=-1.0).then_inc(e_ready, 1)
            act.wait_ge(lam_dots, 1)
            act.activation(lamd[:, 2:4], lamd[:, 0:2], ACT.Exp).then_inc(lam_exp, 1)
            for t in range(TT):
                if t in (0, 4, 8):
                    act.wait_ge(x_in[t // 4], 16)
                if t:
                    act.wait_ge(sq_done, t)
                act.activation(junk[:], xt[:, t, :], ACT.Square, accum_out=ss[:, t:t + 1]).then_inc(sq_done, 1)
                if t == CH[t // 4][-1]:
                    act.wait_ge(mean_ready, t // 4 + 1)
                    act.activation(rs[:, t // 4 * 4:t + 1], ss[:, t // 4 * 4:t + 1], ACT.Sqrt).then_inc(rs_ready, 1)
            act.wait_ge(ab_ready, 2)
            for u, (c, k) in enumerate(UN):
                w = len(CH[c]) * P
                act.wait_ge(turned, u + 1)
                if u >= 2:
                    act.wait_ge(h_ready, u - 1)
                i = 1 if c == 2 else 0
                act.activation(full[:, u % 2, 0:w], banks[u % 4][:, 0:w], ACT.Identity, scale=A[:, k, i:i + 1],
                               bias=mod[:, k, i:i + 1]).then_inc(full_ready, 1)

        @block.vector
        def _(v):
            ch = Chain(v, dve)
            v.wait_ge(small_in, 96)
            v.wait_ge(e_ready, 1)
            ch.link(v.tensor_scalar(econd[:], econd[:], 1.0, None, ALU.add))
            ch.link(v.reciprocal(econd[:], econd[:]))
            v.tensor_tensor(silu[:].rearrange("p k c -> p c k"), cond[:], econd[:], ALU.mult).then_inc(silu_ready, 1)
            ch.link(v.tensor_tensor(keep["silu_x"][:], cond[:, 0, :], econd[:, 0, :], ALU.mult))
            for i in range(2):
                ins = v.tensor_tensor_reduce(out=lamp[:, i, :], in0=lamv[:, 2 * i, :], in1=lamv[:, 2 * i + 1, :],
                                             scale=1.0, scalar=0.0, op0=ALU.mult, op1=ALU.add,
                                             accum_out=lamd[:, i:i + 1])
            ins.then_inc(lam_dots, 1)
            v.wait_ge(lam_exp, 1)
            ch.did(v.scalar_tensor_tensor(out=neg_lam[:], in0=lamd[:, 3:4], scalar=-LAM_INIT, in1=lamd[:, 2:3],
                                          op0=ALU.add, op1=ALU.subtract))
            ch.link(v.tensor_scalar(sub_g[:], sub_g[:], 1.0 - LAM_INIT, None, ALU.mult))
            for c in range(3):
                a, b = CH[c][0], CH[c][-1] + 1
                v.wait_ge(sq_done, b)
                v.tensor_scalar(ss[:, a:b], ss[:, a:b], 1.0 / D, EPS, ALU.mult, ALU.add).then_inc(mean_ready, 1)
                v.wait_ge(rs_ready, c + 1)
                ch.link(v.reciprocal(rs[:, a:b], rs[:, a:b]))
                for t in CH[c]:
                    v.tensor_scalar(xt[:, t, :], xt[:, t, :], rs[:, t:t + 1], None, ALU.mult).then_inc(xn_ready, 1)
            v.wait_ge(ada_done, 1)
            for i in range(2):
                ch.did(v.tensor_tensor(mod[:, :, i], banks[7][:, i:4 * KC:2], ada_b[:, 0:2 * KC], ALU.add))
            ch.settle()
            for i in range(2):
                v.scalar_tensor_tensor(out=A[:, :, i], in0=mod[:, KC:2 * KC, i], scalar=1.0, in1=norm_g[:, 0, :],
                                       op0=ALU.add, op1=ALU.mult).then_inc(ab_ready, 1)
            for u, (c, k) in enumerate(UN):
                w, t0 = len(CH[c]) * P, CH[c][0] * P
                v.wait_ge(full_ready, u + 1)
                ch.link(v.tensor_copy(h_hi[:, k, t0:t0 + w], full[:, u % 2, 0:w]))
                v.tensor_tensor(h_lo[:, k, t0:t0 + w], full[:, u % 2, 0:w], h_hi[:, k, t0:t0 + w].bitcast(F32),
                                ALU.subtract).then_inc(h_ready, 1)


def project(nc, sem, banks, io, keep):
    h_hi, h_lo, ident = keep["h_hi"], keep["h_lo"], keep["ident"]
    with ExitStack() as ctx:
        sb = lambda n, s, d=F32: ctx.enter_context(nc.sbuf_tensor(n, s, d))
        w_raw = [sb(f"w_raw{j}", [P, KC, GW]) for j in range(2)]
        w_hi = [sb(f"w_hi{j}", [P, KC, GW], F32R) for j in range(2)]
        w_lo = [sb(f"w_lo{j}", [P, KC, GW], F32R) for j in range(2)]
        cosT, sinT = sb("cosT", [P, TL, HD]), sb("sinT", [P, TL, HD])
        raw = [sb(f"raw{j}", [P, GW]) for j in range(2)]
        rot = sb("rot", [P, UNITS, HD])
        swp = sb("swp", [P, UNITS, HD])
        cut = [sb(f"cut{j}", [P, UNITS, 2, HD], F32R) for j in range(2)]
        v_cut = [sb(f"v_cut{j}", [P, 2 * P], F32R) for j in range(2)]
        st = [sb(f"st{j}", [P, UNITS, P], F32R) for j in range(2)]
        table_in, w_in = sem("pj_table_in"), [sem(f"pj_w_in{j}") for j in range(2)]
        w_hi_ready, w_lo_ready = sem("pj_w_hi"), sem("pj_w_lo")
        acc_done, raw_ready, cut_ready = sem("pj_acc"), sem("pj_raw"), sem("pj_cut")
        turned, st_ready, dve = sem("pj_turned"), sem("pj_st"), sem("pj_dve")
        st_out, v_out = [sem(f"pj_st_out{j}") for j in range(2)], [sem(f"pj_v_out{j}") for j in range(2)]

        def content(kind, t):
            if kind == "q":
                return 0, 6, False
            return (0, 4, True) if t < TL else (P, 2, True)

        def tiles(kind):
            return TL if kind == "q" else TT

        LOOP_KINDS, LAST_KINDS = ("kv", "kv"), ("kv", "q")
        LAST = 2

        def item(it, j, t):
            return (it * 2 + j) * TT + t

        def uses(it, j, t):
            return (it * 2 + j) * (TT // 2) + t // 2

        CR = 2
        block = ctx.enter_context(nc.Block())

        @block.sync
        def _(sp):
            sp.dma_start(cosT[:], io["cosT"]).then_inc(table_in, 16)
            sp.dma_start(sinT[:], io["sinT"]).then_inc(table_in, 16)
            for j in range(2):
                sp.dma_start(w_raw[j][:], io["w_tok"][j]).then_inc(w_in[j], 16)

            def turn(it, kinds, stacks, more):
                for j, kind in enumerate(kinds):
                    if more:
                        sp.wait_ge(w_lo_ready, (it * 2 + j + 1) * KC)
                        sp.dma_start(w_raw[j][:], io["w_tok"][it * 2 + j + 2]).then_inc(w_in[j], 16)
                    for t in range(tiles(kind)):
                        col, units, has_v = content(kind, t)
                        skip = 4 - units if kind == "kv" else 0
                        if has_v:
                            sp.wait_ge(cut_ready, item(it, j, t) + 1 + CR)
                            sp.dma_start(io["vals"][it * 2 + j, t], v_cut[t % 2][:].bitcast(F32)).then_inc(v_out[t % 2], 16)
                        sp.wait_ge(st_ready, item(it, j, t) + 1 + CR)
                        sp.dma_start(stacks(j)[skip:skip + units, :, t * P:(t + 1) * P].rearrange("u p n -> p u n"),
                                     st[t % 2][:, 0:units, :].bitcast(F32)).then_inc(st_out[t % 2], 16)

            with sp.Fori(0, LAST) as it:
                turn(it, LOOP_KINDS, lambda j: io["stacks_da"][it * 2 + j], True)
            turn(LAST, LAST_KINDS, lambda j: io["stacks_wa"][4 * j:4 * j + 4 + 2 * j], False)
            for s in range(2):
                sp.wait_ge(st_out[s], 16 * (uses(LAST, 1, TL) + 1))
                sp.wait_ge(v_out[s], 16 * (uses(LAST, 1, 0) + 1))

        @block.tensor
        def _(pe):
            def accumulate(it, j, t, kind):
                col, units, has_v = content(kind, t)
                bank = banks[(2 * j + t) % 4]
                pe.wait_ge(raw_ready, item(it, j, t) + 1)
                for k in range(KC):
                    mm = parts_product(pe, bank[:, col:GW], (h_hi[:, k, t * P:(t + 1) * P], h_lo[:, k, t * P:(t + 1) * P]),
                                       (w_hi[j][:, k, col:GW], w_lo[j][:, k, col:GW]), k == 0, k == KC - 1)
                mm.then_inc(acc_done, 1)

            def turn_units(it, j, t, kind):
                col, units, has_v = content(kind, t)
                pe.wait_ge(cut_ready, item(it, j, t) + 1 + CR)
                pe.wait_ge(st_ready, item(it, j, t) + 1)
                for u in range(units):
                    mm = pe.transpose(banks[4 + 2 * (t % 2) + u // 4][:, (u % 4) * P:(u % 4 + 1) * P],
                                      cut[t % 2][:, u, :, :].rearrange("p a d -> p (a d)").bitcast(F32), ident[:])
                mm.then_inc(turned, 1)

            def turn(it, kinds):
                todo = [(j, t, kind) for j, kind in enumerate(kinds) for t in range(tiles(kind))]
                for i, (j, t, kind) in enumerate(todo):
                    if t == 0:
                        pe.wait_ge(w_lo_ready, (it * 2 + j + 1) * KC)
                    accumulate(it, j, t, kind)
                    if i:
                        jj, tt, kk = todo[i - 1]
                        turn_units(it, jj, tt, kk)
                turn_units(it, j, t, kind)

            pe.sem_inc(turned, CR)
            with pe.Fori(0, LAST) as it:
                turn(it, LOOP_KINDS)
            turn(LAST, LAST_KINDS)

        @block.scalar
        def _(act):
            def weight_hi(group, slot, k, landed):
                act.wait_ge(w_in[slot], landed)
                act.activation(w_hi[slot][:, k, :], w_raw[slot][:, k, :], ACT.Copy).then_inc(w_hi_ready, 1)

            def copy_units(it, j, t, kind):
                col, units, has_v = content(kind, t)
                act.wait_ge(turned, item(it, j, t) + 1 + CR)
                act.wait_ge(st_out[t % 2], 16 * uses(it, j, t) + 16)
                b = 4 + 2 * (t % 2)
                n = min(units, 4)
                ins = act.activation(st[t % 2][:, 0:n, :], banks[b][:, 0:n * P].rearrange("p (u n) -> p u n", n=P), ACT.Copy)
                if units > 4:
                    ins = act.activation(st[t % 2][:, 4:units, :],
                                         banks[b + 1][:, 0:(units - 4) * P].rearrange("p (u n) -> p u n", n=P), ACT.Copy)
                ins.then_inc(st_ready, 1)

            def turn(it, kinds, more):
                todo = [(j, t, kind) for j, kind in enumerate(kinds) for t in range(tiles(kind))]
                for i, (j, t, kind) in enumerate(todo):
                    col, units, has_v = content(kind, t)
                    act.wait_ge(acc_done, item(it, j, t) + 1)
                    act.wait_ge(cut_ready, item(it, j, t) + 1)
                    act.activation(raw[t % 2][:, col:GW], banks[(2 * j + t) % 4][:, col:GW], ACT.Copy).then_inc(raw_ready, 1)
                    if (j == 0 or more) and t < KC:
                        weight_hi(it * 2 + j + 1, 1 - j, t, 16 * (it + j + 1))
                    if i:
                        jj, tt, kk = todo[i - 1]
                        copy_units(it, jj, tt, kk)
                copy_units(it, j, t, kind)

            act.sem_inc(raw_ready, 4)
            act.sem_inc(st_ready, CR)
            for s in range(2):
                act.sem_inc(st_out[s], 16)
                act.sem_inc(v_out[s], 16)
            for k in range(KC):
                weight_hi(0, 0, k, 16)
            with act.Fori(0, LAST) as it:
                turn(it, LOOP_KINDS, True)
            turn(LAST, LAST_KINDS, False)

        @block.gpsimd
        def _(pool):
            def weight_lo(group, slot):
                for k in range(KC):
                    pool.wait_ge(w_hi_ready, group * KC + k + 1)
                    nc.gpsimd.tensor_tensor(w_lo[slot][:, k, :], w_raw[slot][:, k, :], w_hi[slot][:, k, :].bitcast(F32),
                                            ALU.subtract).then_inc(w_lo_ready, 1)

            with pool.Fori(0, LAST + 1) as it:
                for j in range(2):
                    weight_lo(it * 2 + j, j)

        @block.vector
        def _(v):
            def cut_tile(ch, it, j, t, kind):
                col, units, has_v = content(kind, t)
                src, c = raw[t % 2], cut[t % 2]
                v.wait_ge(raw_ready, item(it, j, t) + 1 + 4)
                v.wait_ge(turned, item(it, j, t) + 1)
                x = src[:, col:col + units * HD].rearrange("p (u d) -> p u d", d=HD)
                if t < TL:
                    v.wait_ge(cut_ready, item(it, j, t) + CR)
                    cs = cosT[:, t:t + 1, :].to_broadcast([P, units, HD])
                    sn = sinT[:, t:t + 1, :].to_broadcast([P, units, HD])
                    ch.did(v.tensor_tensor(rot[:, 0:units, :], x, cs, ALU.mult))
                    ch.did(v.tensor_tensor(swp[:, 0:units, 0:HD:2], x[:, :, 1:HD:2], sn[:, :, 0:HD:2], ALU.mult))
                    ch.link(v.tensor_tensor(swp[:, 0:units, 1:HD:2], x[:, :, 0:HD:2], sn[:, :, 1:HD:2], ALU.mult))
                    x = rot[:, 0:units, :]
                    ch.link(v.tensor_tensor(x, x, swp[:, 0:units, :], ALU.add))
                ch.did(v.tensor_copy(c[:, 0:units, 0, :], x))
                if has_v:
                    v.wait_ge(v_out[t % 2], 16 * uses(it, j, t) + 16)
                    ch.did(v.tensor_copy(v_cut[t % 2][:, 0:P], src[:, 2 * P:GW]))
                ch.settle()
                ins = v.tensor_tensor(c[:, 0:units, 1, :], x, c[:, 0:units, 0, :].bitcast(F32), ALU.subtract)
                if has_v:
                    ch.did(ins)
                    ins = v.tensor_tensor(v_cut[t % 2][:, P:2 * P], src[:, 2 * P:GW], v_cut[t % 2][:, 0:P].bitcast(F32),
                                          ALU.subtract)
                ins.then_inc(cut_ready, 1)

            OWN = 2 * (7 * TL + 3 * (TT - TL))
            v.sem_inc(cut_ready, CR)
            v.wait_ge(table_in, 32)

            def turn(it, kinds):
                ch = Chain(v, dve, it * OWN)
                for j, kind in enumerate(kinds):
                    for t in range(tiles(kind)):
                        cut_tile(ch, it, j, t, kind)
                return ch.n

            with v.Fori(0, LAST) as it:
                assert turn(it, LOOP_KINDS) == OWN
            turn(LAST, LAST_KINDS)


def wide_product(pe, outs, stat, movs, first, last):
    sh, sl = stat
    for out, (mh, ml) in zip(outs, movs):
        pe.matmul(out, sh, mh, start=first, stop=False)
        pe.matmul(out, sh, ml, start=False, stop=False)
    for out, (mh, ml) in zip(outs, movs):
        mm = pe.matmul(out, sl, mh, start=False, stop=last)
    return mm


def features(nc, sem, banks, io, keep):
    h_hi, h_lo, psum = keep["h_hi"], keep["h_lo"], keep["psum"]
    silu_x, A2, B2, gate_row = keep["silu_x"], keep["A2"], keep["B2"], keep["gate_row"]
    G = len(POOL_WINDOWS)
    TILES = G + 3 * KC
    TURNS = 3 * KC // 2
    PAD = max(POOL_WINDOWS) // 2
    AC = P
    PIECES = 4 * D // AC
    A_TURNS = PIECES // 4
    with ExitStack() as ctx:
        sb = lambda n, s, d=F32: ctx.enter_context(nc.sbuf_tensor(n, s, d))
        w_raw = [sb(f"f_raw{j}", [P, KC, P]) for j in range(2)]
        w_hi = [sb(f"f_hi{j}", [P, KC, P], F32R) for j in range(2)]
        w_lo = [sb(f"f_lo{j}", [P, KC, P], F32R) for j in range(2)]
        gst = [sb(f"gst{j}", [P, HALF]) for j in range(2)]
        upad = sb("upad", [P, SEQ + 2 * PAD])
        win = [sb(f"win{j}", [P, SEQ + 2 * PAD]) for j in range(2)]
        inv = sb("inv", [P, SEQ])
        pl_hi, pl_lo = sb("pl_hi", [P, SEQ], F32R), sb("pl_lo", [P, SEQ], F32R)
        pw = sb("pw", [P, G, P])
        pw_hi, pw_lo = sb("pw_hi", [P, G, P], F32R), sb("pw_lo", [P, G, P], F32R)
        pscale = sb("pscale", [P, G])
        piece = [sb(f"piece{j}", [P, KC, AC]) for j in range(2)]
        acc = sb("acc", [P, 4 * D])
        brow, grow = sb("brow", [P, D]), sb("grow", [P, D])
        ones = sb("ones", [P, P])
        badaT, ngT = sb("badaT", [P, 6 * KC]), sb("ngT", [P, 4, KC])
        m2 = sb("m2", [P, 2 * KC])
        small_in, inv_in, row_in = sem("ft_small_in"), sem("ft_inv_in"), sem("ft_row_in")
        w_in, piece_in = [sem(f"ft_w_in{j}") for j in range(2)], [sem(f"ft_piece_in{j}") for j in range(2)]
        w_hi_ready, w_lo_ready, acc_done, taken = sem("ft_w_hi"), sem("ft_w_lo"), sem("ft_acc"), sem("ft_taken")
        gst_ready, gst_out = sem("ft_gst"), [sem(f"ft_gst_out{j}") for j in range(2)]
        upad_clear, u_ready, u_used, pooled, pool_done, yb_ready = (sem(f"ft_{n}") for n in
                                                        ("clear", "u", "u_used", "pooled", "pool_done", "yb"))
        yb_out, piece_used, ada_ready, dve = sem("ft_yb_out"), sem("ft_piece_used"), sem("ft_ada"), sem("ft_dve")
        pw_ready, rows_done, row_used = sem("ft_pw"), sem("ft_rows"), sem("ft_row_used")
        gates = io["gates"].rearrange("i m p n -> (i m) p n")
        block = ctx.enter_context(nc.Block())

        @block.sync
        def _(sp):
            for j in range(2):
                sp.dma_start(w_raw[j][:], io["w_feat"][j]).then_inc(w_in[j], 16)
            for dst, src in ((pw, io["pool_w"]), (pscale, io["pool_scaleT"]), (badaT, io["b_adaT"]), (ngT, io["norm_gT"])):
                sp.dma_start(dst[:], src).then_inc(small_in, 16)

            def load_w(f, slot):
                sp.wait_ge(w_lo_ready, f - 1)
                sp.dma_start(w_raw[slot][:], io["w_feat"][f]).then_inc(w_in[slot], 16)

            def load_piece(q, slot):
                sp.wait_ge(piece_used, q + 1)
                sp.dma_start(piece[slot][:], io["w_ada"].rearrange("(k p) n -> p k n", p=P)
                             .rearrange("p k (a n) -> a p k n", n=AC)[2 * D // AC + q]).then_inc(piece_in[slot], 16)

            def store_gate(f):
                for n in range(NH):
                    sp.wait_ge(gst_ready, (f - G) * NH + n + 1)
                    sp.dma_start(gates[f - G][:, n * HALF:(n + 1) * HALF], gst[n][:]).then_inc(gst_out[n], 16)

            for g in range(G):
                if g:
                    sp.wait_ge(pooled, g)
                sp.dma_start(inv[:], io["inv_count"][g:g + 1, :].to_broadcast([P, SEQ])).then_inc(inv_in, 16)
                load_w(g + 2, g % 2)
                if g >= 1:
                    sp.wait_ge(yb_ready, g)
                    sp.dma_start(io["yb"][g - 1], win[1][:, 0:SEQ]).then_inc(yb_out, 16)

            def turn(it, pieces, more):
                for j in range(2):
                    f = it * 2 + G + j
                    if more:
                        load_w(f + 2, j)
                    for q in range(2 * pieces):
                        load_piece((it - 1) * 4 + 2 * j + q, q)
                    store_gate(f)

            load_w(G + 2, 0)
            sp.wait_ge(yb_ready, G)
            sp.dma_start(io["yb"][G - 1], win[1][:, 0:SEQ]).then_inc(yb_out, 16)
            store_gate(G)
            load_w(G + 3, 1)
            store_gate(G + 1)
            with sp.Fori(1, 1 + A_TURNS) as it:
                turn(it, 1, True)
            with sp.Fori(1 + A_TURNS, TURNS - 1) as it:
                turn(it, 0, True)
            for i in range(2):
                if i:
                    sp.wait_ge(row_used, 1)
                sp.dma_start(brow[:], io["b_ada"][0:1, (2 + 3 * i) * D:(3 + 3 * i) * D].to_broadcast([P, D])).then_inc(row_in, 16)
                sp.dma_start(grow[:], io["norm_g"][1 + 2 * i:2 + 2 * i, :].to_broadcast([P, D])).then_inc(row_in, 16)
                if not i:
                    turn(TURNS - 1, 0, False)
            for n in range(NH):
                sp.wait_ge(gst_out[n], 16 * (3 * KC + 1))
            sp.wait_ge(yb_out, 16 * G)

        @block.tensor
        def _(pe):
            def tile(f, slot):
                pe.wait_ge(w_lo_ready, f + 1)
                pe.wait_ge(taken, f + 1)
                for k in range(KC):
                    mm = wide_product(pe, [banks[2 * slot + n][:, :] for n in range(NH)],
                                      (w_hi[slot][:, k, :], w_lo[slot][:, k, :]),
                                      [(h_hi[:, k, n * HALF:(n + 1) * HALF], h_lo[:, k, n * HALF:(n + 1) * HALF])
                                       for n in range(NH)], k == 0, k == KC - 1)
                mm.then_inc(acc_done, 1)

            def pool_tile(g):
                pe.wait_ge(pooled, g + 1)
                if g == 0:
                    pe.wait_ge(pw_ready, 1)
                else:
                    pe.wait_ge(yb_ready, g)
                wide_product(pe, [banks[4 + n][:, :] for n in range(NH)], (pw_hi[:, g, :], pw_lo[:, g, :]),
                             [(pl_hi[:, n * HALF:(n + 1) * HALF], pl_lo[:, n * HALF:(n + 1) * HALF])
                              for n in range(NH)], True, True).then_inc(pool_done, 1)

            pe.sem_inc(acc_done, 2)
            for f in range(G):
                tile(f, f % 2)
                if f:
                    pool_tile(f - 1)
            tile(G, 0)
            pool_tile(G - 1)
            tile(G + 1, 1)
            with pe.Fori(1, TURNS) as it:
                for j in range(2):
                    tile(it * 2 + G + j, j)
            pe.wait_ge(ada_ready, 1)
            for i in range(2):
                for n in range(NH):
                    pe.matmul(banks[4 + 2 * i + n][:, :], ones[:], acc[:, 3 * i * D + n * HALF:3 * i * D + (n + 1) * HALF],
                              start=True, stop=True)
            pe.wait_ge(taken, TILES + 2)
            for b in range(2 * KC):
                mm = pe.matmul(banks[0][:, b:b + 1], acc[:, D + b * P:D + (b + 1) * P], ones[:, 0:1], start=True, stop=True)
            mm.then_inc(rows_done, 1)

        @block.scalar
        def _(act):
            def weight_hi(f, slot, landed):
                act.wait_ge(w_in[slot], landed)
                act.wait_ge(acc_done, f + 1)
                act.activation(w_hi[slot][:], w_raw[slot][:], ACT.Copy).then_inc(w_hi_ready, 1)

            def gate(f, slot):
                act.wait_ge(acc_done, f + 3)
                for n in range(NH):
                    act.wait_ge(gst_out[n], 16 * (f - G) + 16)
                    ins = act.activation(gst[n][:], banks[2 * slot + n][:, :], ACT.Sigmoid)
                    ins.then_inc(gst_ready, 1)
                act.wait_ge(gst_ready, (f - G) * NH + NH)
                act.sem_inc(taken, 1)

            act.sem_inc(taken, 2)
            for n in range(NH):
                act.sem_inc(gst_out[n], 16)
            weight_hi(0, 0, 16)
            weight_hi(1, 1, 16)
            act.wait_ge(small_in, 64)
            act.activation(pw_hi[:], pw[:], ACT.Copy).then_inc(pw_ready, 1)
            act.wait_ge(upad_clear, 1)
            for g in range(G):
                act.wait_ge(acc_done, g + 3)
                if g:
                    act.wait_ge(u_used, g)
                act.activation(upad[:, PAD:PAD + SEQ], psum[:, 2 * HALF * (g % 2):2 * HALF * (g % 2 + 1)],
                               ACT.Copy).then_inc(u_ready, 1)
                act.wait_ge(u_ready, g + 1)
                act.sem_inc(taken, 1)
                weight_hi(g + 2, g % 2, 16 * ((g + 2) // 2 + 1))

            def turn(it, more):
                for j in range(2):
                    f = it * 2 + G + j
                    gate(f, j)
                    if more:
                        weight_hi(f + 2, j, 16 * (it + G // 2 + 2))

            with act.Fori(0, TURNS - 1) as it:
                turn(it, True)
            turn(TURNS - 1, False)

        @block.gpsimd
        def _(pool):
            with pool.Fori(0, TILES // 2) as it:
                for j in range(2):
                    pool.wait_ge(w_hi_ready, it * 2 + j + 1)
                    nc.gpsimd.tensor_tensor(w_lo[j][:], w_raw[j][:], w_hi[j][:].bitcast(F32),
                                            ALU.subtract).then_inc(w_lo_ready, 1)

        @block.vector
        def _(v):
            ch = Chain(v, dve)
            ch.did(v.memset(upad[:, 0:PAD], 0.0))
            ch.did(v.memset(upad[:, PAD + SEQ:], 0.0))
            ch.link(v.memset(ones[:], 1.0))
            v.sem_inc(upad_clear, 1)
            v.sem_inc(piece_used, 2)
            v.wait_ge(pw_ready, 1)
            v.tensor_tensor(pw_lo[:], pw[:], pw_hi[:].bitcast(F32), ALU.subtract).then_inc(pw_ready, 1)
            for g, w in enumerate(POOL_WINDOWS):
                v.wait_ge(u_ready, g + 1)
                if g:
                    v.wait_ge(yb_out, 16 * g)
                src, width, step, i = upad, SEQ + 2 * PAD, 1, 0
                while step < w:
                    dst = win[i]
                    ch.link(v.tensor_tensor(dst[:, 0:width - step], src[:, 0:width - step], src[:, step:width], ALU.add))
                    src, width, step, i = dst, width - step, 2 * step, 1 - i
                other = win[i]
                v.wait_ge(inv_in, 16 * (g + 1))
                ch.link(v.tensor_tensor(other[:, 0:SEQ], src[:, PAD - w // 2:PAD - w // 2 + SEQ], inv[:], ALU.mult))
                ch.link(v.tensor_tensor(other[:, 0:SEQ], other[:, 0:SEQ], upad[:, PAD:PAD + SEQ], ALU.subtract))
                v.sem_inc(u_used, 1)
                if g:
                    v.wait_ge(pool_done, g)
                ch.link(v.tensor_copy(pl_hi[:], other[:, 0:SEQ]))
                v.tensor_tensor(pl_lo[:], other[:, 0:SEQ], pl_hi[:].bitcast(F32), ALU.subtract).then_inc(pooled, 1)
                v.wait_ge(pooled, g + 1)
                v.wait_ge(pool_done, g + 1)
                v.tensor_scalar(win[1][:, 0:SEQ], psum[:, 4 * HALF:6 * HALF], pscale[:, g:g + 1], None,
                                ALU.mult).then_inc(yb_ready, 1)

            n0 = ch.n
            with v.Fori(0, A_TURNS) as it:
                own = Chain(v, dve, it * (4 * (KC - 1)) + n0)
                for q in range(4):
                    out = acc[:].rearrange("p (a n) -> p a n", n=AC)[:, it * 4 + q, :]
                    v.wait_ge(piece_in[q % 2], it * 32 + 16 * (q // 2) + 16)
                    own.link(v.tensor_scalar(out, piece[q % 2][:, 0, :], silu_x[:, 0:1], None, ALU.mult))
                    for k in range(1, KC):
                        ins = v.scalar_tensor_tensor(out=out, in0=piece[q % 2][:, k, :], scalar=silu_x[:, k:k + 1], in1=out,
                                                     op0=ALU.mult, op1=ALU.add)
                        if k < KC - 1:
                            own.link(ins)
                    ins.then_inc(piece_used, 1)
                assert own.n == 4 * (KC - 1)
            v.wait_ge(piece_used, PIECES + 2)
            v.sem_inc(ada_ready, 1)
            v.wait_ge(rows_done, 1)
            fin = Chain(v, dve, n0 + A_TURNS * 4 * (KC - 1))
            for i in range(2):
                v.wait_ge(row_in, 32 * (i + 1))
                fin.link(v.tensor_tensor(gate_row[i][:], psum[:, (4 + 2 * i) * HALF:(6 + 2 * i) * HALF], brow[:], ALU.add))
                v.tensor_tensor(gate_row[i][:], gate_row[i][:], grow[:], ALU.mult).then_inc(row_used, 1)
            fin.link(v.tensor_tensor(m2[:], banks[0][:, 0:2 * KC], badaT[:, 3 * KC:5 * KC], ALU.add))
            fin.did(v.tensor_copy(B2[:], m2[:, 0:KC]))
            fin.link(v.scalar_tensor_tensor(out=A2[:], in0=m2[:, KC:2 * KC], scalar=1.0, in1=ngT[:, 2, :], op0=ALU.add,
                                            op1=ALU.mult))


def diff(nc, sem, banks, io, keep):
    psum, ident, neg_lam, sub_g = keep["psum"], keep["ident"], keep["neg_lam"], keep["sub_g"]
    TILES = 2 * TL
    CHUNKS = TILES // 4
    COLS = [(0, HALF), (HALF, HALF), (2 * HALF, TOK - 2 * HALF)]
    TP = [range(0, 4), range(4, 8), range(8, TT)]
    with ExitStack() as ctx:
        sb = lambda n, s, d=F32: ctx.enter_context(nc.sbuf_tensor(n, s, d))
        q_st = [sb(f"q_st{j}", [P, 2, SEQ], F32R) for j in range(2)]
        k_st = [sb(f"k_st{j}", [P, 2, TOK], F32R) for j in range(2)]
        k_sw = [sb(f"k_sw{j}", [P, 2, TOK], F32R) for j in range(2)]
        val = [sb(f"val{j}", [P, TT, 2 * P], F32R) for j in range(2)]
        e = [[sb(f"e{b}{s}", [P, TOK]) for s in range(2)] for b in range(2)]
        at_hi, at_lo = sb("at_hi", [P, TT, HALF], F32R), sb("at_lo", [P, TT, HALF], F32R)
        ya, ms = sb("ya", [P, DA_HEADS, SEQ]), sb("ms", [P, DA_HEADS, SEQ])
        sq = sb("sq", [P, HALF])
        ones = sb("ones_d", [P, P])
        mx = sb("mx", [P, 2])
        neg_m = sb("neg_m", [P, 2, 2])
        sums = sb("sums", [P, 2, 2])
        rec = sb("rec", [P, 2, 2])
        c1 = sb("c1", [P, 2])
        head_in = [sem(f"da_head_in{j}") for j in range(2)]
        sc_done, neg_ready, exp_done = ([sem(f"da_{n}{s}") for s in range(2)] for n in ("sc", "neg", "exp"))
        rec_ready, e1_ready, a_ready, at_ready = sem("da_rec"), sem("da_e1"), sem("da_a"), sem("da_at")
        turned, hi_ready, free = ([sem(f"da_{n}{b}") for b in range(2)] for n in ("turned", "hi", "free"))
        sq_ready, ms_ready, ones_ready, dve = sem("da_sq"), sem("da_ms"), sem("da_ones"), sem("da_dve")
        root_ready, ya_ready, ya_out = sem("da_root"), sem("da_ya"), sem("da_ya_out")

        steps = []
        for i in range(TILES + 1):
            if i < TILES:
                steps.append(("scores", i))
            if i >= 5 and (i - 1) % 4 == 0 and i < TILES:
                steps.append(("av", (i - 5) // 4))
            if i:
                steps.append(("turn", i - 1))
            if i >= 5 and (i - 1) % 4 == 0 and i < TILES:
                steps.append(("square", (i - 5) // 4))
        steps += [("av", CHUNKS - 1), ("square", CHUNKS - 1)]
        ring = {}
        for what in steps:
            if what[0] != "scores":
                for part in range(3 if what[0] == "turn" else 1):
                    ring[what + (part,)] = len(ring)
        PER_BANK = len(ring) // 2
        assert len(ring) % 2 == 0

        def slot(it, *what):
            n = ring[what]
            return n % 2, it * PER_BANK + n // 2

        block = ctx.enter_context(nc.Block())

        @block.sync
        def _(sp):
            def load_head(h):
                j = h % 2
                src = io["stacks_da"][h]
                for dst, s in ((q_st[j][:], src[0:2, :, 0:SEQ]), (k_st[j][:], src[2:4])):
                    sp.dma_start(dst.bitcast(F32), s.rearrange("s p n -> p s n")).then_inc(head_in[j], 16)
                for a, b in ((0, HD), (HD, 0)):
                    sp.dma_start(k_sw[j][a:a + HD].bitcast(F32),
                                 src[2:4, b:b + HD].rearrange("s p n -> p s n")).then_inc(head_in[j], 16)
                sp.dma_start(val[j][:].bitcast(F32), io["vals"][h].rearrange("t p n -> p t n")).then_inc(head_in[j], 16)

            load_head(0)
            load_head(1)
            for j in range(2):
                b, used = slot(0, "av", 2 * j + 1, 0)
                sp.wait_ge(turned[b], used + 1)
                load_head(2 + j)
            for h in range(DA_HEADS):
                sp.wait_ge(ya_ready, h + 1)
                sp.dma_start(io["ya"][h], ya[:, h, :]).then_inc(ya_out, 16)
            sp.wait_ge(ya_out, 16 * DA_HEADS)

        @block.tensor
        def _(pe):
            def use(it, *what):
                b, used = slot(it, *what)
                pe.wait_ge(free[b], used + 1)
                return b, banks[6 + b]

            def scores(it, i):
                j, t = i // TL, i % TL
                if t == 0:
                    pe.wait_ge(head_in[j], 80 * it + 80)
                for s in range(2):
                    pe.wait_ge(exp_done[s], it * TILES + i + 1)
                    q = q_st[j][:, s, t * P:(t + 1) * P]
                    for c, (c0, w) in enumerate(COLS):
                        out = banks[3 * s + c][:, 0:w]
                        pe.matmul(out, q, k_st[j][:, s, c0:c0 + w], start=True, stop=False)
                        mm = pe.matmul(out, q, k_sw[j][:, s, c0:c0 + w], start=False, stop=True)
                    mm.then_inc(sc_done[s], 1)

            def turn(it, i):
                pe.wait_ge(a_ready, it * TILES + i + 1)
                for part, tiles in enumerate(TP):
                    b, bank = use(it, "turn", i, part)
                    for n, k in enumerate(tiles):
                        mm = pe.transpose(bank[:, n * P:(n + 1) * P], e[i % 2][0][:, k * P:(k + 1) * P], ident[:])
                    mm.then_inc(turned[b], 1)

            def av(it, c):
                pe.wait_ge(at_ready, it * TILES + 4 * c + 4)
                b, bank = use(it, "av", c, 0)
                v = val[c // 2]
                for k in range(TT):
                    mm = parts_product(pe, bank, (v[:, k, 0:P], v[:, k, P:2 * P]), (at_hi[:, k, :], at_lo[:, k, :]),
                                       k == 0, k == TT - 1)
                mm.then_inc(turned[b], 1)

            def square(it, c):
                pe.wait_ge(sq_ready, it * CHUNKS + c + 1)
                b, bank = use(it, "square", c, 0)
                pe.matmul(bank, ones[:], sq[:], start=True, stop=True).then_inc(turned[b], 1)

            pe.wait_ge(ones_ready, 1)
            with pe.Fori(0, 2) as it:
                for what, i in steps:
                    {"scores": scores, "turn": turn, "av": av, "square": square}[what](it, i)

        @block.scalar
        def _(act):
            def exp(it, i, s):
                N = it * TILES + i
                act.wait_ge(neg_ready[s], N + 1)
                act.wait_ge(sc_done[s], N + 1)
                if i >= 2:
                    b, used = slot(it, "turn", i - 2, 2)
                    act.wait_ge(turned[b], used + 1)
                act.activation(e[i % 2][s][:], psum[:, 3 * s * HALF:3 * s * HALF + TOK], ACT.Exp, scale=SCALE,
                               bias=neg_m[:, i % 2, s:s + 1], accum_out=sums[:, i % 2, s:s + 1]).then_inc(exp_done[s], 1)

            def scale_e1(it, i):
                act.wait_ge(rec_ready, it * TILES + i + 1)
                act.activation(e[i % 2][1][:], e[i % 2][1][:], ACT.Copy, scale=c1[:, i % 2:i % 2 + 1]).then_inc(e1_ready, 1)

            def hi(it, i, part):
                b, used = slot(it, "turn", i, part)
                act.wait_ge(turned[b], used + 1)
                tiles = TP[part]
                w = len(tiles) * P
                act.activation(at_hi[:, tiles[0]:tiles[-1] + 1, (i % 4) * P:(i % 4 + 1) * P],
                               banks[6 + b][:, 0:w].rearrange("p (k n) -> p k n", n=P), ACT.Copy).then_inc(hi_ready[b], 1)

            def products(it, c):
                b, used = slot(it, "av", c, 0)
                act.wait_ge(turned[b], used + 1)
                act.activation(ya[:, it * 2 + c // 2, (c % 2) * HALF:(c % 2 + 1) * HALF], banks[6 + b], ACT.Copy)\
                   .then_inc(hi_ready[b], 1)
                if c:
                    sb_, used_sq = slot(it, "square", c - 1, 0)
                    act.wait_ge(turned[sb_], used_sq + 1)
                act.activation(sq[:], banks[6 + b], ACT.Square).then_inc(sq_ready, 1)
                act.wait_ge(hi_ready[b], used + 1)
                act.wait_ge(sq_ready, it * CHUNKS + c + 1)
                act.sem_inc(free[b], 1)

            for s in range(2):
                act.sem_inc(exp_done[s], 1)
            with act.Fori(0, 2) as it:
                for i in range(TILES + 1):
                    if i:
                        scale_e1(it, i - 1)
                    if i < TILES:
                        exp(it, i, 0)
                    if i >= 5 and (i - 1) % 4 == 0 and i < TILES:
                        products(it, (i - 5) // 4)
                    if i:
                        hi(it, i - 1, 0)
                        hi(it, i - 1, 1)
                    if i < TILES:
                        exp(it, i, 1)
                    if i:
                        hi(it, i - 1, 2)
                products(it, CHUNKS - 1)
            act.wait_ge(ms_ready, 2 * CHUNKS)
            for h in range(DA_HEADS):
                act.activation(ms[:, h, :], ms[:, h, :], ACT.Sqrt).then_inc(root_ready, 1)

        @block.vector
        def _(v):
            def maximum(ch, it, i, s):
                v.wait_ge(sc_done[s], it * TILES + i + 1)
                ch.link(v.tensor_reduce(mx[:, s:s + 1], psum[:, 3 * s * HALF:3 * s * HALF + TOK], AX.X, ALU.max))
                v.tensor_scalar(neg_m[:, i % 2, s:s + 1], mx[:, s:s + 1], -SCALE, None, ALU.mult).then_inc(neg_ready[s], 1)

            def reciprocals(ch, it, i):
                for s in range(2):
                    v.wait_ge(exp_done[s], it * TILES + i + 2)
                ch.link(v.reciprocal(rec[:, i % 2, :], sums[:, i % 2, :]))
                v.tensor_scalar(c1[:, i % 2:i % 2 + 1], rec[:, i % 2, 1:2], neg_lam[:, 0:1], None,
                                ALU.mult).then_inc(rec_ready, 1)

            def combine(it, i):
                v.wait_ge(e1_ready, it * TILES + i + 1)
                v.scalar_tensor_tensor(out=e[i % 2][0][:], in0=e[i % 2][0][:], scalar=rec[:, i % 2, 0:1],
                                       in1=e[i % 2][1][:], op0=ALU.mult, op1=ALU.add).then_inc(a_ready, 1)

            def lo(it, i, part):
                b, used = slot(it, "turn", i, part)
                v.wait_ge(hi_ready[b], used + 1)
                tiles = TP[part]
                w, at = len(tiles) * P, (slice(None), slice(tiles[0], tiles[-1] + 1), slice((i % 4) * P, (i % 4 + 1) * P))
                v.tensor_tensor(at_lo[at], banks[6 + b][:, 0:w].rearrange("p (k n) -> p k n", n=P),
                                at_hi[at].bitcast(F32), ALU.subtract).then_inc(free[b], 1)
                if part == 2:
                    v.wait_ge(free[b], used + 2)
                    v.wait_ge(free[1 - b], slot(it, "turn", i, 1)[1] + 2)
                    v.sem_inc(at_ready, 1)

            def mean_square(it, c):
                b, used = slot(it, "square", c, 0)
                v.wait_ge(turned[b], used + 1)
                v.tensor_scalar(ms[:, it * 2 + c // 2, (c % 2) * HALF:(c % 2 + 1) * HALF], banks[6 + b], 1.0 / DA_V, EPS,
                                ALU.mult, ALU.add).then_inc(ms_ready, 1)
                v.wait_ge(ms_ready, it * CHUNKS + c + 1)
                v.sem_inc(hi_ready[b], 1)
                v.sem_inc(free[b], 1)

            v.memset(ones[:], 1.0).then_inc(ones_ready, 1)
            for b in range(2):
                v.sem_inc(free[b], 1)
            OWN = 3 * TILES
            with v.Fori(0, 2) as it:
                ch = Chain(v, dve, it * OWN)
                for i in range(TILES + 1):
                    if i < TILES:
                        maximum(ch, it, i, 0)
                    if i:
                        combine(it, i - 1)
                    if i < TILES:
                        maximum(ch, it, i, 1)
                    if i:
                        for part in range(3):
                            lo(it, i - 1, part)
                    if i >= 5 and (i - 1) % 4 == 0 and i < TILES:
                        mean_square(it, (i - 5) // 4)
                    if i < TILES:
                        reciprocals(ch, it, i)
                mean_square(it, CHUNKS - 1)
                assert ch.n == OWN
            ch = Chain(v, dve, 2 * OWN)
            for h in range(DA_HEADS):
                v.wait_ge(root_ready, h + 1)
                ch.link(v.reciprocal(ms[:, h, :], ms[:, h, :]))
                v.scalar_tensor_tensor(out=ya[:, h, :], in0=ya[:, h, :], scalar=sub_g[:, 0:1], in1=ms[:, h, :],
                                       op0=ALU.mult, op1=ALU.mult).then_inc(ya_ready, 1)


def window(nc, sem, banks, io, keep):
    psum, ident, y_hi, y_lo = keep["psum"], keep["ident"], keep["y_hi"], keep["y_lo"]
    UN = 2 * TL
    BAND = 3 * P
    KEYS = CTX + BAND
    with ExitStack() as ctx:
        sb = lambda n, s, d=F32: ctx.enter_context(nc.sbuf_tensor(n, s, d))
        q_st = sb("wq_st", [P, WA_GROUP, SEQ], F32R)
        y_in = sb("y_in", [P, SEQ])
        k_st, k_sw = sb("wk_st", [P, TOK], F32R), sb("wk_sw", [P, TOK], F32R)
        val = sb("wval", [P, TT, 2, HD], F32R)
        e = [[sb(f"we{b}{s}", [P, KEYS]) for s in range(2)] for b in range(2)]
        pt_hi, pt_lo = (sb(f"pt_{n}", [P, KEYS // P, WA_GROUP, P], F32R) for n in ("hi", "lo"))
        low, o_sum = sb("low", [HD, HALF]), sb("o_sum", [P, 2, P])
        yc = sb("yc", [P, 2, P])
        ident_r, mask_r = sb("ident_r", [P, P], F32R), sb("mask_r", [P, BAND], F32R)
        mask = sb("mask", [P, BAND])
        sink = sb("sink", [P, WA_HEADS])
        nsink = sb("nsink", [P, WA_HEADS])
        mx, neg_m, sums, es, rec = sb("wmx", [P, 2]), sb("wneg_m", [P, 2, 2]), sb("wsums", [P, 2, 2]), sb("wes", [P, 2, 2]), sb("wrec", [P, 2, 2])
        const_in, kv_in, y_landed = sem("wa_const_in"), sem("wa_kv_in"), sem("wa_y_in")
        const_ready, y_hi_ready, y_lo_ready = sem("wa_const"), sem("wa_y_hi"), sem("wa_y_lo")
        sc_done, neg_ready, exp_done = ([sem(f"wa_{n}{s}") for s in range(2)] for n in ("sc", "neg", "exp"))
        es_ready, p_ready, pt_ready, low_ready, dve = sem("wa_es"), sem("wa_p"), sem("wa_pt"), sem("wa_low"), sem("wa_dve")
        turned, hi_ready, free = ([sem(f"wa_{n}{b}") for b in range(2)] for n in ("turned", "hi", "free"))
        yc_ready = sem("wa_yc")

        def tiles_of(blk):
            return [0, 1] + [2 + b for b in range(max(blk - 1, 0), min(blk + 2, TL))]

        def squares(u):
            todo = [(s, k) for s in range(2) for k in range(len(tiles_of(u // 2)))]
            return [todo[n:n + 4] for n in range(0, len(todo), 4)]

        steps = []
        for u in range(UN + 1):
            if u < UN:
                steps.append(("scores", u))
            if u >= 3 and u % 2 and u < UN:
                steps.append(("av", (u - 3) // 2))
            if u:
                steps.append(("turn", u - 1))
        steps.append(("av", TL - 1))
        ring = {}
        for what in steps:
            if what[0] != "scores":
                for part in range(len(squares(what[1])) if what[0] == "turn" else 1):
                    ring[what + (part,)] = len(ring)
        assert len(ring) % 2 == 0
        PER_BANK = len(ring) // 2

        def slot(kv, *what):
            n = ring[what]
            return n % 2, kv * PER_BANK + n // 2

        block = ctx.enter_context(nc.Block())

        @block.sync
        def _(sp):
            sp.dma_start(mask[:], io["mask"]).then_inc(const_in, 16)
            sp.dma_start(sink[:], io["wa_sink"].to_broadcast([P, WA_HEADS])).then_inc(const_in, 16)

            def load_kv(kv):
                heads = [kv * WA_GROUP + n for n in range(WA_GROUP)]
                for n, h in enumerate(heads):
                    src = io["stacks_wa"][h - 6 if h >= 6 else h + 4]
                    sp.dma_start(q_st[:, n, :].bitcast(F32), src[:, 0:SEQ]).then_inc(kv_in, 16)
                k = io["stacks_wa"][2 + kv]
                for dst, a, b in ((k_st, 0, 0), (k_st, HD, HD), (k_sw, 0, HD), (k_sw, HD, 0)):
                    for d0, s0, w in ((0, SEQ, CTX), (CTX, 0, SEQ)):
                        sp.dma_start(dst[a:a + HD, d0:d0 + w].bitcast(F32), k[b:b + HD, s0:s0 + w]).then_inc(kv_in, 16)
                v = io["vals"][DA_HEADS].rearrange("t p (c g d) -> g p t c d", c=2, g=WA_KV)[kv]
                for c in range(2):
                    sp.dma_start(val[:, 2:TT, c, :].bitcast(F32), v[:, 0:TL, c, :]).then_inc(kv_in, 16)
                    sp.dma_start(val[:, 0:2, c, :].bitcast(F32), v[:, TL:TT, c, :]).then_inc(kv_in, 16)

            load_kv(0)
            for n in range(2 * BC):
                if n:
                    sp.wait_ge(y_lo_ready, n)
                sp.dma_start(y_in[:], io[("ya", "yb")[n // BC]][n % BC]).then_inc(y_landed, 16)
            b, used = slot(0, "av", TL - 1, 0)
            sp.wait_ge(turned[b], used + 1)
            load_kv(1)

        KV_DMAS = 16 * (4 + 8 + 4)

        @block.tensor
        def _(pe):
            def use(kv, *what):
                b, used = slot(kv, *what)
                pe.wait_ge(free[b], used + 1)
                return b, banks[6 + b]

            def scores(kv, u):
                blk, pair = u // 2, u % 2
                if u == 0:
                    pe.wait_ge(kv_in, KV_DMAS * kv + KV_DMAS)
                band = tiles_of(blk)[2]
                width = (len(tiles_of(blk)) - 2) * P
                for s in range(2):
                    pe.wait_ge(exp_done[s], kv * UN + u + 1)
                    q = q_st[:, 2 * pair + s, blk * P:(blk + 1) * P]
                    pe.matmul(banks[2 * s][:, CTX:HALF], q, k_st[:, 0:CTX], start=True, stop=False)
                    pe.matmul(banks[2 * s][:, CTX:HALF], q, k_sw[:, 0:CTX], start=False, stop=True)
                    out, at = banks[2 * s + 1][:, 0:width], slice(band * P, band * P + width)
                    pe.matmul(out, q, k_st[:, at], start=True, stop=False)
                    pe.matmul(out, q, k_sw[:, at], start=False, stop=False)
                    m0 = (band - 2 - (blk - 1)) * P
                    mm = pe.matmul(out, ident_r[:], mask_r[:, m0:m0 + width], start=False, stop=True)
                    mm.then_inc(sc_done[s], 1)

            def turn(kv, u):
                pe.wait_ge(p_ready, kv * UN + u + 1)
                for part, todo in enumerate(squares(u)):
                    b, bank = use(kv, "turn", u, part)
                    for n, (s, k) in enumerate(todo):
                        mm = pe.transpose(bank[:, n * P:(n + 1) * P], e[u % 2][s][:, k * P:(k + 1) * P], ident[:])
                    mm.then_inc(turned[b], 1)

            def av(kv, blk):
                pe.wait_ge(pt_ready, kv * UN + 2 * blk + 2)
                b, bank = use(kv, "av", blk, 0)
                tiles = tiles_of(blk)
                for n, k in enumerate(tiles):
                    v = val[:, k, :, :].rearrange("p c d -> p (c d)")
                    for part in (pt_hi, pt_lo):
                        mm = pe.matmul(bank, v, part[:, n, :, :].rearrange("p h q -> p (h q)"),
                                       start=(n == 0 and part is pt_hi), stop=(n == len(tiles) - 1 and part is pt_lo))
                mm.then_inc(turned[b], 1)

            pe.wait_ge(const_ready, 2)
            with pe.Fori(0, WA_KV) as kv:
                for what, u in steps:
                    {"scores": scores, "turn": turn, "av": av}[what](kv, u)

        @block.scalar
        def _(act):
            def exp(kv, u, s):
                N = kv * UN + u
                keys = len(tiles_of(u // 2)) * P
                act.wait_ge(neg_ready[s], N + 1)
                act.wait_ge(sc_done[s], N + 1)
                if u >= 2:
                    b, used = slot(kv, "turn", u - 2, len(squares(u - 2)) - 1)
                    act.wait_ge(turned[b], used + 1)
                act.activation(e[u % 2][s][:, 0:keys], psum[:, 2 * s * HALF + CTX:2 * s * HALF + CTX + keys], ACT.Exp, scale=SCALE,
                               bias=neg_m[:, u % 2, s:s + 1], accum_out=sums[:, u % 2, s:s + 1]).then_inc(exp_done[s], 1)
                act.activation(es[:, u % 2, s:s + 1], neg_m[:, u % 2, s:s + 1], ACT.Exp,
                               bias=sink[:, bass.ds(kv * WA_GROUP + 2 * (u % 2) + s, 1)]).then_inc(es_ready, 1)

            def hi(kv, u, part):
                b, used = slot(kv, "turn", u, part)
                act.wait_ge(turned[b], used + 1)
                runs = split_runs(squares(u)[part])
                for r, (n0, s, k0, cnt) in enumerate(runs):
                    ins = act.activation(pt_hi[:, k0:k0 + cnt, 2 * (u % 2) + s, :],
                                         banks[6 + b][:, n0 * P:(n0 + cnt) * P].rearrange("p (k n) -> p k n", n=P), ACT.Copy)
                ins.then_inc(hi_ready[b], 1)

            def products(kv, blk):
                b, used = slot(kv, "av", blk, 0)
                act.wait_ge(turned[b], used + 1)
                act.wait_ge(yc_ready, kv * TL + blk + 1)
                act.activation(low[:], banks[6 + b][HD:P, :], ACT.Copy).then_inc(hi_ready[b], 1)

            act.wait_ge(const_in, 32)
            act.activation(mask_r[:], mask[:], ACT.Copy).then_inc(const_ready, 1)
            act.activation(ident_r[:], ident[:], ACT.Copy).then_inc(const_ready, 1)
            for s in range(2):
                act.sem_inc(exp_done[s], 1)
            for n in range(2 * BC):
                act.wait_ge(y_landed, 16 * (n + 1))
                act.activation(y_hi[n // BC][:, n % BC, :], y_in[:], ACT.Copy).then_inc(y_hi_ready, 1)
            with act.Fori(0, WA_KV) as kv:
                for u in range(UN + 1):
                    if u < UN:
                        exp(kv, u, 0)
                    if u >= 3 and u % 2 and u < UN:
                        products(kv, (u - 3) // 2)
                    if u:
                        hi(kv, u - 1, 0)
                        hi(kv, u - 1, 1)
                    if u < UN:
                        exp(kv, u, 1)
                    if u and len(squares(u - 1)) > 2:
                        hi(kv, u - 1, 2)
                products(kv, TL - 1)

        @block.gpsimd
        def _(pool):
            for n in range(2 * BC):
                pool.wait_ge(y_hi_ready, n + 1)
                nc.gpsimd.tensor_tensor(y_lo[n // BC][:, n % BC, :], y_in[:], y_hi[n // BC][:, n % BC, :].bitcast(F32),
                                        ALU.subtract).then_inc(y_lo_ready, 1)

        @block.vector
        def _(v):
            def maximum(ch, kv, u, s):
                keys = len(tiles_of(u // 2)) * P
                v.wait_ge(sc_done[s], kv * UN + u + 1)
                ch.link(v.tensor_reduce(mx[:, s:s + 1], psum[:, 2 * s * HALF + CTX:2 * s * HALF + CTX + keys], AX.X, ALU.max))
                v.tensor_scalar(neg_m[:, u % 2, s:s + 1], mx[:, s:s + 1], -SCALE,
                                nsink[:, bass.ds(kv * WA_GROUP + 2 * (u % 2) + s, 1)], ALU.mult, ALU.min)\
                 .then_inc(neg_ready[s], 1)

            def reciprocals(ch, kv, u):
                for s in range(2):
                    v.wait_ge(exp_done[s], kv * UN + u + 2)
                v.wait_ge(es_ready, 2 * (kv * UN + u) + 2)
                ch.link(v.tensor_tensor(sums[:, u % 2, :], sums[:, u % 2, :], es[:, u % 2, :], ALU.add))
                ch.link(v.reciprocal(rec[:, u % 2, :], sums[:, u % 2, :]))

            def normalise(kv, u):
                keys = len(tiles_of(u // 2)) * P
                for s in range(2):
                    ins = v.tensor_scalar(e[u % 2][s][:, 0:keys], e[u % 2][s][:, 0:keys], rec[:, u % 2, s:s + 1], None,
                                          ALU.mult)
                ins.then_inc(p_ready, 1)

            def lo(kv, u, part):
                b, used = slot(kv, "turn", u, part)
                v.wait_ge(hi_ready[b], used + 1)
                for n0, s, k0, cnt in split_runs(squares(u)[part]):
                    at = (slice(None), slice(k0, k0 + cnt), 2 * (u % 2) + s, slice(None))
                    ins = v.tensor_tensor(pt_lo[at], banks[6 + b][:, n0 * P:(n0 + cnt) * P].rearrange("p (k n) -> p k n", n=P),
                                          pt_hi[at].bitcast(F32), ALU.subtract)
                ins.then_inc(free[b], 1)
                if part == len(squares(u)) - 1:
                    v.wait_ge(free[b], used + 2)
                    v.sem_inc(pt_ready, 1)

            def products(ch, kv, blk):
                b, used = slot(kv, "av", blk, 0)
                v.wait_ge(hi_ready[b], used + 1)
                for odd in range(2):
                    pick = lambda a: a.rearrange("p (a o q) -> p o a q", a=2, o=2)[:, odd]
                    ins = v.tensor_tensor(yc[odd * HD:odd * HD + HD], pick(banks[6 + b][0:HD, :]), pick(low[:]), ALU.add)
                    if odd:
                        ins.then_inc(free[b], 1)
                v.wait_ge(free[b], used + 2)
                at = (slice(None), bass.ds(kv * 2, 2), slice(blk * P, (blk + 1) * P))
                ch.link(v.tensor_copy(y_hi[2][at], yc[:]))
                v.tensor_tensor(y_lo[2][at], yc[:], y_hi[2][at].bitcast(F32), ALU.subtract).then_inc(yc_ready, 1)
                v.wait_ge(yc_ready, kv * TL + blk + 2)

            v.wait_ge(const_in, 32)
            ch = Chain(v, dve)
            ch.link(v.tensor_scalar(nsink[:], sink[:], -1.0, None, ALU.mult))
            for b in range(2):
                v.sem_inc(free[b], 1)
            v.sem_inc(yc_ready, 1)
            OWN = 4 * UN + TL
            with v.Fori(0, WA_KV) as kv:
                ch = Chain(v, dve, kv * OWN + 1)
                for u in range(UN + 1):
                    if u < UN:
                        maximum(ch, kv, u, 0)
                    if u:
                        normalise(kv, u - 1)
                    if u < UN:
                        maximum(ch, kv, u, 1)
                    if u >= 3 and u % 2 and u < UN:
                        products(ch, kv, (u - 3) // 2)
                    if u:
                        for part in range(len(squares(u - 1))):
                            lo(kv, u - 1, part)
                    if u < UN:
                        reciprocals(ch, kv, u)
                products(ch, kv, TL - 1)
                assert ch.n == OWN


def split_runs(todo):
    runs = []
    for n, (s, k) in enumerate(todo):
        if runs and runs[-1][1] == s:
            runs[-1][3] += 1
        else:
            runs.append([n, s, k, 1])
    return runs


def merge(nc, sem, banks, io, keep):
    y_hi, y_lo, m = keep["y_hi"], keep["y_lo"], keep["m"]
    psum = keep["psum"]
    WN = 3 * BC * P
    with ExitStack() as ctx:
        sb = lambda n, s, d=F32: ctx.enter_context(nc.sbuf_tensor(n, s, d))
        w_raw = [sb(f"b_raw{j}", [P, 3, BC, P]) for j in range(2)]
        w_hi = [sb(f"b_hi{j}", [P, 3, BC, P], F32R) for j in range(2)]
        w_lo = [sb(f"b_lo{j}", [P, 3, BC, P], F32R) for j in range(2)]
        g = [sb(f"b_g{j}", [P, 3, SEQ]) for j in range(2)]
        tmp = sb("b_tmp", [P, SEQ])
        w_in, g_in = [sem(f"mg_w_in{j}") for j in range(2)], [sem(f"mg_g_in{j}") for j in range(2)]
        w_hi_ready, w_lo_ready, acc_done, m_ready, taken, dve = (sem(f"mg_{n}") for n in
                                                                ("w_hi", "w_lo", "acc", "m", "taken", "dve"))
        gates = io["gates"].rearrange("i m p n -> m p i n")
        TURNS = KC // 2
        block = ctx.enter_context(nc.Block())

        @block.sync
        def _(sp):
            def load(i, j):
                sp.dma_start(w_raw[j][:], io["w_br"][i]).then_inc(w_in[j], 16)
                sp.dma_start(g[j][:], gates[i]).then_inc(g_in[j], 16)
            load(0, 0)
            load(1, 1)
            with sp.Fori(0, TURNS - 1) as it:
                for j in range(2):
                    sp.wait_ge(w_lo_ready, it * 2 + j + 1)
                    sp.wait_ge(m_ready, it * 2 + j + 1)
                    load(it * 2 + j + 2, j)

        @block.tensor
        def _(pe):
            def tile(t, j, phase):
                pe.wait_ge(w_lo_ready, t + 1)
                for i in range(3):
                    r = (3 * phase + i) % 4
                    pe.wait_ge(taken, t * 3 + i + 1)
                    for k in range(BC):
                        mm = wide_product(pe, [banks[2 * r + n] for n in range(NH)],
                                          (w_hi[j][:, i, k, :], w_lo[j][:, i, k, :]),
                                          [(y_hi[i][:, k, n * HALF:(n + 1) * HALF], y_lo[i][:, k, n * HALF:(n + 1) * HALF])
                                           for n in range(NH)], k == 0, k == BC - 1)
                    mm.then_inc(acc_done, 1)

            with pe.Fori(0, TURNS // 2) as it:
                for q in range(4):
                    tile(it * 4 + q, q % 2, q)

        @block.scalar
        def _(act):
            with act.Fori(0, TURNS) as it:
                for j in range(2):
                    act.wait_ge(w_in[j], it * 16 + 16)
                    act.wait_ge(acc_done, (it * 2 + j) * 3 + 1)
                    act.activation(w_hi[j][:], w_raw[j][:], ACT.Copy).then_inc(w_hi_ready, 1)

        @block.gpsimd
        def _(pool):
            with pool.Fori(0, TURNS) as it:
                for j in range(2):
                    pool.wait_ge(w_hi_ready, it * 2 + j + 1)
                    nc.gpsimd.tensor_tensor(w_lo[j][:], w_raw[j][:], w_hi[j][:].bitcast(F32),
                                            ALU.subtract).then_inc(w_lo_ready, 1)

        @block.vector
        def _(v):
            v.sem_inc(taken, 4)
            v.sem_inc(acc_done, 7)
            OWN = 4
            with v.Fori(0, TURNS // 2) as it:
                ch = Chain(v, dve, it * OWN)
                for q in range(4):
                    t = it * 4 + q
                    out = m[:, t, :]
                    v.wait_ge(g_in[q % 2], (it * 2 + q // 2) * 16 + 16)
                    for i in range(3):
                        r = (3 * q + i) % 4
                        v.wait_ge(acc_done, t * 3 + i + 8)
                        ins = v.tensor_tensor(out if i == 0 else tmp[:], psum[:, 2 * r * HALF:2 * (r + 1) * HALF],
                                              g[q % 2][:, i, :], ALU.mult)
                        ins.then_inc(taken, 1)
                        v.wait_ge(taken, t * 3 + i + 5)
                        if i == 1:
                            ch.link(v.tensor_tensor(out, out, tmp[:], ALU.add))
                        if i == 2:
                            v.tensor_tensor(out, out, tmp[:], ALU.add).then_inc(m_ready, 1)
                            v.wait_ge(m_ready, t + 1)
                assert ch.n == OWN


def residual(nc, sem, banks, io, keep):
    psum, ident, m, h_hi, h_lo = keep["psum"], keep["ident"], keep["m"], keep["h2_hi"], keep["h2_lo"]
    A2, B2, row = keep["A2"], keep["B2"], keep["gate_row"][0]
    with ExitStack() as ctx:
        sb = lambda n, s, d=F32: ctx.enter_context(nc.sbuf_tensor(n, s, d))
        w_raw = [sb(f"o_raw{j}", [P, D]) for j in range(2)]
        w_hi, w_lo = sb("o_hi", [P, KC, D], F32R), sb("o_lo", [P, KC, D], F32R)
        m_hi, m_lo = ([sb(f"m_{n}{j}", [P, KC, P], F32R) for j in range(2)] for n in ("hi", "lo"))
        x = [sb(f"o_x{j}", [P, D]) for j in range(2)]
        junk, xn = w_raw
        full = sb("o_full", [P, KC, P])
        ss, rs = sb("o_ss", [P, 2, 2]), sb("o_rs", [P, 2, 2])
        w_in, x_in, x_out = ([sem(f"rs_{n}{j}") for j in range(2)] for n in ("w_in", "x_in", "x_out"))
        w_hi_ready, w_lo_ready, m_hi_ready, m_lo_ready = (sem(f"rs_{n}") for n in ("w_hi", "w_lo", "m_hi", "m_lo"))
        acc_done, ss_ready, mean_ready, root_ready, taken = (sem(f"rs_{n}") for n in ("acc", "ss", "mean", "root", "taken"))
        x_ready, xn_ready, turned, full_ready, h_ready, dve = (sem(f"rs_{n}") for n in ("x", "xn", "turned", "full", "h", "dve"))
        block = ctx.enter_context(nc.Block())

        @block.sync
        def _(sp):
            for k in range(KC):
                if k >= 2:
                    sp.wait_ge(w_lo_ready, k - 1)
                sp.dma_start(w_raw[k % 2][:], io["w_out"][k * P:(k + 1) * P, :]).then_inc(w_in[k % 2], 16)
            for t in range(TL):
                if t >= 2:
                    sp.wait_ge(x_out[t % 2], 16 * (t // 2))
                    sp.wait_ge(xn_ready, t - 1)
                sp.dma_start(x[t % 2][:], io["x"][t * P:(t + 1) * P, :]).then_inc(x_in[t % 2], 16)
                if t:
                    sp.wait_ge(x_ready, t)
                    sp.dma_start(io["x_mid"][t - 1], x[(t - 1) % 2][:]).then_inc(x_out[(t - 1) % 2], 16)
            sp.wait_ge(x_ready, TL)
            sp.dma_start(io["x_mid"][TL - 1], x[(TL - 1) % 2][:]).then_inc(x_out[(TL - 1) % 2], 16)
            for j in range(2):
                sp.wait_ge(x_out[j], 16 * TL // 2)

        @block.tensor
        def _(pe):
            def turn(t):
                pe.wait_ge(xn_ready, t + 1)
                if t >= 2:
                    pe.wait_ge(full_ready, KC * (t - 1))
                for k in range(KC):
                    mm = pe.transpose(banks[4 + 2 * (t % 2) + k // 4][:, (k % 4) * P:(k % 4 + 1) * P], xn[:, k * P:(k + 1) * P],
                                      ident[:])
                mm.then_inc(turned, 1)

            for t in range(TL):
                pe.wait_ge(m_lo_ready, t + 1)
                if t >= 2:
                    pe.wait_ge(taken, t - 1)
                for k in range(KC):
                    if t == 0:
                        pe.wait_ge(w_lo_ready, k + 1)
                    for n in range(NH):
                        mm = parts_product(pe, banks[2 * (t % 2) + n], (m_hi[t % 2][:, k, :], m_lo[t % 2][:, k, :]),
                                           (w_hi[:, k, n * HALF:(n + 1) * HALF], w_lo[:, k, n * HALF:(n + 1) * HALF]),
                                           k == 0, k == KC - 1)
                mm.then_inc(acc_done, 1)
                if t:
                    turn(t - 1)
            turn(TL - 1)

        @block.scalar
        def _(act):
            def cut_m(t):
                if t >= 2:
                    act.wait_ge(acc_done, t - 1)
                act.activation(m_hi[t % 2][:], m[:, :, t * P:(t + 1) * P], ACT.Copy).then_inc(m_hi_ready, 1)

            cut_m(0)
            for k in range(KC):
                act.wait_ge(w_in[k % 2], 16 * (k // 2 + 1))
                act.activation(w_hi[:, k, :], w_raw[k % 2][:], ACT.Copy).then_inc(w_hi_ready, 1)
            cut_m(1)
            for t in range(TL):
                acc = psum[:, 2 * (t % 2) * HALF:2 * (t % 2 + 1) * HALF]
                act.wait_ge(acc_done, t + 1)
                if t:
                    act.wait_ge(ss_ready, 2 * t)
                act.activation(junk[:], acc, ACT.Square, accum_out=ss[:, t % 2, 0:1]).then_inc(ss_ready, 1)
                act.wait_ge(mean_ready, 2 * t + 1)
                act.activation(rs[:, t % 2, 0:1], ss[:, t % 2, 0:1], ACT.Sqrt).then_inc(root_ready, 1)
                act.wait_ge(x_ready, t + 1)
                act.wait_ge(ss_ready, 2 * t + 1)
                act.activation(junk[:], x[t % 2][:], ACT.Square, accum_out=ss[:, t % 2, 1:2]).then_inc(ss_ready, 1)
                act.wait_ge(mean_ready, 2 * t + 2)
                act.activation(rs[:, t % 2, 1:2], ss[:, t % 2, 1:2], ACT.Sqrt).then_inc(root_ready, 1)
                if t + 2 < TL:
                    cut_m(t + 2)
                act.wait_ge(turned, t + 1)
                if t:
                    act.wait_ge(h_ready, t)
                for k in range(KC):
                    act.activation(full[:, k, :], banks[4 + 2 * (t % 2) + k // 4][:, (k % 4) * P:(k % 4 + 1) * P],
                                   ACT.Identity, scale=A2[:, k:k + 1], bias=B2[:, k:k + 1]).then_inc(full_ready, 1)

        @block.gpsimd
        def _(pool):
            def cut_m(t):
                pool.wait_ge(m_hi_ready, t + 1)
                nc.gpsimd.tensor_tensor(m_lo[t % 2][:], m[:, :, t * P:(t + 1) * P], m_hi[t % 2][:].bitcast(F32),
                                        ALU.subtract).then_inc(m_lo_ready, 1)
            for t in range(TL):
                cut_m(t)

        @block.vector
        def _(v):
            ch = Chain(v, dve)
            for k in range(KC):
                v.wait_ge(w_hi_ready, k + 1)
                v.tensor_tensor(w_lo[:, k, :], w_raw[k % 2][:], w_hi[:, k, :].bitcast(F32), ALU.subtract).then_inc(w_lo_ready, 1)
            for t in range(TL):
                acc = psum[:, 2 * (t % 2) * HALF:2 * (t % 2 + 1) * HALF]
                root = lambda i: rs[:, t % 2, i:i + 1]
                v.wait_ge(ss_ready, 2 * t + 1)
                v.tensor_scalar(ss[:, t % 2, 0:1], ss[:, t % 2, 0:1], 1.0 / D, EPS, ALU.mult, ALU.add).then_inc(mean_ready, 1)
                v.wait_ge(root_ready, 2 * t + 1)
                ch.link(v.reciprocal(root(0), root(0)))
                if t:
                    v.wait_ge(turned, t)
                ch.link(v.scalar_tensor_tensor(out=xn[:], in0=acc, scalar=root(0), in1=row[:], op0=ALU.mult, op1=ALU.mult))
                v.sem_inc(taken, 1)
                v.wait_ge(x_in[t % 2], 16 * (t // 2 + 1))
                v.tensor_tensor(x[t % 2][:], x[t % 2][:], xn[:], ALU.add).then_inc(x_ready, 1)
                v.wait_ge(ss_ready, 2 * t + 2)
                v.tensor_scalar(ss[:, t % 2, 1:2], ss[:, t % 2, 1:2], 1.0 / D, EPS, ALU.mult, ALU.add).then_inc(mean_ready, 1)
                v.wait_ge(root_ready, 2 * t + 2)
                ch.link(v.reciprocal(root(1), root(1)))
                v.wait_ge(x_ready, t + 1)
                v.tensor_scalar(xn[:], x[t % 2][:], root(1), None, ALU.mult).then_inc(xn_ready, 1)
                v.wait_ge(full_ready, KC * (t + 1))
                at = (slice(None), slice(None), slice(t * P, (t + 1) * P))
                ch.link(v.tensor_copy(h_hi[at], full[:]))
                v.tensor_tensor(h_lo[at], full[:], h_hi[at].bitcast(F32), ALU.subtract).then_inc(h_ready, 1)


def ffn_in(nc, sem, banks, io, keep):
    psum, h_hi, h_lo, f = keep["psum"], keep["h2_hi"], keep["h2_lo"], keep["f"]
    DEPTH = 4
    TURNS = 2 * FC // DEPTH
    with ExitStack() as ctx:
        sb = lambda n, s, d=F32: ctx.enter_context(nc.sbuf_tensor(n, s, d))
        w_raw = [sb(f"i_raw{j}", [P, KC, P]) for j in range(2)]
        w_hi = [sb(f"i_hi{j}", [P, KC, P], F32R) for j in range(2)]
        w_lo = [sb(f"i_lo{j}", [P, KC, P], F32R) for j in range(2)]
        act_g = [sb(f"i_act{j}", [P, HALF]) for j in range(2)]
        w_in = [sem(f"fi_w_in{j}") for j in range(2)]
        w_hi_ready, w_lo_ready, acc_done, silu_ready, f_ready = (sem(f"fi_{n}") for n in ("w_hi", "w_lo", "acc", "silu", "f"))
        w_ff = io["w_ff"]
        block = ctx.enter_context(nc.Block())

        @block.sync
        def _(sp):
            for j in range(2):
                sp.dma_start(w_raw[j][:], w_ff[0, j]).then_inc(w_in[j], 16)
            with sp.Fori(1, FC) as m:
                for j in range(2):
                    sp.wait_ge(w_lo_ready, m * 2 + j - 1)
                    sp.dma_start(w_raw[j][:], w_ff[m, j]).then_inc(w_in[j], 16)

        @block.tensor
        def _(pe):
            with pe.Fori(0, TURNS) as it:
                for b in range(DEPTH):
                    pe.wait_ge(w_lo_ready, it * DEPTH + b + 1)
                    if b % 2 == 0:
                        pe.wait_ge(f_ready, it * DEPTH + b + 1)
                    for k in range(KC):
                        mm = wide_product(pe, [banks[2 * b + n] for n in range(NH)],
                                          (w_hi[b % 2][:, k, :], w_lo[b % 2][:, k, :]),
                                          [(h_hi[:, k, n * HALF:(n + 1) * HALF], h_lo[:, k, n * HALF:(n + 1) * HALF])
                                           for n in range(NH)], k == 0, k == KC - 1)
                    mm.then_inc(acc_done, 1)

        @block.scalar
        def _(act):
            def weight_hi(b, slot, landed):
                act.wait_ge(w_in[slot], landed)
                act.wait_ge(acc_done, b + 1)
                act.activation(w_hi[slot][:], w_raw[slot][:], ACT.Copy).then_inc(w_hi_ready, 1)

            def silu(it, b):
                act.wait_ge(acc_done, it * DEPTH + b + 3)
                for n in range(NH):
                    act.wait_ge(f_ready, it * DEPTH + b + n + 3)
                    act.activation(act_g[n][:], banks[2 * b + n], ACT.Silu).then_inc(silu_ready, 1)

            def turn(it, more):
                for b in range(DEPTH):
                    if b % 2 == 0:
                        silu(it, b)
                    if b < 2 or more:
                        weight_hi(it * DEPTH + b + 2, b % 2, (it * 2 + b // 2 + 1) * 16 + 16)

            weight_hi(0, 0, 16)
            weight_hi(1, 1, 16)
            with act.Fori(0, TURNS - 1) as it:
                turn(it, True)
            turn(TURNS - 1, False)

        @block.gpsimd
        def _(pool):
            with pool.Fori(0, FC) as m:
                for j in range(2):
                    pool.wait_ge(w_hi_ready, m * 2 + j + 1)
                    nc.gpsimd.tensor_tensor(w_lo[j][:], w_raw[j][:], w_hi[j][:].bitcast(F32),
                                            ALU.subtract).then_inc(w_lo_ready, 1)

        @block.vector
        def _(v):
            v.sem_inc(f_ready, 4)
            v.sem_inc(acc_done, 2)
            with v.Fori(0, TURNS) as it:
                for b in range(1, DEPTH, 2):
                    v.wait_ge(acc_done, it * DEPTH + b + 3)
                    for n in range(NH):
                        v.wait_ge(silu_ready, it * DEPTH + b + n)
                        v.tensor_tensor(f[:, it * 2 + b // 2, n * HALF:(n + 1) * HALF], banks[2 * b + n], act_g[n][:],
                                        ALU.mult).then_inc(f_ready, 1)


def ffn_out(nc, sem, banks, io, keep):
    psum, f, row = keep["psum"], keep["f"], keep["gate_row"][1]
    T = 4
    with ExitStack() as ctx:
        sb = lambda n, s, d=F32: ctx.enter_context(nc.sbuf_tensor(n, s, d))
        w_raw = [sb(f"u_raw{j}", [P, D]) for j in range(2)]
        w_hi, w_lo = ([sb(f"u_{n}{j}", [P, D], F32R) for j in range(2)] for n in ("hi", "lo"))
        f_hi, f_lo = ([sb(f"uf_{n}{j}", [P, HALF], F32R) for j in range(2)] for n in ("hi", "lo"))
        y = [sb(f"u_y{t}", [P, D]) for t in range(T)]
        x = [sb(f"u_x{t}", [P, D]) for t in range(T)]
        junk = sb("u_junk", [P, D])
        ss = sb("u_ss", [P, T])
        w_in, x_in = [sem(f"fo_w_in{j}") for j in range(2)], sem("fo_x_in")
        w_hi_ready, w_lo_ready, f_hi_ready, f_lo_ready, acc_k, acc_done = (
            sem(f"fo_{n}") for n in ("w_hi", "w_lo", "f_hi", "f_lo", "acc_k", "acc"))
        y_copied, ss_ready, mean_ready, root_ready, out_ready, stored, dve = (
            sem(f"fo_{n}") for n in ("y", "ss", "mean", "root", "out", "stored", "dve"))
        STEPS = NH * FC
        block = ctx.enter_context(nc.Block())

        @block.sync
        def _(sp):
            w_out = io["w_ffn_out"].rearrange("(k p) n -> k p n", p=P)

            def load_x(c):
                for t in range(T):
                    sp.dma_start(x[t][:], io["x_mid"][c * T + t]).then_inc(x_in, 16)

            load_x(0)
            for j in range(2):
                sp.dma_start(w_raw[j][:], w_out[j]).then_inc(w_in[j], 16)
            for c in range(NH):
                with sp.Fori(0, FC // 2 - 1) as it:
                    for j in range(2):
                        sp.wait_ge(w_lo_ready, it * 2 + (j + c * FC + 1))
                        sp.dma_start(w_raw[j][:], w_out[it * 2 + j + 2]).then_inc(w_in[j], 16)
                if c + 1 < NH:
                    for j in range(2):
                        sp.wait_ge(w_lo_ready, c * FC + FC - 1 + j)
                        sp.dma_start(w_raw[j][:], w_out[j]).then_inc(w_in[j], 16)
                for t in range(T):
                    sp.wait_ge(out_ready, c * T + t + 1)
                    sp.dma_start(io["out"][(c * T + t) * P:(c * T + t + 1) * P, :], y[t][:]).then_inc(stored, 16)
                if c + 1 < NH:
                    load_x(c + 1)
            sp.wait_ge(stored, 16 * NH * T)

        @block.tensor
        def _(pe):
            def chunk(step, j, first, last):
                pe.wait_ge(w_lo_ready, step + 1)
                pe.wait_ge(f_lo_ready, step + 1)
                for t in range(T):
                    for n in range(NH):
                        mm = parts_product(pe, banks[2 * t + n],
                                           (f_hi[j][:, t * P:(t + 1) * P], f_lo[j][:, t * P:(t + 1) * P]),
                                           (w_hi[j][:, n * HALF:(n + 1) * HALF], w_lo[j][:, n * HALF:(n + 1) * HALF]),
                                           first, last)
                    if last:
                        mm.then_inc(acc_done, 1)
                if not last:
                    mm.then_inc(acc_k, 1)

            for c in range(NH):
                if c:
                    pe.wait_ge(y_copied, c * T)
                for j in range(2):
                    chunk(c * FC + j, j, j == 0, False)
                with pe.Fori(1, FC // 2 - 1) as it:
                    for j in range(2):
                        chunk(it * 2 + (c * FC + j), j, False, False)
                for j in range(2):
                    chunk(c * FC + FC - 2 + j, j, False, j == 1)

        @block.scalar
        def _(act):
            def cut(step, c, k, j, landed):
                act.wait_ge(w_in[j], landed)
                if c and isinstance(k, int) and k < 2:
                    act.wait_ge(acc_done, c * T)
                act.wait_ge(acc_k, k + (c * (FC - 1) + 1))
                act.activation(w_hi[j][:], w_raw[j][:], ACT.Copy).then_inc(w_hi_ready, 1)
                act.activation(f_hi[j][:], f[:, k, c * HALF:(c + 1) * HALF], ACT.Copy).then_inc(f_hi_ready, 1)

            def copy_out(c):
                for t in range(T):
                    act.wait_ge(acc_done, c * T + t + 1)
                    if c:
                        act.wait_ge(stored, 16 * T * c)
                    act.activation(y[t][:], psum[:, 2 * t * HALF:2 * (t + 1) * HALF], ACT.Copy).then_inc(y_copied, 1)

            def norms(c):
                for t in range(T):
                    n = c * T + t
                    act.wait_ge(y_copied, n + 1)
                    if n:
                        act.wait_ge(ss_ready, n)
                    act.activation(junk[:], y[t][:], ACT.Square, accum_out=ss[:, t:t + 1]).then_inc(ss_ready, 1)
                act.wait_ge(mean_ready, c + 1)
                act.activation(ss[:], ss[:], ACT.Sqrt).then_inc(root_ready, 1)

            act.sem_inc(acc_k, 2)
            for c in range(NH):
                for k in range(2):
                    if c == 0:
                        cut(k, 0, k, k, 16)
                with act.Fori(1, FC // 2) as it:
                    for j in range(2):
                        cut(it * 2 + (c * FC + j), c, it * 2 + j, j, it * 16 + (16 * (c * FC // 2) + 16))
                copy_out(c)
                if c + 1 < NH:
                    for k in range(2):
                        cut((c + 1) * FC + k, c + 1, k, k, 16 * ((c + 1) * FC // 2) + 16)
                norms(c)

        @block.gpsimd
        def _(pool):
            for c in range(NH):
                with pool.Fori(0, FC // 2) as it:
                    for j in range(2):
                        pool.wait_ge(f_hi_ready, it * 2 + (c * FC + j + 1))
                        nc.gpsimd.tensor_tensor(f_lo[j][:], f[:, it * 2 + j, c * HALF:(c + 1) * HALF], f_hi[j][:].bitcast(F32),
                                                ALU.subtract).then_inc(f_lo_ready, 1)

        @block.vector
        def _(v):
            def weight_lo(step, j):
                v.wait_ge(w_hi_ready, step + 1)
                v.tensor_tensor(w_lo[j][:], w_raw[j][:], w_hi[j][:].bitcast(F32), ALU.subtract).then_inc(w_lo_ready, 1)

            ch = Chain(v, dve)
            for k in range(2):
                weight_lo(k, k)
            for c in range(NH):
                with v.Fori(1, FC // 2) as it:
                    for j in range(2):
                        weight_lo(it * 2 + (c * FC + j), j)
                if c + 1 < NH:
                    for k in range(2):
                        weight_lo((c + 1) * FC + k, k)
                v.wait_ge(ss_ready, T * (c + 1))
                v.tensor_scalar(ss[:], ss[:], 1.0 / D, EPS, ALU.mult, ALU.add).then_inc(mean_ready, 1)
                v.wait_ge(root_ready, c + 1)
                ch.link(v.reciprocal(ss[:], ss[:]))
                v.wait_ge(x_in, 16 * T * (c + 1))
                for t in range(T):
                    ch.link(v.scalar_tensor_tensor(out=y[t][:], in0=y[t][:], scalar=ss[:, t:t + 1], in1=row[:], op0=ALU.mult,
                                                   op1=ALU.mult))
                    v.tensor_tensor(y[t][:], y[t][:], x[t][:], ALU.add).then_inc(out_ready, 1)


def tables():
    f = np.float32
    rows = SEQ // GRID_W
    row = np.repeat(np.arange(rows, dtype=f), GRID_W)
    col = np.tile(np.arange(GRID_W, dtype=f), rows)
    n_freq = HD // 4
    inv = (f(ROPE_THETA) ** (-np.arange(n_freq, dtype=f) / f(n_freq))).astype(f)
    ang = np.concatenate([row[:, None] * inv, col[:, None] * inv], axis=-1).astype(f)
    cos, sin = np.cos(ang).astype(f), np.sin(ang).astype(f)
    cos2 = np.repeat(cos, 2, axis=1)
    sin2 = np.stack([-sin, sin], axis=-1).reshape(SEQ, HD)
    turn = lambda a: np.ascontiguousarray(a.reshape(TL, P, HD).transpose(1, 0, 2))
    q, j = np.arange(P)[:, None], np.arange(P)[None, :]
    mask = np.zeros((P, 3, P), f)
    mask[:, 0, :] = np.where(j >= q, 0.0, MASKED)
    mask[:, 2, :] = np.where(j <= q, 0.0, MASKED)
    t = np.arange(SEQ)
    inv_count = np.stack([1.0 / (np.clip(t + w - w // 2, 0, SEQ) - np.clip(t - w // 2, 0, SEQ)) for w in POOL_WINDOWS])
    return {"cosT": turn(cos2), "sinT": turn(sin2), "ident": np.eye(P, dtype=f), "mask": mask.reshape(P, 3 * P),
            "inv_count": inv_count.astype(f)}


def lay_out(x, c, ctx, c_ctx, w_ada, b_ada, norm_g, w_in, da_lambda, da_subln_g, pool_w, pool_scale, wa_sink,
            w_branch, w_out, w_ffn_in, w_ffn_out):
    a = lambda v: np.ascontiguousarray(v)
    w = np.asarray(w_in)[0]
    q0, k0, v0, u0 = 0, 512, 1024, 1536
    qw0, kw0, vw0, g0 = 2048, 2560, 2688, 2816
    groups = [[(q0 + h * P, P), (k0 + h * P, P), (v0 + h * P, P)] for h in range(DA_HEADS)]
    groups += [[(qw0 + 6 * HD, P), (kw0, P), (vw0, P)], [(qw0, GW)]]
    chunks = lambda m: m.reshape(m.shape[0] // P, P, -1).transpose(1, 0, 2)
    w_tok = a(np.stack([chunks(np.concatenate([w[:, s:s + n] for s, n in g], axis=1)) for g in groups]))
    feat = np.concatenate([w[:, u0:u0 + BW], w[:, g0:]], axis=1)
    w_feat = a(feat.reshape(KC, P, -1, P).transpose(2, 1, 0, 3))
    w_br = a(np.asarray(w_branch)[0].reshape(3, BC, P, KC, P).transpose(3, 2, 0, 1, 4))
    w_ff = a(np.asarray(w_ffn_in)[0].reshape(KC, P, 2, FC, P).transpose(3, 2, 1, 0, 4))
    cT = a(np.stack([np.asarray(c)[0], np.asarray(c_ctx)]).reshape(2, KC, P).transpose(2, 0, 1))
    return {
        "x": a(np.asarray(x)[0]), "ctx": a(np.asarray(ctx)[0]), "cT": cT,
        "w_ada": a(np.asarray(w_ada)[0]), "b_adaT": a(np.asarray(b_ada)[0].reshape(6 * KC, P).T), "b_ada": a(b_ada),
        "norm_gT": a(np.asarray(norm_g)[0].reshape(4, KC, P).transpose(2, 0, 1)), "norm_g": a(np.asarray(norm_g)[0]),
        "w_tok": w_tok, "w_feat": w_feat, "da_lambda": a(np.asarray(da_lambda)[0].reshape(1, -1)),
        "sub_g": a(np.asarray(da_subln_g)[0].reshape(P, 1)), "pool_w": a(np.asarray(pool_w)[0].transpose(1, 0, 2)),
        "pool_scaleT": a(np.asarray(pool_scale)[0].reshape(BC, P).T), "wa_sink": a(np.asarray(wa_sink)),
        "w_br": w_br, "w_out": a(np.asarray(w_out)[0]), "w_ff": w_ff, "w_ffn_out": a(np.asarray(w_ffn_out)[0]),
    }


SCRATCH = {"stacks_da": [DA_HEADS, 4, P, TOK], "stacks_wa": [10, P, TOK], "vals": [DA_HEADS + 1, TT, P, 2 * P],
           "gates": [3, KC, P, SEQ], "yb": [BC, P, SEQ], "ya": [BC, P, SEQ], "x_mid": [TL, P, D]}


def program(nc, io, upto=99):
    with ExitStack() as ctx:
        taken = []

        def sem(name):
            taken.append(nc.alloc_semaphore(name=name))
            return taken[-1]

        tensor = lambda stack, n, s, d=F32, side="left": stack.enter_context(nc.sbuf_tensor(n, s, d, side=side))
        psum = ctx.enter_context(nc.psum_tensor("psum", [P, 8 * HALF], F32))
        banks = [psum[:, i * HALF:(i + 1) * HALF] for i in range(8)]
        keep = {"psum": psum, "silu_x": tensor(ctx, "silu_x", [P, KC]), "ident": tensor(ctx, "ident", [P, P]),
                "neg_lam": tensor(ctx, "neg_lam", [P, 1]), "sub_g": tensor(ctx, "sub_g_sb", [P, 1]),
                "gate_row": [tensor(ctx, f"gate_row{i}", [P, D]) for i in range(2)],
                "A2": tensor(ctx, "A2", [P, KC]), "B2": tensor(ctx, "B2", [P, KC])}
        with ExitStack() as first:
            keep["h_hi"] = tensor(first, "h_hi", [P, KC, TOK], F32R)
            keep["h_lo"] = tensor(first, "h_lo", [P, KC, TOK], F32R)
            prepare(nc, sem, banks, io, keep)
            if upto >= 2:
                project(nc, sem, banks, io, keep)
            if upto >= 3:
                features(nc, sem, banks, io, keep)
        if upto >= 4:
            diff(nc, sem, banks, io, keep)
        if upto < 5:
            return
        nc.clear_and_free_semaphores(taken)
        nc.all_engine_barrier()
        with ExitStack() as ys, ExitStack() as ms:
            for part in ("hi", "lo"):
                keep[f"y_{part}"] = [tensor(ys, f"y_{part}{i}", [P, BC, SEQ], F32R) for i in range(3)]
            window(nc, sem, banks, io, keep)
            keep["m"] = tensor(ms, "m", [P, KC, SEQ], F32, "right")
            if upto >= 6:
                merge(nc, sem, banks, io, keep)
            ys.close()
            with ExitStack() as h2:
                keep["h2_hi"] = tensor(h2, "h2_hi", [P, KC, SEQ], F32R)
                keep["h2_lo"] = tensor(h2, "h2_lo", [P, KC, SEQ], F32R)
                if upto >= 7:
                    residual(nc, sem, banks, io, keep)
                ms.close()
                keep["f"] = tensor(ctx, "f", [P, FC, SEQ], F32, "right")
                if upto >= 8:
                    ffn_in(nc, sem, banks, io, keep)
        if upto >= 9:
            ffn_out(nc, sem, banks, io, keep)


def kernel(**inputs):
    import concourse.bacc as bacc
    from concourse.bass_utils import run_bass_kernel_spmd

    laid = lay_out(**inputs)
    laid.update(tables())
    nc = bacc.Bacc("TRN2", target_bir_lowering=False, num_devices=1)
    io = {k: nc.dram_tensor(f"in_{k}", a.shape, mybir.dt.from_np(a.dtype), kind="ExternalInput").ap()
          for k, a in laid.items()}
    for k, shape in SCRATCH.items():
        io[k] = nc.dram_tensor(f"{k}_dram", shape, F32, kind="Internal").ap()
    io["out"] = nc.dram_tensor("out", [SEQ, D], F32, kind="ExternalOutput").ap()
    program(nc, io)
    result = run_bass_kernel_spmd(nc, [{f"in_{k}": a for k, a in laid.items()}], core_ids=[0])
    return result.results[0]["out"].reshape(1, SEQ, D)
```

```python
import math
from contextlib import ExitStack

import numpy as np

import concourse.bass as bass
from concourse import mybir

F32 = mybir.dt.float32
F32R = mybir.dt.float32r
ALU = mybir.AluOpType
ACT = mybir.ActivationFunctionType
AX = mybir.AxisListType

P = 128
D = 1024
SEQ = 1024
CTX = 256
TOK = SEQ + CTX
KC = D // P
TL = SEQ // P
TT = TOK // P
HALF = 512
NH = SEQ // HALF
GRID_W = 64
EPS = 1e-6
ROPE_THETA = 10000.0
HD = 64
DA_HEADS = 4
DA_V = 128
WA_HEADS = 8
WA_KV = 2
WA_GROUP = WA_HEADS // WA_KV
BW = 512
BC = BW // P
POOL_WINDOWS = (2, 4, 8, 16)
D_FF = ((8 * D + 3 * 256 - 1) // (3 * 256)) * 256
FC = D_FF // P
LAM_INIT = 0.8 - 0.6 * math.exp(-0.3 * 0)
SCALE = HD ** -0.5
MASKED = -1e30
GW = 3 * P
UNITS = 6


def parts_product(pe, out, stat, mov, first, last):
    (sh, sl), (mh, ml) = stat, mov
    pe.matmul(out, sh, mh, start=first, stop=False)
    pe.matmul(out, sh, ml, start=False, stop=False)
    return pe.matmul(out, sl, mh, start=False, stop=last)


class Chain:

    def __init__(self, eng, sem, base=0):
        self.eng, self.sem, self.base, self.n = eng, sem, base, 0

    def did(self, ins):
        ins.then_inc(self.sem, 1)
        self.n += 1

    def settle(self):
        self.eng.wait_ge(self.sem, self.base + self.n)

    def link(self, ins):
        self.did(ins)
        self.settle()


def prepare(nc, sem, banks, io, keep):
    h_hi, h_lo, ident, neg_lam, sub_g = keep["h_hi"], keep["h_lo"], keep["ident"], keep["neg_lam"], keep["sub_g"]
    ADA = 4
    UN = [(c, k) for c in range(3) for k in range(KC)]
    with ExitStack() as ctx:
        sb = lambda n, s, d=F32: ctx.enter_context(nc.sbuf_tensor(n, s, d))
        xt = sb("xt", [P, TT, D])
        ada = [sb(f"ada{j}", [P, KC, HALF]) for j in range(ADA)]
        junk = sb("junk", [P, D])
        full = sb("full", [P, 2, HALF])
        cond = sb("cond", [P, 2, KC])
        econd = sb("econd", [P, 2, KC])
        silu = sb("silu", [P, KC, 2])
        ada_b = sb("ada_b", [P, 48])
        norm_g = sb("norm_g", [P, 4, KC])
        mod = sb("mod", [P, 2 * KC, 2])
        A = sb("A", [P, KC, 2])
        lamv = sb("lamv", [P, 4, HD])
        lamp = sb("lamp", [P, 2, HD])
        lamd = sb("lamd", [P, 4])
        ss = sb("ss", [P, TT])
        rs = sb("rs", [P, TT])
        small_in, x_in = sem("pr_small_in"), [sem(f"pr_x_in{j}") for j in range(3)]
        ada_in = [sem(f"pr_ada_in{j}") for j in range(ADA)]
        e_ready, silu_ready, ada_done, ab_ready = sem("pr_e"), sem("pr_silu"), sem("pr_ada_done"), sem("pr_ab")
        sq_done, mean_ready, rs_ready, xn_ready = sem("pr_sq"), sem("pr_mean"), sem("pr_rs"), sem("pr_xn")
        turned, full_ready, h_ready, dve, act_own = sem("pr_turned"), sem("pr_full"), sem("pr_h"), sem("pr_dve"), sem("pr_act")
        lam_dots, lam_exp = sem("pr_lam_dots"), sem("pr_lam_exp")
        CH = [range(0, 4), range(4, 8), range(8, 10)]

        block = ctx.enter_context(nc.Block())

        @block.sync
        def _(sp):
            for dst, src in ((cond, io["cT"]), (ada_b, io["b_adaT"]), (norm_g, io["norm_gT"]), (ident, io["ident"]),
                             (sub_g, io["sub_g"])):
                sp.dma_start(dst[:], src).then_inc(small_in, 16)
            sp.dma_start(lamv[:].rearrange("p a b -> p (a b)"),
                         io["da_lambda"].to_broadcast([P, 4 * HD])).then_inc(small_in, 16)
            xv = io["x"].rearrange("(t p) d -> p t d", p=P)
            cv = io["ctx"].rearrange("(t p) d -> p t d", p=P)
            av = io["w_ada"].rearrange("(k p) n -> p k n", p=P)
            sp.dma_start(xt[:, 0:4, :], xv[:, 0:4, :]).then_inc(x_in[0], 16)
            for j in range(ADA):
                sp.dma_start(ada[j][:], av[:, :, j * HALF:(j + 1) * HALF]).then_inc(ada_in[j], 16)
                if j == 1:
                    sp.dma_start(xt[:, 4:8, :], xv[:, 4:8, :]).then_inc(x_in[1], 16)
                    sp.dma_start(xt[:, 8:10, :], cv).then_inc(x_in[2], 16)

        @block.tensor
        def _(pe):
            pe.wait_ge(silu_ready, 1)
            for j in range(ADA):
                pe.wait_ge(ada_in[j], 16)
                for b in range(4):
                    n = 4 * j + b
                    for k in range(KC):
                        mm = pe.matmul(banks[7][:, 2 * n:2 * n + 2], ada[j][:, k, b * P:(b + 1) * P], silu[:, k, :],
                                       start=(k == 0), stop=(k == KC - 1))
            mm.then_inc(ada_done, 1)
            for u, (c, k) in enumerate(UN):
                pe.wait_ge(xn_ready, [4, 8, 10][c])
                if u >= 4:
                    pe.wait_ge(full_ready, u - 3)
                for j, t in enumerate(CH[c]):
                    mm = pe.transpose(banks[u % 4][:, j * P:(j + 1) * P], xt[:, t, k * P:(k + 1) * P], ident[:])
                mm.then_inc(turned, 1)

        @block.scalar
        def _(act):
            act.wait_ge(small_in, 96)
            act.activation(econd[:], cond[:], ACT.Exp, scale=-1.0).then_inc(e_ready, 1)
            act.wait_ge(lam_dots, 1)
            act.activation(lamd[:, 2:4], lamd[:, 0:2], ACT.Exp).then_inc(lam_exp, 1)
            for t in range(TT):
                if t in (0, 4, 8):
                    act.wait_ge(x_in[t // 4], 16)
                if t:
                    act.wait_ge(sq_done, t)
                act.activation(junk[:], xt[:, t, :], ACT.Square, accum_out=ss[:, t:t + 1]).then_inc(sq_done, 1)
                if t == CH[t // 4][-1]:
                    act.wait_ge(mean_ready, t // 4 + 1)
                    act.activation(rs[:, t // 4 * 4:t + 1], ss[:, t // 4 * 4:t + 1], ACT.Sqrt).then_inc(rs_ready, 1)
            act.wait_ge(ab_ready, 2)
            for u, (c, k) in enumerate(UN):
                w = len(CH[c]) * P
                act.wait_ge(turned, u + 1)
                if u >= 2:
                    act.wait_ge(h_ready, u - 1)
                i = 1 if c == 2 else 0
                act.activation(full[:, u % 2, 0:w], banks[u % 4][:, 0:w], ACT.Identity, scale=A[:, k, i:i + 1],
                               bias=mod[:, k, i:i + 1]).then_inc(full_ready, 1)

        @block.vector
        def _(v):
            ch = Chain(v, dve)
            v.wait_ge(small_in, 96)
            v.wait_ge(e_ready, 1)
            ch.link(v.tensor_scalar(econd[:], econd[:], 1.0, None, ALU.add))
            ch.link(v.reciprocal(econd[:], econd[:]))
            v.tensor_tensor(silu[:].rearrange("p k c -> p c k"), cond[:], econd[:], ALU.mult).then_inc(silu_ready, 1)
            ch.link(v.tensor_tensor(keep["silu_x"][:], cond[:, 0, :], econd[:, 0, :], ALU.mult))
            for i in range(2):
                ins = v.tensor_tensor_reduce(out=lamp[:, i, :], in0=lamv[:, 2 * i, :], in1=lamv[:, 2 * i + 1, :],
                                             scale=1.0, scalar=0.0, op0=ALU.mult, op1=ALU.add,
                                             accum_out=lamd[:, i:i + 1])
            ins.then_inc(lam_dots, 1)
            v.wait_ge(lam_exp, 1)
            ch.did(v.scalar_tensor_tensor(out=neg_lam[:], in0=lamd[:, 3:4], scalar=-LAM_INIT, in1=lamd[:, 2:3],
                                          op0=ALU.add, op1=ALU.subtract))
            ch.link(v.tensor_scalar(sub_g[:], sub_g[:], 1.0 - LAM_INIT, None, ALU.mult))
            for c in range(3):
                a, b = CH[c][0], CH[c][-1] + 1
                v.wait_ge(sq_done, b)
                v.tensor_scalar(ss[:, a:b], ss[:, a:b], 1.0 / D, EPS, ALU.mult, ALU.add).then_inc(mean_ready, 1)
                v.wait_ge(rs_ready, c + 1)
                ch.link(v.reciprocal(rs[:, a:b], rs[:, a:b]))
                for t in CH[c]:
                    v.tensor_scalar(xt[:, t, :], xt[:, t, :], rs[:, t:t + 1], None, ALU.mult).then_inc(xn_ready, 1)
            v.wait_ge(ada_done, 1)
            for i in range(2):
                ch.did(v.tensor_tensor(mod[:, :, i], banks[7][:, i:4 * KC:2], ada_b[:, 0:2 * KC], ALU.add))
            ch.settle()
            for i in range(2):
                v.scalar_tensor_tensor(out=A[:, :, i], in0=mod[:, KC:2 * KC, i], scalar=1.0, in1=norm_g[:, 0, :],
                                       op0=ALU.add, op1=ALU.mult).then_inc(ab_ready, 1)
            for u, (c, k) in enumerate(UN):
                w, t0 = len(CH[c]) * P, CH[c][0] * P
                v.wait_ge(full_ready, u + 1)
                ch.link(v.tensor_copy(h_hi[:, k, t0:t0 + w], full[:, u % 2, 0:w]))
                v.tensor_tensor(h_lo[:, k, t0:t0 + w], full[:, u % 2, 0:w], h_hi[:, k, t0:t0 + w].bitcast(F32),
                                ALU.subtract).then_inc(h_ready, 1)


def project(nc, sem, banks, io, keep):
    h_hi, h_lo, ident = keep["h_hi"], keep["h_lo"], keep["ident"]
    with ExitStack() as ctx:
        sb = lambda n, s, d=F32: ctx.enter_context(nc.sbuf_tensor(n, s, d))
        w_raw = [sb(f"w_raw{j}", [P, KC, GW]) for j in range(2)]
        w_hi = [sb(f"w_hi{j}", [P, KC, GW], F32R) for j in range(2)]
        w_lo = [sb(f"w_lo{j}", [P, KC, GW], F32R) for j in range(2)]
        cosT, sinT = sb("cosT", [P, TL, HD]), sb("sinT", [P, TL, HD])
        raw = [sb(f"raw{j}", [P, GW]) for j in range(2)]
        rot = sb("rot", [P, UNITS, HD])
        swp = sb("swp", [P, UNITS, HD])
        cut = [sb(f"cut{j}", [P, UNITS, 2, HD], F32R) for j in range(2)]
        st = [sb(f"st{j}", [P, UNITS, P], F32R) for j in range(2)]
        table_in, w_in = sem("pj_table_in"), [sem(f"pj_w_in{j}") for j in range(2)]
        w_hi_ready, w_lo_ready = sem("pj_w_hi"), sem("pj_w_lo")
        acc_done, raw_ready, cut_ready = sem("pj_acc"), sem("pj_raw"), sem("pj_cut")
        turned, st_ready, dve = sem("pj_turned"), sem("pj_st"), sem("pj_dve")
        st_out, v_out = [sem(f"pj_st_out{j}") for j in range(2)], [sem(f"pj_v_out{j}") for j in range(2)]

        def content(kind, t):
            if kind == "q":
                return 0, 6, False
            return (0, 4, True) if t < TL else (P, 2, True)

        def tiles(kind):
            return TL if kind == "q" else TT

        LOOP_KINDS, LAST_KINDS = ("kv", "kv"), ("kv", "q")
        LAST = 2

        def item(it, j, t):
            return (it * 2 + j) * TT + t

        def uses(it, j, t):
            return (it * 2 + j) * (TT // 2) + t // 2

        CR = 2
        block = ctx.enter_context(nc.Block())

        @block.sync
        def _(sp):
            sp.dma_start(cosT[:], io["cosT"]).then_inc(table_in, 16)
            sp.dma_start(sinT[:], io["sinT"]).then_inc(table_in, 16)
            for j in range(2):
                sp.dma_start(w_raw[j][:], io["w_tok"][j]).then_inc(w_in[j], 16)

            def turn(it, kinds, stacks, more):
                for j, kind in enumerate(kinds):
                    if more:
                        sp.wait_ge(w_lo_ready, (it * 2 + j + 1) * KC)
                        sp.dma_start(w_raw[j][:], io["w_tok"][it * 2 + j + 2]).then_inc(w_in[j], 16)
                    for t in range(tiles(kind)):
                        col, units, has_v = content(kind, t)
                        skip = 4 - units if kind == "kv" else 0
                        if has_v:
                            sp.wait_ge(raw_ready, item(it, j, t) + 1 + 4)
                            sp.dma_start(io["vals"][it * 2 + j, t], raw[t % 2][:, 2 * P:GW]).then_inc(v_out[t % 2], 16)
                        sp.wait_ge(st_ready, item(it, j, t) + 1 + CR)
                        sp.dma_start(stacks(j)[skip:skip + units, :, t * P:(t + 1) * P].rearrange("u p n -> p u n"),
                                     st[t % 2][:, 0:units, :].bitcast(F32)).then_inc(st_out[t % 2], 16)

            with sp.Fori(0, LAST) as it:
                turn(it, LOOP_KINDS, lambda j: io["stacks_da"][it * 2 + j], True)
            turn(LAST, LAST_KINDS, lambda j: io["stacks_wa"][4 * j:4 * j + 4 + 2 * j], False)
            for s in range(2):
                sp.wait_ge(st_out[s], 16 * (uses(LAST, 1, TL) + 1))
                sp.wait_ge(v_out[s], 16 * (uses(LAST, 1, 0) + 1))

        @block.tensor
        def _(pe):
            def accumulate(it, j, t, kind):
                col, units, has_v = content(kind, t)
                bank = banks[(2 * j + t) % 4]
                pe.wait_ge(raw_ready, item(it, j, t) + 1)
                for k in range(KC):
                    mm = parts_product(pe, bank[:, col:GW], (h_hi[:, k, t * P:(t + 1) * P], h_lo[:, k, t * P:(t + 1) * P]),
                                       (w_hi[j][:, k, col:GW], w_lo[j][:, k, col:GW]), k == 0, k == KC - 1)
                mm.then_inc(acc_done, 1)

            def turn_units(it, j, t, kind):
                col, units, has_v = content(kind, t)
                pe.wait_ge(cut_ready, item(it, j, t) + 1 + CR)
                pe.wait_ge(st_ready, item(it, j, t) + 1)
                for u in range(units):
                    mm = pe.transpose(banks[4 + 2 * (t % 2) + u // 4][:, (u % 4) * P:(u % 4 + 1) * P],
                                      cut[t % 2][:, u, :, :].rearrange("p a d -> p (a d)").bitcast(F32), ident[:])
                mm.then_inc(turned, 1)

            def turn(it, kinds):
                todo = [(j, t, kind) for j, kind in enumerate(kinds) for t in range(tiles(kind))]
                for i, (j, t, kind) in enumerate(todo):
                    if t == 0:
                        pe.wait_ge(w_lo_ready, (it * 2 + j + 1) * KC)
                    accumulate(it, j, t, kind)
                    if i:
                        jj, tt, kk = todo[i - 1]
                        turn_units(it, jj, tt, kk)
                turn_units(it, j, t, kind)

            pe.sem_inc(turned, CR)
            with pe.Fori(0, LAST) as it:
                turn(it, LOOP_KINDS)
            turn(LAST, LAST_KINDS)

        @block.scalar
        def _(act):
            def weight_hi(group, slot, k, landed):
                act.wait_ge(w_in[slot], landed)
                act.activation(w_hi[slot][:, k, :], w_raw[slot][:, k, :], ACT.Copy).then_inc(w_hi_ready, 1)

            def copy_units(it, j, t, kind):
                col, units, has_v = content(kind, t)
                act.wait_ge(turned, item(it, j, t) + 1 + CR)
                act.wait_ge(st_out[t % 2], 16 * uses(it, j, t) + 16)
                b = 4 + 2 * (t % 2)
                n = min(units, 4)
                ins = act.activation(st[t % 2][:, 0:n, :], banks[b][:, 0:n * P].rearrange("p (u n) -> p u n", n=P), ACT.Copy)
                if units > 4:
                    ins = act.activation(st[t % 2][:, 4:units, :],
                                         banks[b + 1][:, 0:(units - 4) * P].rearrange("p (u n) -> p u n", n=P), ACT.Copy)
                ins.then_inc(st_ready, 1)

            def turn(it, kinds, more):
                todo = [(j, t, kind) for j, kind in enumerate(kinds) for t in range(tiles(kind))]
                for i, (j, t, kind) in enumerate(todo):
                    col, units, has_v = content(kind, t)
                    act.wait_ge(acc_done, item(it, j, t) + 1)
                    act.wait_ge(cut_ready, item(it, j, t) + 1)
                    act.wait_ge(v_out[t % 2], 16 * uses(it, j, t if kind == "kv" else 0) + 16)
                    act.activation(raw[t % 2][:, col:GW], banks[(2 * j + t) % 4][:, col:GW], ACT.Copy).then_inc(raw_ready, 1)
                    if (j == 0 or more) and t < KC:
                        weight_hi(it * 2 + j + 1, 1 - j, t, 16 * (it + j + 1))
                    if i:
                        jj, tt, kk = todo[i - 1]
                        copy_units(it, jj, tt, kk)
                copy_units(it, j, t, kind)

            act.sem_inc(raw_ready, 4)
            act.sem_inc(st_ready, CR)
            for s in range(2):
                act.sem_inc(st_out[s], 16)
                act.sem_inc(v_out[s], 16)
            for k in range(KC):
                weight_hi(0, 0, k, 16)
            with act.Fori(0, LAST) as it:
                turn(it, LOOP_KINDS, True)
            turn(LAST, LAST_KINDS, False)

        @block.gpsimd
        def _(pool):
            def weight_lo(group, slot):
                for k in range(KC):
                    pool.wait_ge(w_hi_ready, group * KC + k + 1)
                    nc.gpsimd.tensor_tensor(w_lo[slot][:, k, :], w_raw[slot][:, k, :], w_hi[slot][:, k, :].bitcast(F32),
                                            ALU.subtract).then_inc(w_lo_ready, 1)

            with pool.Fori(0, LAST + 1) as it:
                for j in range(2):
                    weight_lo(it * 2 + j, j)

        @block.vector
        def _(v):
            def cut_tile(ch, it, j, t, kind):
                col, units, has_v = content(kind, t)
                src, c = raw[t % 2], cut[t % 2]
                v.wait_ge(raw_ready, item(it, j, t) + 1 + 4)
                v.wait_ge(turned, item(it, j, t) + 1)
                x = src[:, col:col + units * HD].rearrange("p (u d) -> p u d", d=HD)
                if t < TL:
                    v.wait_ge(cut_ready, item(it, j, t) + CR)
                    cs = cosT[:, t:t + 1, :].to_broadcast([P, units, HD])
                    sn = sinT[:, t:t + 1, :].to_broadcast([P, units, HD])
                    ch.did(v.tensor_tensor(rot[:, 0:units, :], x, cs, ALU.mult))
                    ch.did(v.tensor_tensor(swp[:, 0:units, 0:HD:2], x[:, :, 1:HD:2], sn[:, :, 0:HD:2], ALU.mult))
                    ch.link(v.tensor_tensor(swp[:, 0:units, 1:HD:2], x[:, :, 0:HD:2], sn[:, :, 1:HD:2], ALU.mult))
                    x = rot[:, 0:units, :]
                    ch.link(v.tensor_tensor(x, x, swp[:, 0:units, :], ALU.add))
                ch.did(v.tensor_copy(c[:, 0:units, 0, :], x))
                ch.settle()
                v.tensor_tensor(c[:, 0:units, 1, :], x, c[:, 0:units, 0, :].bitcast(F32), ALU.subtract)\
                 .then_inc(cut_ready, 1)

            OWN = 2 * (5 * TL + (TT - TL))
            v.sem_inc(cut_ready, CR)
            v.wait_ge(table_in, 32)

            def turn(it, kinds):
                ch = Chain(v, dve, it * OWN)
                for j, kind in enumerate(kinds):
                    for t in range(tiles(kind)):
                        cut_tile(ch, it, j, t, kind)
                return ch.n

            with v.Fori(0, LAST) as it:
                assert turn(it, LOOP_KINDS) == OWN
            turn(LAST, LAST_KINDS)


def wide_product(pe, outs, stat, movs, first, last):
    sh, sl = stat
    for out, (mh, ml) in zip(outs, movs):
        pe.matmul(out, sh, mh, start=first, stop=False)
        pe.matmul(out, sh, ml, start=False, stop=False)
    for out, (mh, ml) in zip(outs, movs):
        mm = pe.matmul(out, sl, mh, start=False, stop=last)
    return mm


def features(nc, sem, banks, io, keep):
    h_hi, h_lo, psum = keep["h_hi"], keep["h_lo"], keep["psum"]
    silu_x, A2, B2, gate_row = keep["silu_x"], keep["A2"], keep["B2"], keep["gate_row"]
    G = len(POOL_WINDOWS)
    TILES = G + 3 * KC
    TURNS = 3 * KC // 2
    PAD = max(POOL_WINDOWS) // 2
    AC = P
    PIECES = 4 * D // AC
    A_TURNS = PIECES // 4
    with ExitStack() as ctx:
        sb = lambda n, s, d=F32: ctx.enter_context(nc.sbuf_tensor(n, s, d))
        w_raw = [sb(f"f_raw{j}", [P, KC, P]) for j in range(2)]
        w_hi = [sb(f"f_hi{j}", [P, KC, P], F32R) for j in range(2)]
        w_lo = [sb(f"f_lo{j}", [P, KC, P], F32R) for j in range(2)]
        gst = [sb(f"gst{j}", [P, HALF]) for j in range(2)]
        upad = sb("upad", [P, SEQ + 2 * PAD])
        win = [sb(f"win{j}", [P, SEQ + 2 * PAD]) for j in range(2)]
        inv = sb("inv", [P, SEQ])
        pl_hi, pl_lo = sb("pl_hi", [P, SEQ], F32R), sb("pl_lo", [P, SEQ], F32R)
        pw = sb("pw", [P, G, P])
        pw_hi, pw_lo = sb("pw_hi", [P, G, P], F32R), sb("pw_lo", [P, G, P], F32R)
        pscale = sb("pscale", [P, G])
        piece = [sb(f"piece{j}", [P, KC, AC]) for j in range(2)]
        acc = sb("acc", [P, 4 * D])
        brow, grow = sb("brow", [P, D]), sb("grow", [P, D])
        ones = sb("ones", [P, P])
        badaT, ngT = sb("badaT", [P, 6 * KC]), sb("ngT", [P, 4, KC])
        m2 = sb("m2", [P, 2 * KC])
        small_in, inv_in, row_in = sem("ft_small_in"), sem("ft_inv_in"), sem("ft_row_in")
        w_in, piece_in = [sem(f"ft_w_in{j}") for j in range(2)], [sem(f"ft_piece_in{j}") for j in range(2)]
        w_hi_ready, w_lo_ready, acc_done, taken = sem("ft_w_hi"), sem("ft_w_lo"), sem("ft_acc"), sem("ft_taken")
        gst_ready, gst_out = sem("ft_gst"), [sem(f"ft_gst_out{j}") for j in range(2)]
        upad_clear, u_ready, u_used, pooled, pool_done, yb_ready = (sem(f"ft_{n}") for n in
                                                        ("clear", "u", "u_used", "pooled", "pool_done", "yb"))
        yb_out, piece_used, ada_ready, dve = sem("ft_yb_out"), sem("ft_piece_used"), sem("ft_ada"), sem("ft_dve")
        pw_ready, rows_done, row_used = sem("ft_pw"), sem("ft_rows"), sem("ft_row_used")
        gates = io["gates"].rearrange("i m p n -> (i m) p n")
        block = ctx.enter_context(nc.Block())

        @block.sync
        def _(sp):
            for j in range(2):
                sp.dma_start(w_raw[j][:], io["w_feat"][j]).then_inc(w_in[j], 16)
            for dst, src in ((pw, io["pool_w"]), (pscale, io["pool_scaleT"]), (badaT, io["b_adaT"]), (ngT, io["norm_gT"])):
                sp.dma_start(dst[:], src).then_inc(small_in, 16)

            def load_w(f, slot):
                sp.wait_ge(w_lo_ready, f - 1)
                sp.dma_start(w_raw[slot][:], io["w_feat"][f]).then_inc(w_in[slot], 16)

            def load_piece(q, slot):
                sp.wait_ge(piece_used, q + 1)
                sp.dma_start(piece[slot][:], io["w_ada"].rearrange("(k p) n -> p k n", p=P)
                             .rearrange("p k (a n) -> a p k n", n=AC)[2 * D // AC + q]).then_inc(piece_in[slot], 16)

            def store_gate(f):
                for n in range(NH):
                    sp.wait_ge(gst_ready, (f - G) * NH + n + 1)
                    sp.dma_start(gates[f - G][:, n * HALF:(n + 1) * HALF], gst[n][:]).then_inc(gst_out[n], 16)

            for g in range(G):
                if g:
                    sp.wait_ge(pooled, g)
                sp.dma_start(inv[:], io["inv_count"][g:g + 1, :].to_broadcast([P, SEQ])).then_inc(inv_in, 16)
                load_w(g + 2, g % 2)
                if g >= 1:
                    sp.wait_ge(yb_ready, g)
                    sp.dma_start(io["yb"][g - 1], win[1][:, 0:SEQ]).then_inc(yb_out, 16)

            def turn(it, pieces, more):
                for j in range(2):
                    f = it * 2 + G + j
                    if more:
                        load_w(f + 2, j)
                    for q in range(2 * pieces):
                        load_piece((it - 1) * 4 + 2 * j + q, q)
                    store_gate(f)

            load_w(G + 2, 0)
            sp.wait_ge(yb_ready, G)
            sp.dma_start(io["yb"][G - 1], win[1][:, 0:SEQ]).then_inc(yb_out, 16)
            store_gate(G)
            load_w(G + 3, 1)
            store_gate(G + 1)
            with sp.Fori(1, 1 + A_TURNS) as it:
                turn(it, 1, True)
            with sp.Fori(1 + A_TURNS, TURNS - 1) as it:
                turn(it, 0, True)
            for i in range(2):
                if i:
                    sp.wait_ge(row_used, 1)
                sp.dma_start(brow[:], io["b_ada"][0:1, (2 + 3 * i) * D:(3 + 3 * i) * D].to_broadcast([P, D])).then_inc(row_in, 16)
                sp.dma_start(grow[:], io["norm_g"][1 + 2 * i:2 + 2 * i, :].to_broadcast([P, D])).then_inc(row_in, 16)
                if not i:
                    turn(TURNS - 1, 0, False)
            for n in range(NH):
                sp.wait_ge(gst_out[n], 16 * (3 * KC + 1))
            sp.wait_ge(yb_out, 16 * G)

        @block.tensor
        def _(pe):
            def tile(f, slot):
                pe.wait_ge(w_lo_ready, f + 1)
                pe.wait_ge(taken, f + 1)
                for k in range(KC):
                    mm = wide_product(pe, [banks[2 * slot + n][:, :] for n in range(NH)],
                                      (w_hi[slot][:, k, :], w_lo[slot][:, k, :]),
                                      [(h_hi[:, k, n * HALF:(n + 1) * HALF], h_lo[:, k, n * HALF:(n + 1) * HALF])
                                       for n in range(NH)], k == 0, k == KC - 1)
                mm.then_inc(acc_done, 1)

            def pool_tile(g):
                pe.wait_ge(pooled, g + 1)
                if g == 0:
                    pe.wait_ge(pw_ready, 1)
                else:
                    pe.wait_ge(yb_ready, g)
                wide_product(pe, [banks[4 + n][:, :] for n in range(NH)], (pw_hi[:, g, :], pw_lo[:, g, :]),
                             [(pl_hi[:, n * HALF:(n + 1) * HALF], pl_lo[:, n * HALF:(n + 1) * HALF])
                              for n in range(NH)], True, True).then_inc(pool_done, 1)

            pe.sem_inc(acc_done, 2)
            for f in range(G):
                tile(f, f % 2)
                if f:
                    pool_tile(f - 1)
            tile(G, 0)
            pool_tile(G - 1)
            tile(G + 1, 1)
            with pe.Fori(1, TURNS) as it:
                for j in range(2):
                    tile(it * 2 + G + j, j)
            pe.wait_ge(ada_ready, 1)
            for i in range(2):
                for n in range(NH):
                    pe.matmul(banks[4 + 2 * i + n][:, :], ones[:], acc[:, 3 * i * D + n * HALF:3 * i * D + (n + 1) * HALF],
                              start=True, stop=True)
            pe.wait_ge(taken, TILES + 2)
            for b in range(2 * KC):
                mm = pe.matmul(banks[0][:, b:b + 1], acc[:, D + b * P:D + (b + 1) * P], ones[:, 0:1], start=True, stop=True)
            mm.then_inc(rows_done, 1)

        @block.scalar
        def _(act):
            def weight_hi(f, slot, landed):
                act.wait_ge(w_in[slot], landed)
                act.wait_ge(acc_done, f + 1)
                act.activation(w_hi[slot][:], w_raw[slot][:], ACT.Copy).then_inc(w_hi_ready, 1)

            def gate(f, slot):
                act.wait_ge(acc_done, f + 3)
                for n in range(NH):
                    act.wait_ge(gst_out[n], 16 * (f - G) + 16)
                    ins = act.activation(gst[n][:], banks[2 * slot + n][:, :], ACT.Sigmoid)
                    ins.then_inc(gst_ready, 1)
                act.wait_ge(gst_ready, (f - G) * NH + NH)
                act.sem_inc(taken, 1)

            act.sem_inc(taken, 2)
            for n in range(NH):
                act.sem_inc(gst_out[n], 16)
            weight_hi(0, 0, 16)
            weight_hi(1, 1, 16)
            act.wait_ge(small_in, 64)
            act.activation(pw_hi[:], pw[:], ACT.Copy).then_inc(pw_ready, 1)
            act.wait_ge(upad_clear, 1)
            for g in range(G):
                act.wait_ge(acc_done, g + 3)
                if g:
                    act.wait_ge(u_used, g)
                act.activation(upad[:, PAD:PAD + SEQ], psum[:, 2 * HALF * (g % 2):2 * HALF * (g % 2 + 1)],
                               ACT.Copy).then_inc(u_ready, 1)
                act.wait_ge(u_ready, g + 1)
                act.sem_inc(taken, 1)
                weight_hi(g + 2, g % 2, 16 * ((g + 2) // 2 + 1))

            def turn(it, more):
                for j in range(2):
                    f = it * 2 + G + j
                    gate(f, j)
                    if more:
                        weight_hi(f + 2, j, 16 * (it + G // 2 + 2))

            with act.Fori(0, TURNS - 1) as it:
                turn(it, True)
            turn(TURNS - 1, False)

        @block.gpsimd
        def _(pool):
            with pool.Fori(0, TILES // 2) as it:
                for j in range(2):
                    pool.wait_ge(w_hi_ready, it * 2 + j + 1)
                    nc.gpsimd.tensor_tensor(w_lo[j][:], w_raw[j][:], w_hi[j][:].bitcast(F32),
                                            ALU.subtract).then_inc(w_lo_ready, 1)

        @block.vector
        def _(v):
            ch = Chain(v, dve)
            ch.did(v.memset(upad[:, 0:PAD], 0.0))
            ch.did(v.memset(upad[:, PAD + SEQ:], 0.0))
            ch.link(v.memset(ones[:], 1.0))
            v.sem_inc(upad_clear, 1)
            v.sem_inc(piece_used, 2)
            v.wait_ge(pw_ready, 1)
            v.tensor_tensor(pw_lo[:], pw[:], pw_hi[:].bitcast(F32), ALU.subtract).then_inc(pw_ready, 1)
            for g, w in enumerate(POOL_WINDOWS):
                v.wait_ge(u_ready, g + 1)
                if g:
                    v.wait_ge(yb_out, 16 * g)
                src, width, step, i = upad, SEQ + 2 * PAD, 1, 0
                while step < w:
                    dst = win[i]
                    ch.link(v.tensor_tensor(dst[:, 0:width - step], src[:, 0:width - step], src[:, step:width], ALU.add))
                    src, width, step, i = dst, width - step, 2 * step, 1 - i
                other = win[i]
                v.wait_ge(inv_in, 16 * (g + 1))
                ch.link(v.tensor_tensor(other[:, 0:SEQ], src[:, PAD - w // 2:PAD - w // 2 + SEQ], inv[:], ALU.mult))
                ch.link(v.tensor_tensor(other[:, 0:SEQ], other[:, 0:SEQ], upad[:, PAD:PAD + SEQ], ALU.subtract))
                v.sem_inc(u_used, 1)
                if g:
                    v.wait_ge(pool_done, g)
                ch.link(v.tensor_copy(pl_hi[:], other[:, 0:SEQ]))
                v.tensor_tensor(pl_lo[:], other[:, 0:SEQ], pl_hi[:].bitcast(F32), ALU.subtract).then_inc(pooled, 1)
                v.wait_ge(pooled, g + 1)
                v.wait_ge(pool_done, g + 1)
                v.tensor_scalar(win[1][:, 0:SEQ], psum[:, 4 * HALF:6 * HALF], pscale[:, g:g + 1], None,
                                ALU.mult).then_inc(yb_ready, 1)

            n0 = ch.n
            with v.Fori(0, A_TURNS) as it:
                own = Chain(v, dve, it * (4 * (KC - 1)) + n0)
                for q in range(4):
                    out = acc[:].rearrange("p (a n) -> p a n", n=AC)[:, it * 4 + q, :]
                    v.wait_ge(piece_in[q % 2], it * 32 + 16 * (q // 2) + 16)
                    own.link(v.tensor_scalar(out, piece[q % 2][:, 0, :], silu_x[:, 0:1], None, ALU.mult))
                    for k in range(1, KC):
                        ins = v.scalar_tensor_tensor(out=out, in0=piece[q % 2][:, k, :], scalar=silu_x[:, k:k + 1], in1=out,
                                                     op0=ALU.mult, op1=ALU.add)
                        if k < KC - 1:
                            own.link(ins)
                    ins.then_inc(piece_used, 1)
                assert own.n == 4 * (KC - 1)
            v.wait_ge(piece_used, PIECES + 2)
            v.sem_inc(ada_ready, 1)
            v.wait_ge(rows_done, 1)
            fin = Chain(v, dve, n0 + A_TURNS * 4 * (KC - 1))
            for i in range(2):
                v.wait_ge(row_in, 32 * (i + 1))
                fin.link(v.tensor_tensor(gate_row[i][:], psum[:, (4 + 2 * i) * HALF:(6 + 2 * i) * HALF], brow[:], ALU.add))
                v.tensor_tensor(gate_row[i][:], gate_row[i][:], grow[:], ALU.mult).then_inc(row_used, 1)
            fin.link(v.tensor_tensor(m2[:], banks[0][:, 0:2 * KC], badaT[:, 3 * KC:5 * KC], ALU.add))
            fin.did(v.tensor_copy(B2[:], m2[:, 0:KC]))
            fin.link(v.scalar_tensor_tensor(out=A2[:], in0=m2[:, KC:2 * KC], scalar=1.0, in1=ngT[:, 2, :], op0=ALU.add,
                                            op1=ALU.mult))


def diff(nc, sem, banks, io, keep):
    psum, ident, neg_lam, o, ss = keep["psum"], keep["ident"], keep["neg_lam"], keep["o"], keep["o_ss"]
    TILES = 2 * TL
    LAG_TURN, LAG_AV = 2, 3
    COLS = [(0, HALF), (HALF, HALF), (2 * HALF, TOK - 2 * HALF)]
    with ExitStack() as ctx:
        sb = lambda n, s, d=F32: ctx.enter_context(nc.sbuf_tensor(n, s, d))
        q_st = [sb(f"q_st{j}", [P, 2, SEQ], F32R) for j in range(2)]
        k_st = [sb(f"k_st{j}", [P, 2, TOK], F32R) for j in range(2)]
        k_sw = [sb(f"k_sw{j}", [P, 2, TOK], F32R) for j in range(2)]
        val = [sb(f"val{j}", [P, TT, P]) for j in range(2)]
        e = [[sb(f"e{b}{s}", [P, TOK]) for s in range(2)] for b in range(2)]
        a = [sb(f"a{b}", [P, TOK]) for b in range(2)]
        at = [sb(f"at{b}", [P, TT, P]) for b in range(2)]
        junk = sb("junk_d", [P, P])
        mx = sb("mx", [P, 2])
        neg_m = sb("neg_m", [P, 2, 2])
        sums = sb("sums", [P, 2, 2])
        rec = sb("rec", [P, 4, 2])
        c1 = sb("c1", [P, 2])
        head_in = [sem(f"da_head_in{j}") for j in range(2)]
        sc_done, neg_ready, exp_done = ([sem(f"da_{n}{s}") for s in range(2)] for n in ("sc", "neg", "exp"))
        a_ready, av_done, o_ready, sq_done, dve = sem("da_a"), sem("da_av"), sem("da_o"), sem("da_sq"), sem("da_dve")
        turned, free = ([sem(f"da_{n}{b}") for b in range(2)] for n in ("turned", "free"))

        RING = ("last", "low", "high")
        KEYS = {"low": range(0, 4), "high": range(4, 8), "last": range(8, TT)}
        STEPS = TILES + LAG_AV

        USES = (3 * TILES + 2) // 2

        def slot(it, i, what):
            n = 3 * (i - LAG_TURN) + RING.index(what)
            return n % 2, it * USES + n // 2

        block = ctx.enter_context(nc.Block())

        @block.sync
        def _(sp):
            def load_head(h):
                j = h % 2
                src = io["stacks_da"][h]
                for dst, s in ((q_st[j][:], src[0:2, :, 0:SEQ]), (k_st[j][:], src[2:4])):
                    sp.dma_start(dst.bitcast(F32), s.rearrange("s p n -> p s n")).then_inc(head_in[j], 16)
                for a0, b0 in ((0, HD), (HD, 0)):
                    sp.dma_start(k_sw[j][a0:a0 + HD].bitcast(F32),
                                 src[2:4, b0:b0 + HD].rearrange("s p n -> p s n")).then_inc(head_in[j], 16)
                sp.dma_start(val[j][:], io["vals"][h].rearrange("t p n -> p t n")).then_inc(head_in[j], 16)

            load_head(0)
            load_head(1)
            for j in range(2):
                sp.wait_ge(av_done, TL * (j + 1))
                load_head(2 + j)

        @block.tensor
        def _(pe):
            def use(it, i, what):
                b, used = slot(it, i, what)
                pe.wait_ge(free[b], used + 1)
                return b, banks[6 + b]

            def scores(it, i):
                j, t = i // TL, i % TL
                if t == 0:
                    pe.wait_ge(head_in[j], 80 * it + 80)
                for s in range(2):
                    pe.wait_ge(exp_done[s], it * TILES + i + 1)
                    q = q_st[j][:, s, t * P:(t + 1) * P]
                    for c, (c0, w) in enumerate(COLS):
                        out = banks[3 * s + c][:, 0:w]
                        pe.matmul(out, q, k_st[j][:, s, c0:c0 + w], start=True, stop=False)
                        mm = pe.matmul(out, q, k_sw[j][:, s, c0:c0 + w], start=False, stop=True)
                    mm.then_inc(sc_done[s], 1)

            def turn(it, t, i, what):
                b, bank = use(it, i, what)
                for n, k in enumerate(KEYS[what]):
                    mm = pe.transpose(bank[:, n * P:(n + 1) * P], a[t % 2][:, k * P:(k + 1) * P], ident[:])
                return b, mm

            def products(t, bank):
                for k in range(TT):
                    mm = pe.matmul(bank[:, 2 * P:3 * P], at[t % 2][:, k, :], val[t // TL][:, k, :], start=(k == 0), stop=(k == TT - 1))
                return mm

            with pe.Fori(0, 2) as it:
                for i in range(STEPS):
                    t = i - LAG_TURN
                    if i < TILES:
                        scores(it, i)
                    if t >= 0:
                        if t < TILES:
                            pe.wait_ge(a_ready, it * TILES + t + 3)
                            b, mm = turn(it, t, i, "last")
                        else:
                            b, bank = use(it, i, "last")
                        if t >= 1:
                            for what in ("low", "high"):
                                bb, used = slot(it, i - 1, what)
                                pe.wait_ge(free[bb], used + 2)
                            mm = products(t - 1, banks[6 + b])
                            mm.then_inc(av_done, 1)
                            pe.wait_ge(av_done, it * TILES + t)
                            pe.sem_inc(turned[b], 1)
                        else:
                            mm.then_inc(turned[b], 1)
                    if 0 <= t < TILES:
                        for what in ("low", "high"):
                            b, mm = turn(it, t, i, what)
                            mm.then_inc(turned[b], 1)
                pe.sem_inc(turned[slot(it, STEPS - 1, "low")[0]], 1)

        @block.scalar
        def _(act):
            def exp(it, i, s):
                N = it * TILES + i
                act.wait_ge(neg_ready[s], N + 1)
                act.wait_ge(sc_done[s], N + 1)
                act.wait_ge(a_ready, N + 1)
                act.activation(e[i % 2][s][:], psum[:, 3 * s * HALF:3 * s * HALF + TOK], ACT.Exp, scale=SCALE,
                               bias=neg_m[:, i % 2, s:s + 1], accum_out=sums[:, i % 2, s:s + 1]).then_inc(exp_done[s], 1)

            def copy_out(it, i, what):
                b, used = slot(it, i, what)
                act.wait_ge(turned[b], used + 1)
                tiles, t = KEYS[what], i - LAG_TURN
                act.activation(at[t % 2][:, tiles[0]:tiles[-1] + 1, :],
                               banks[6 + b].rearrange("p (k n) -> p k n", n=P), ACT.Copy).then_inc(free[b], 1)

            def square(it, t):
                col = it * TILES + t
                act.wait_ge(o_ready, it * TILES + t + 1)
                act.wait_ge(sq_done, it * TILES + t + 1)
                act.activation(junk[:], o[:, bass.ds(col, 1), :].rearrange("p a n -> p (a n)"), ACT.Square,
                               accum_out=ss[:, bass.ds(col, 1)]).then_inc(sq_done, 1)

            act.sem_inc(sq_done, 1)
            for s in range(2):
                act.sem_inc(exp_done[s], 1)
            with act.Fori(0, 2) as it:
                for i in range(STEPS):
                    if i < TILES:
                        exp(it, i, 0)
                        exp(it, i, 1)
                    if LAG_TURN <= i < TILES + LAG_TURN:
                        copy_out(it, i, "low")
                        copy_out(it, i, "high")
                    if i >= LAG_AV:
                        square(it, i - LAG_AV)

        @block.vector
        def _(v):
            def maximum(ch, it, i, s):
                v.wait_ge(sc_done[s], it * TILES + i + 1)
                ch.link(v.tensor_reduce(mx[:, s:s + 1], psum[:, 3 * s * HALF:3 * s * HALF + TOK], AX.X, ALU.max))
                v.tensor_scalar(neg_m[:, i % 2, s:s + 1], mx[:, s:s + 1], -SCALE, None, ALU.mult).then_inc(neg_ready[s], 1)

            def reciprocals(ch, it, i):
                for s in range(2):
                    v.wait_ge(exp_done[s], it * TILES + i + 2)
                ch.link(v.reciprocal(rec[:, i % 4, :], sums[:, i % 2, :]))
                ch.link(v.tensor_scalar(c1[:, i % 2:i % 2 + 1], rec[:, i % 4, 1:2], sums[:, i % 2, 0:1], neg_lam[:, 0:1],
                                        ALU.mult, ALU.mult))

            def combine(it, t):
                if t >= 2:
                    b, used = slot(it, t - 2 + LAG_TURN, "high")
                    v.wait_ge(turned[b], used + 1)
                v.scalar_tensor_tensor(out=a[t % 2][:], in0=e[t % 2][1][:], scalar=c1[:, t % 2:t % 2 + 1],
                                       in1=e[t % 2][0][:], op0=ALU.mult, op1=ALU.add).then_inc(a_ready, 1)

            def copy_out(ch, it, i):
                b, used = slot(it, i, "last")
                t = i - LAG_TURN
                v.wait_ge(turned[b], used + 1)
                if t < TILES:
                    ch.did(v.tensor_copy(at[t % 2][:, 8:TT, :], banks[6 + b][:, 0:2 * P].rearrange("p (k n) -> p k n", n=P)))
                if t >= 1:
                    col = it * TILES + (t - 1)
                    out = o[:, bass.ds(col, 1), :].rearrange("p a n -> p (a n)")
                    v.tensor_scalar(out, banks[6 + b][:, 2 * P:3 * P], rec[:, (t - 1) % 4, 0:1], None, ALU.mult).then_inc(o_ready, 1)
                    v.wait_ge(o_ready, it * TILES + t)
                ch.settle()
                v.sem_inc(free[b], 1)

            for b in range(2):
                v.sem_inc(free[b], 1)
            v.sem_inc(a_ready, 2)
            OWN = 5 * TILES
            with v.Fori(0, 2) as it:
                ch = Chain(v, dve, it * OWN)
                for i in range(STEPS):
                    if i < TILES:
                        maximum(ch, it, i, 0)
                        maximum(ch, it, i, 1)
                    if i >= LAG_TURN:
                        copy_out(ch, it, i)
                    if 1 <= i < TILES + 1:
                        combine(it, i - 1)
                    if i < TILES:
                        reciprocals(ch, it, i)
                v.sem_inc(free[slot(it, STEPS - 1, "low")[0]], 1)
                assert ch.n == OWN


def window(nc, sem, banks, io, keep):
    psum, ident, y_hi, y_lo = keep["psum"], keep["ident"], keep["y_hi"], keep["y_lo"]
    o_da, ss, sub_g = keep["o"], keep["o_ss"], keep["sub_g"]
    UN = 2 * TL
    BAND = 3 * P
    KEYS = CTX + BAND
    GROUPS = DA_HEADS * TL // 4
    with ExitStack() as ctx:
        sb = lambda n, s, d=F32: ctx.enter_context(nc.sbuf_tensor(n, s, d))
        q_st = sb("wq_st", [P, WA_GROUP, SEQ], F32R)
        k_st, k_sw = sb("wk_st", [P, TOK], F32R), sb("wk_sw", [P, TOK], F32R)
        val = sb("wval", [P, TT, HD])
        e = [[sb(f"we{b}{s}", [P, KEYS]) for s in range(2)] for b in range(2)]
        pt = [sb(f"wpt{b}", [P, 2, KEYS // P, P]) for b in range(2)]
        o = [sb(f"wo{b}", [P, 2, HD]) for b in range(2)]
        ident_r, mask_r = sb("ident_r", [P, P], F32R), sb("mask_r", [P, BAND], F32R)
        mask = sb("mask", [P, BAND])
        sink, nsink = sb("sink", [P, WA_HEADS]), sb("nsink", [P, WA_HEADS])
        mx, neg_m, sums, es, rec = (sb("wmx", [P, 2]), sb("wneg_m", [P, 2, 2]), sb("wsums", [P, 2, 2]), sb("wes", [P, 2, 2]),
                                    sb("wrec", [P, 4, 2]))
        y_in = [sb(f"y_in{j}", [P, SEQ]) for j in range(2)]
        const_in, qk_in, v_in, y_landed = sem("wa_const_in"), sem("wa_qk_in"), sem("wa_v_in"), [sem(f"wa_y_in{j}") for j in range(2)]
        const_ready, yb_hi_ready, yb_lo_ready = sem("wa_const"), sem("wa_yb_hi"), sem("wa_yb_lo")
        ss_ready, root_ready, da_ready, da_turned, ya_hi_ready, ya_lo_ready = (
            sem(f"wa_{n}") for n in ("ss", "root", "da", "da_turned", "ya_hi", "ya_lo"))
        sc_done, neg_ready, exp_done = ([sem(f"wa_{n}{s}") for s in range(2)] for n in ("sc", "neg", "exp"))
        es_in_ready, es_ready, o_ready, yc_hi_ready, dve = (sem(f"wa_{n}") for n in ("es_in", "es", "o", "yc_hi", "dve"))
        turned, free = ([sem(f"wa_{n}{b}") for b in range(4)] for n in ("turned", "free"))

        def tiles_of(u):
            blk = u // 2
            return [0, 1] + [2 + b for b in range(max(blk - 1, 0), min(blk + 2, TL))]

        def squares(u):
            todo = [(s, k) for s in range(2) for k in range(len(tiles_of(u)))]
            return [todo[n:n + 4] for n in range(0, len(todo), 4)]

        STEPS = UN + 3
        ring = {}
        for i in range(STEPS):
            if 0 <= i - 2 < UN:
                ring["av", i - 2, 0] = len(ring)
            if 0 <= i - 1 < UN:
                for part in range(len(squares(i - 1))):
                    ring["turn", i - 1, part] = len(ring)
            if 0 <= i - 3 < UN:
                ring["out", i - 3, 0] = len(ring)
        assert len(ring) % 4 == 0
        PER_BANK = len(ring) // 4

        def slot(kv, what, u, part=0):
            n = ring[what, u, part]
            return n % 4, kv * PER_BANK + n // 4

        block = ctx.enter_context(nc.Block())

        @block.sync
        def _(sp):
            def load_qk(kv):
                k = io["stacks_wa"][2 + kv]
                for dst, a, b in ((k_st, 0, 0), (k_st, HD, HD), (k_sw, 0, HD), (k_sw, HD, 0)):
                    for d0, s0, w in ((0, SEQ, CTX), (CTX, 0, SEQ)):
                        sp.dma_start(dst[a:a + HD, d0:d0 + w].bitcast(F32), k[b:b + HD, s0:s0 + w]).then_inc(qk_in, 16)
                for n in range(WA_GROUP):
                    h = kv * WA_GROUP + n
                    src = io["stacks_wa"][h - 6 if h >= 6 else h + 4]
                    sp.dma_start(q_st[:, n, :].bitcast(F32), src[:, 0:SEQ]).then_inc(qk_in, 16)

            def load_v(kv):
                v = io["vals"][DA_HEADS].rearrange("t p (g d) -> g p t d", g=WA_KV)[kv]
                sp.dma_start(val[:, 2:TT, :], v[:, 0:TL, :]).then_inc(v_in, 16)
                sp.dma_start(val[:, 0:2, :], v[:, TL:TT, :]).then_inc(v_in, 16)

            sp.dma_start(mask[:], io["mask"]).then_inc(const_in, 16)
            sp.dma_start(sink[:], io["wa_sink"].to_broadcast([P, WA_HEADS])).then_inc(const_in, 16)
            load_qk(0)
            load_v(0)
            for n in range(BC):
                if n >= 2:
                    sp.wait_ge(yb_lo_ready, n - 1)
                sp.dma_start(y_in[n % 2][:], io["yb"][n]).then_inc(y_landed[n % 2], 16)
            for s in range(2):
                sp.wait_ge(sc_done[s], UN)
            load_qk(1)
            b, used = slot(0, "av", UN - 1)
            sp.wait_ge(turned[b], used + 1)
            load_v(1)

        QK_DMAS, V_DMAS = 16 * (8 + WA_GROUP), 16 * 2

        @block.tensor
        def _(pe):
            def use(kv, what, u, part=0):
                b, used = slot(kv, what, u, part)
                pe.wait_ge(free[b], used + 1)
                return b, banks[4 + b]

            def scores(kv, u):
                blk, pair = u // 2, u % 2
                if u == 0:
                    pe.wait_ge(qk_in, QK_DMAS * kv + QK_DMAS)
                band = tiles_of(u)[2]
                width = (len(tiles_of(u)) - 2) * P
                for s in range(2):
                    pe.wait_ge(exp_done[s], kv * UN + u + 1)
                    q = q_st[:, 2 * pair + s, blk * P:(blk + 1) * P]
                    pe.matmul(banks[2 * s][:, CTX:HALF], q, k_st[:, 0:CTX], start=True, stop=False)
                    pe.matmul(banks[2 * s][:, CTX:HALF], q, k_sw[:, 0:CTX], start=False, stop=True)
                    out, at = banks[2 * s + 1][:, 0:width], slice(band * P, band * P + width)
                    pe.matmul(out, q, k_st[:, at], start=True, stop=False)
                    pe.matmul(out, q, k_sw[:, at], start=False, stop=False)
                    m0 = (band - 2 - (blk - 1)) * P
                    mm = pe.matmul(out, ident_r[:], mask_r[:, m0:m0 + width], start=False, stop=True)
                    mm.then_inc(sc_done[s], 1)

            def turn(kv, u):
                for s in range(2):
                    pe.wait_ge(exp_done[s], kv * UN + u + 2)
                for part, todo in enumerate(squares(u)):
                    b, bank = use(kv, "turn", u, part)
                    for n, (s, k) in enumerate(todo):
                        mm = pe.transpose(bank[:, n * P:(n + 1) * P], e[u % 2][s][:, k * P:(k + 1) * P], ident[:])
                    mm.then_inc(turned[b], 1)

            def products(kv, u):
                if u == 0:
                    pe.wait_ge(v_in, V_DMAS * kv + V_DMAS)
                for part in range(len(squares(u))):
                    b, used = slot(kv, "turn", u, part)
                    pe.wait_ge(free[b], used + 2)
                b, bank = use(kv, "av", u)
                tiles = tiles_of(u)
                for s in range(2):
                    for n, k in enumerate(tiles):
                        mm = pe.matmul(bank[:, s * HD:(s + 1) * HD], pt[u % 2][:, s, n, :], val[:, k, :], start=(n == 0),
                                       stop=(n == len(tiles) - 1))
                mm.then_inc(turned[b], 1)

            def out(kv, u):
                pe.wait_ge(o_ready, kv * UN + u + 1)
                b, bank = use(kv, "out", u)
                pe.transpose(bank[:, 0:P], o[u % 2][:].rearrange("p s d -> p (s d)"), ident[:]).then_inc(turned[b], 1)

            for g in range(GROUPS):
                pe.wait_ge(da_ready, g + 1)
                if g >= 4:
                    pe.wait_ge(ya_lo_ready, g - 3)
                for n in range(4):
                    mm = pe.transpose(banks[g % 4][:, n * P:(n + 1) * P], o_da[:, 4 * g + n, :], ident[:])
                mm.then_inc(da_turned, 1)
            pe.wait_ge(const_ready, 2)
            pe.wait_ge(ya_lo_ready, GROUPS)
            with pe.Fori(0, WA_KV) as kv:
                for i in range(STEPS):
                    if i < UN:
                        scores(kv, i)
                    if 0 <= i - 2 < UN:
                        products(kv, i - 2)
                    if 0 <= i - 1 < UN:
                        turn(kv, i - 1)
                    if 0 <= i - 3 < UN:
                        out(kv, i - 3)

        @block.scalar
        def _(act):
            def exp(kv, u, s):
                N = kv * UN + u
                keys = len(tiles_of(u)) * P
                act.wait_ge(neg_ready[s], N + 1)
                act.wait_ge(sc_done[s], N + 1)
                if u >= 2:
                    b, used = slot(kv, "turn", u - 2, len(squares(u - 2)) - 1)
                    act.wait_ge(turned[b], used + 1)
                act.activation(e[u % 2][s][:, 0:keys], psum[:, 2 * s * HALF + CTX:2 * s * HALF + CTX + keys], ACT.Exp, scale=SCALE,
                               bias=neg_m[:, u % 2, s:s + 1], accum_out=sums[:, u % 2, s:s + 1]).then_inc(exp_done[s], 1)

            def sinks(kv, u):
                act.wait_ge(es_in_ready, kv * UN + u + 1)
                act.activation(es[:, u % 2, :], es[:, u % 2, :], ACT.Exp).then_inc(es_ready, 1)

            def copy_out(kv, u):
                b, used = slot(kv, "turn", u, 0)
                act.wait_ge(turned[b], used + 1)
                act.activation(pt[u % 2][:, 0, 0:4, :], banks[4 + b].rearrange("p (k n) -> p k n", n=P), ACT.Copy)\
                   .then_inc(free[b], 1)

            def output_hi(kv, u):
                b, used = slot(kv, "out", u)
                act.wait_ge(turned[b], used + 1)
                dst = y_hi[2][:, bass.ds(kv * 2 + u % 2, 1), u // 2 * P:(u // 2 + 1) * P].rearrange("p a q -> p (a q)")
                act.activation(dst, banks[4 + b][:, 0:P], ACT.Copy).then_inc(yc_hi_ready, 1)

            act.wait_ge(ss_ready, 1)
            act.activation(ss[:], ss[:], ACT.Sqrt).then_inc(root_ready, 1)
            act.wait_ge(const_in, 32)
            act.activation(mask_r[:], mask[:], ACT.Copy).then_inc(const_ready, 1)
            act.activation(ident_r[:], ident[:], ACT.Copy).then_inc(const_ready, 1)
            for s in range(2):
                act.sem_inc(exp_done[s], 1)
            for g in range(GROUPS):
                act.wait_ge(da_turned, g + 1)
                act.activation(y_hi[0][:, g // NH, g % NH * HALF:(g % NH + 1) * HALF], banks[g % 4], ACT.Copy,
                               scale=sub_g[:, 0:1]).then_inc(ya_hi_ready, 1)
            for n in range(BC):
                act.wait_ge(y_landed[n % 2], 16 * (n // 2 + 1))
                act.activation(y_hi[1][:, n, :], y_in[n % 2][:], ACT.Copy).then_inc(yb_hi_ready, 1)
            with act.Fori(0, WA_KV) as kv:
                for i in range(STEPS):
                    if i < UN:
                        exp(kv, i, 0)
                        exp(kv, i, 1)
                    if 0 <= i - 1 < UN:
                        copy_out(kv, i - 1)
                    if i < UN:
                        sinks(kv, i)
                    if 0 <= i - 3 < UN:
                        output_hi(kv, i - 3)

        @block.gpsimd
        def _(pool):
            for n in range(BC):
                pool.wait_ge(yb_hi_ready, n + 1)
                nc.gpsimd.tensor_tensor(y_lo[1][:, n, :], y_in[n % 2][:], y_hi[1][:, n, :].bitcast(F32),
                                        ALU.subtract).then_inc(yb_lo_ready, 1)

        @block.vector
        def _(v):
            def maximum(ch, kv, u, s):
                keys = len(tiles_of(u)) * P
                v.wait_ge(sc_done[s], kv * UN + u + 1)
                ch.link(v.tensor_reduce(mx[:, s:s + 1], psum[:, 2 * s * HALF + CTX:2 * s * HALF + CTX + keys], AX.X, ALU.max))
                v.tensor_scalar(neg_m[:, u % 2, s:s + 1], mx[:, s:s + 1], -SCALE,
                                nsink[:, bass.ds(kv * WA_GROUP + 2 * (u % 2) + s, 1)], ALU.mult, ALU.min)\
                 .then_inc(neg_ready[s], 1)

            def sinks(kv, u):
                for s in range(2):
                    v.wait_ge(neg_ready[s], kv * UN + u + 1)
                v.tensor_tensor(es[:, u % 2, :], neg_m[:, u % 2, :], sink[:, bass.ds(kv * WA_GROUP + 2 * (u % 2), 2)], ALU.add)\
                 .then_inc(es_in_ready, 1)

            def reciprocals(ch, kv, u):
                for s in range(2):
                    v.wait_ge(exp_done[s], kv * UN + u + 2)
                v.wait_ge(es_ready, kv * UN + u + 1)
                ch.link(v.tensor_tensor(sums[:, u % 2, :], sums[:, u % 2, :], es[:, u % 2, :], ALU.add))
                ch.link(v.reciprocal(rec[:, u % 4, :], sums[:, u % 2, :]))

            def output(kv, u):
                b, used = slot(kv, "av", u)
                v.wait_ge(turned[b], used + 1)
                v.tensor_tensor(o[u % 2][:], banks[4 + b][:, 0:P].rearrange("p (s d) -> p s d", s=2),
                                rec[:, u % 4, :].unsqueeze(2).to_broadcast([P, 2, HD]), ALU.mult).then_inc(o_ready, 1)
                v.wait_ge(o_ready, kv * UN + u + 1)
                v.sem_inc(free[b], 1)

            def copy_out(kv, u, part):
                b, used = slot(kv, "turn", u, part)
                v.wait_ge(turned[b], used + 1)
                for n0, s, k0, cnt in split_runs(squares(u)[part]):
                    ins = v.tensor_copy(pt[u % 2][:, s, k0:k0 + cnt, :],
                                        banks[4 + b][:, n0 * P:(n0 + cnt) * P].rearrange("p (k n) -> p k n", n=P))
                ins.then_inc(free[b], 1)

            def output_lo(kv, u):
                b, used = slot(kv, "out", u)
                v.wait_ge(yc_hi_ready, kv * UN + u + 1)
                at = (slice(None), bass.ds(kv * 2 + u % 2, 1), slice(u // 2 * P, (u // 2 + 1) * P))
                v.tensor_tensor(y_lo[2][at].rearrange("p a q -> p (a q)"), banks[4 + b][:, 0:P],
                                y_hi[2][at].rearrange("p a q -> p (a q)").bitcast(F32), ALU.subtract).then_inc(free[b], 1)

            def normalise(g):
                out = o_da[:, 4 * g:4 * g + 4, :]
                v.tensor_tensor(out, out, ss[:, 4 * g:4 * g + 4].unsqueeze(2).to_broadcast([P, 4, P]), ALU.mult)\
                 .then_inc(da_ready, 1)

            ch = Chain(v, dve)
            v.tensor_scalar(ss[:], ss[:], 1.0 / DA_V, EPS, ALU.mult, ALU.add).then_inc(ss_ready, 1)
            v.wait_ge(root_ready, 1)
            ch.link(v.reciprocal(ss[:], ss[:]))
            normalise(0)
            normalise(1)
            for g in range(GROUPS):
                v.wait_ge(ya_hi_ready, g + 1)
                at = (slice(None), g // NH, slice(g % NH * HALF, (g % NH + 1) * HALF))
                v.scalar_tensor_tensor(out=y_lo[0][at], in0=banks[g % 4], scalar=sub_g[:, 0:1], in1=y_hi[0][at].bitcast(F32),
                                       op0=ALU.mult, op1=ALU.subtract).then_inc(ya_lo_ready, 1)
                if g + 2 < GROUPS:
                    normalise(g + 2)
            v.wait_ge(const_in, 32)
            ch.link(v.tensor_scalar(nsink[:], sink[:], -1.0, None, ALU.mult))
            for b in range(4):
                v.sem_inc(free[b], 1)
            OWN = 4 * UN
            with v.Fori(0, WA_KV) as kv:
                ch = Chain(v, dve, kv * OWN + 2)
                for i in range(STEPS):
                    if i < UN:
                        maximum(ch, kv, i, 0)
                        maximum(ch, kv, i, 1)
                        sinks(kv, i)
                    if 0 <= i - 2 < UN:
                        output(kv, i - 2)
                    if 0 <= i - 1 < UN:
                        for part in range(1, len(squares(i - 1))):
                            copy_out(kv, i - 1, part)
                    if 0 <= i - 3 < UN:
                        output_lo(kv, i - 3)
                    if i < UN:
                        reciprocals(ch, kv, i)
                assert ch.n == OWN


def split_runs(todo):
    runs = []
    for n, (s, k) in enumerate(todo):
        if runs and runs[-1][1] == s:
            runs[-1][3] += 1
        else:
            runs.append([n, s, k, 1])
    return runs


def merge(nc, sem, banks, io, keep):
    y_hi, y_lo, m = keep["y_hi"], keep["y_lo"], keep["m"]
    psum = keep["psum"]
    WN = 3 * BC * P
    with ExitStack() as ctx:
        sb = lambda n, s, d=F32: ctx.enter_context(nc.sbuf_tensor(n, s, d))
        w_raw = [sb(f"b_raw{j}", [P, 3, BC, P]) for j in range(2)]
        w_hi = [sb(f"b_hi{j}", [P, 3, BC, P], F32R) for j in range(2)]
        w_lo = [sb(f"b_lo{j}", [P, 3, BC, P], F32R) for j in range(2)]
        g = [sb(f"b_g{j}", [P, 3, SEQ]) for j in range(2)]
        tmp = sb("b_tmp", [P, SEQ])
        w_in, g_in = [sem(f"mg_w_in{j}") for j in range(2)], [sem(f"mg_g_in{j}") for j in range(2)]
        w_hi_ready, w_lo_ready, acc_done, m_ready, taken, dve = (sem(f"mg_{n}") for n in
                                                                ("w_hi", "w_lo", "acc", "m", "taken", "dve"))
        gates = io["gates"].rearrange("i m p n -> m p i n")
        TURNS = KC // 2
        block = ctx.enter_context(nc.Block())

        @block.sync
        def _(sp):
            def load(i, j):
                sp.dma_start(w_raw[j][:], io["w_br"][i]).then_inc(w_in[j], 16)
                sp.dma_start(g[j][:], gates[i]).then_inc(g_in[j], 16)
            load(0, 0)
            load(1, 1)
            with sp.Fori(0, TURNS - 1) as it:
                for j in range(2):
                    sp.wait_ge(w_lo_ready, it * 2 + j + 1)
                    sp.wait_ge(m_ready, it * 2 + j + 1)
                    load(it * 2 + j + 2, j)

        @block.tensor
        def _(pe):
            def tile(t, j, phase):
                pe.wait_ge(w_lo_ready, t + 1)
                for i in range(3):
                    r = (3 * phase + i) % 4
                    pe.wait_ge(taken, t * 3 + i + 1)
                    for k in range(BC):
                        mm = wide_product(pe, [banks[2 * r + n] for n in range(NH)],
                                          (w_hi[j][:, i, k, :], w_lo[j][:, i, k, :]),
                                          [(y_hi[i][:, k, n * HALF:(n + 1) * HALF], y_lo[i][:, k, n * HALF:(n + 1) * HALF])
                                           for n in range(NH)], k == 0, k == BC - 1)
                    mm.then_inc(acc_done, 1)

            with pe.Fori(0, TURNS // 2) as it:
                for q in range(4):
                    tile(it * 4 + q, q % 2, q)

        @block.scalar
        def _(act):
            with act.Fori(0, TURNS) as it:
                for j in range(2):
                    act.wait_ge(w_in[j], it * 16 + 16)
                    act.wait_ge(acc_done, (it * 2 + j) * 3 + 1)
                    act.activation(w_hi[j][:], w_raw[j][:], ACT.Copy).then_inc(w_hi_ready, 1)

        @block.gpsimd
        def _(pool):
            with pool.Fori(0, TURNS) as it:
                for j in range(2):
                    pool.wait_ge(w_hi_ready, it * 2 + j + 1)
                    nc.gpsimd.tensor_tensor(w_lo[j][:], w_raw[j][:], w_hi[j][:].bitcast(F32),
                                            ALU.subtract).then_inc(w_lo_ready, 1)

        @block.vector
        def _(v):
            v.sem_inc(taken, 4)
            v.sem_inc(acc_done, 7)
            OWN = 4
            with v.Fori(0, TURNS // 2) as it:
                ch = Chain(v, dve, it * OWN)
                for q in range(4):
                    t = it * 4 + q
                    out = m[:, t, :]
                    v.wait_ge(g_in[q % 2], (it * 2 + q // 2) * 16 + 16)
                    for i in range(3):
                        r = (3 * q + i) % 4
                        v.wait_ge(acc_done, t * 3 + i + 8)
                        ins = v.tensor_tensor(out if i == 0 else tmp[:], psum[:, 2 * r * HALF:2 * (r + 1) * HALF],
                                              g[q % 2][:, i, :], ALU.mult)
                        ins.then_inc(taken, 1)
                        v.wait_ge(taken, t * 3 + i + 5)
                        if i == 1:
                            ch.link(v.tensor_tensor(out, out, tmp[:], ALU.add))
                        if i == 2:
                            v.tensor_tensor(out, out, tmp[:], ALU.add).then_inc(m_ready, 1)
                            v.wait_ge(m_ready, t + 1)
                assert ch.n == OWN


def residual(nc, sem, banks, io, keep):
    psum, ident, m, h_hi, h_lo = keep["psum"], keep["ident"], keep["m"], keep["h2_hi"], keep["h2_lo"]
    A2, B2, row = keep["A2"], keep["B2"], keep["gate_row"][0]
    with ExitStack() as ctx:
        sb = lambda n, s, d=F32: ctx.enter_context(nc.sbuf_tensor(n, s, d))
        w_raw = [sb(f"o_raw{j}", [P, D]) for j in range(2)]
        w_hi, w_lo = sb("o_hi", [P, KC, D], F32R), sb("o_lo", [P, KC, D], F32R)
        m_hi, m_lo = ([sb(f"m_{n}{j}", [P, KC, P], F32R) for j in range(2)] for n in ("hi", "lo"))
        x = [sb(f"o_x{j}", [P, D]) for j in range(2)]
        junk, xn = w_raw
        full = sb("o_full", [P, KC, P])
        ss, rs = sb("o_ss", [P, 2, 2]), sb("o_rs", [P, 2, 2])
        w_in, x_in, x_out = ([sem(f"rs_{n}{j}") for j in range(2)] for n in ("w_in", "x_in", "x_out"))
        w_hi_ready, w_lo_ready, m_hi_ready, m_lo_ready = (sem(f"rs_{n}") for n in ("w_hi", "w_lo", "m_hi", "m_lo"))
        acc_done, ss_ready, mean_ready, root_ready, taken = (sem(f"rs_{n}") for n in ("acc", "ss", "mean", "root", "taken"))
        x_ready, xn_ready, turned, full_ready, h_ready, dve = (sem(f"rs_{n}") for n in ("x", "xn", "turned", "full", "h", "dve"))
        block = ctx.enter_context(nc.Block())

        @block.sync
        def _(sp):
            for k in range(KC):
                if k >= 2:
                    sp.wait_ge(w_lo_ready, k - 1)
                sp.dma_start(w_raw[k % 2][:], io["w_out"][k * P:(k + 1) * P, :]).then_inc(w_in[k % 2], 16)
            for t in range(TL):
                if t >= 2:
                    sp.wait_ge(x_out[t % 2], 16 * (t // 2))
                    sp.wait_ge(xn_ready, t - 1)
                sp.dma_start(x[t % 2][:], io["x"][t * P:(t + 1) * P, :]).then_inc(x_in[t % 2], 16)
                if t:
                    sp.wait_ge(x_ready, t)
                    sp.dma_start(io["x_mid"][t - 1], x[(t - 1) % 2][:]).then_inc(x_out[(t - 1) % 2], 16)
            sp.wait_ge(x_ready, TL)
            sp.dma_start(io["x_mid"][TL - 1], x[(TL - 1) % 2][:]).then_inc(x_out[(TL - 1) % 2], 16)
            for j in range(2):
                sp.wait_ge(x_out[j], 16 * TL // 2)

        @block.tensor
        def _(pe):
            def turn(t):
                pe.wait_ge(xn_ready, t + 1)
                if t >= 2:
                    pe.wait_ge(full_ready, KC * (t - 1))
                for k in range(KC):
                    mm = pe.transpose(banks[4 + 2 * (t % 2) + k // 4][:, (k % 4) * P:(k % 4 + 1) * P], xn[:, k * P:(k + 1) * P],
                                      ident[:])
                mm.then_inc(turned, 1)

            for t in range(TL):
                pe.wait_ge(m_lo_ready, t + 1)
                if t >= 2:
                    pe.wait_ge(taken, t - 1)
                for k in range(KC):
                    if t == 0:
                        pe.wait_ge(w_lo_ready, k + 1)
                    for n in range(NH):
                        mm = parts_product(pe, banks[2 * (t % 2) + n], (m_hi[t % 2][:, k, :], m_lo[t % 2][:, k, :]),
                                           (w_hi[:, k, n * HALF:(n + 1) * HALF], w_lo[:, k, n * HALF:(n + 1) * HALF]),
                                           k == 0, k == KC - 1)
                mm.then_inc(acc_done, 1)
                if t:
                    turn(t - 1)
            turn(TL - 1)

        @block.scalar
        def _(act):
            def cut_m(t):
                if t >= 2:
                    act.wait_ge(acc_done, t - 1)
                act.activation(m_hi[t % 2][:], m[:, :, t * P:(t + 1) * P], ACT.Copy).then_inc(m_hi_ready, 1)

            cut_m(0)
            for k in range(KC):
                act.wait_ge(w_in[k % 2], 16 * (k // 2 + 1))
                act.activation(w_hi[:, k, :], w_raw[k % 2][:], ACT.Copy).then_inc(w_hi_ready, 1)
            cut_m(1)
            for t in range(TL):
                acc = psum[:, 2 * (t % 2) * HALF:2 * (t % 2 + 1) * HALF]
                act.wait_ge(acc_done, t + 1)
                if t:
                    act.wait_ge(ss_ready, 2 * t)
                act.activation(junk[:], acc, ACT.Square, accum_out=ss[:, t % 2, 0:1]).then_inc(ss_ready, 1)
                act.wait_ge(mean_ready, 2 * t + 1)
                act.activation(rs[:, t % 2, 0:1], ss[:, t % 2, 0:1], ACT.Sqrt).then_inc(root_ready, 1)
                act.wait_ge(x_ready, t + 1)
                act.wait_ge(ss_ready, 2 * t + 1)
                act.activation(junk[:], x[t % 2][:], ACT.Square, accum_out=ss[:, t % 2, 1:2]).then_inc(ss_ready, 1)
                act.wait_ge(mean_ready, 2 * t + 2)
                act.activation(rs[:, t % 2, 1:2], ss[:, t % 2, 1:2], ACT.Sqrt).then_inc(root_ready, 1)
                if t + 2 < TL:
                    cut_m(t + 2)
                act.wait_ge(turned, t + 1)
                if t:
                    act.wait_ge(h_ready, t)
                for k in range(KC):
                    act.activation(full[:, k, :], banks[4 + 2 * (t % 2) + k // 4][:, (k % 4) * P:(k % 4 + 1) * P],
                                   ACT.Identity, scale=A2[:, k:k + 1], bias=B2[:, k:k + 1]).then_inc(full_ready, 1)

        @block.gpsimd
        def _(pool):
            def cut_m(t):
                pool.wait_ge(m_hi_ready, t + 1)
                nc.gpsimd.tensor_tensor(m_lo[t % 2][:], m[:, :, t * P:(t + 1) * P], m_hi[t % 2][:].bitcast(F32),
                                        ALU.subtract).then_inc(m_lo_ready, 1)
            for t in range(TL):
                cut_m(t)

        @block.vector
        def _(v):
            ch = Chain(v, dve)
            for k in range(KC):
                v.wait_ge(w_hi_ready, k + 1)
                v.tensor_tensor(w_lo[:, k, :], w_raw[k % 2][:], w_hi[:, k, :].bitcast(F32), ALU.subtract).then_inc(w_lo_ready, 1)
            for t in range(TL):
                acc = psum[:, 2 * (t % 2) * HALF:2 * (t % 2 + 1) * HALF]
                root = lambda i: rs[:, t % 2, i:i + 1]
                v.wait_ge(ss_ready, 2 * t + 1)
                v.tensor_scalar(ss[:, t % 2, 0:1], ss[:, t % 2, 0:1], 1.0 / D, EPS, ALU.mult, ALU.add).then_inc(mean_ready, 1)
                v.wait_ge(root_ready, 2 * t + 1)
                ch.link(v.reciprocal(root(0), root(0)))
                if t:
                    v.wait_ge(turned, t)
                ch.link(v.scalar_tensor_tensor(out=xn[:], in0=acc, scalar=root(0), in1=row[:], op0=ALU.mult, op1=ALU.mult))
                v.sem_inc(taken, 1)
                v.wait_ge(x_in[t % 2], 16 * (t // 2 + 1))
                v.tensor_tensor(x[t % 2][:], x[t % 2][:], xn[:], ALU.add).then_inc(x_ready, 1)
                v.wait_ge(ss_ready, 2 * t + 2)
                v.tensor_scalar(ss[:, t % 2, 1:2], ss[:, t % 2, 1:2], 1.0 / D, EPS, ALU.mult, ALU.add).then_inc(mean_ready, 1)
                v.wait_ge(root_ready, 2 * t + 2)
                ch.link(v.reciprocal(root(1), root(1)))
                v.wait_ge(x_ready, t + 1)
                v.tensor_scalar(xn[:], x[t % 2][:], root(1), None, ALU.mult).then_inc(xn_ready, 1)
                v.wait_ge(full_ready, KC * (t + 1))
                at = (slice(None), slice(None), slice(t * P, (t + 1) * P))
                ch.link(v.tensor_copy(h_hi[at], full[:]))
                v.tensor_tensor(h_lo[at], full[:], h_hi[at].bitcast(F32), ALU.subtract).then_inc(h_ready, 1)


def ffn_in(nc, sem, banks, io, keep):
    psum, h_hi, h_lo, f = keep["psum"], keep["h2_hi"], keep["h2_lo"], keep["f"]
    DEPTH = 4
    TURNS = 2 * FC // DEPTH
    with ExitStack() as ctx:
        sb = lambda n, s, d=F32: ctx.enter_context(nc.sbuf_tensor(n, s, d))
        w_raw = [sb(f"i_raw{j}", [P, KC, P]) for j in range(2)]
        w_hi = [sb(f"i_hi{j}", [P, KC, P], F32R) for j in range(2)]
        w_lo = [sb(f"i_lo{j}", [P, KC, P], F32R) for j in range(2)]
        act_g = [sb(f"i_act{j}", [P, HALF]) for j in range(2)]
        w_in = [sem(f"fi_w_in{j}") for j in range(2)]
        w_hi_ready, w_lo_ready, acc_done, silu_ready, f_ready = (sem(f"fi_{n}") for n in ("w_hi", "w_lo", "acc", "silu", "f"))
        w_ff = io["w_ff"]
        block = ctx.enter_context(nc.Block())

        @block.sync
        def _(sp):
            for j in range(2):
                sp.dma_start(w_raw[j][:], w_ff[0, j]).then_inc(w_in[j], 16)
            with sp.Fori(1, FC) as m:
                for j in range(2):
                    sp.wait_ge(w_lo_ready, m * 2 + j - 1)
                    sp.dma_start(w_raw[j][:], w_ff[m, j]).then_inc(w_in[j], 16)

        @block.tensor
        def _(pe):
            with pe.Fori(0, TURNS) as it:
                for b in range(DEPTH):
                    pe.wait_ge(w_lo_ready, it * DEPTH + b + 1)
                    if b % 2 == 0:
                        pe.wait_ge(f_ready, it * DEPTH + b + 1)
                    for k in range(KC):
                        mm = wide_product(pe, [banks[2 * b + n] for n in range(NH)],
                                          (w_hi[b % 2][:, k, :], w_lo[b % 2][:, k, :]),
                                          [(h_hi[:, k, n * HALF:(n + 1) * HALF], h_lo[:, k, n * HALF:(n + 1) * HALF])
                                           for n in range(NH)], k == 0, k == KC - 1)
                    mm.then_inc(acc_done, 1)

        @block.scalar
        def _(act):
            def weight_hi(b, slot, landed):
                act.wait_ge(w_in[slot], landed)
                act.wait_ge(acc_done, b + 1)
                act.activation(w_hi[slot][:], w_raw[slot][:], ACT.Copy).then_inc(w_hi_ready, 1)

            def silu(it, b):
                act.wait_ge(acc_done, it * DEPTH + b + 3)
                for n in range(NH):
                    act.wait_ge(f_ready, it * DEPTH + b + n + 3)
                    act.activation(act_g[n][:], banks[2 * b + n], ACT.Silu).then_inc(silu_ready, 1)

            def turn(it, more):
                for b in range(DEPTH):
                    if b % 2 == 0:
                        silu(it, b)
                    if b < 2 or more:
                        weight_hi(it * DEPTH + b + 2, b % 2, (it * 2 + b // 2 + 1) * 16 + 16)

            weight_hi(0, 0, 16)
            weight_hi(1, 1, 16)
            with act.Fori(0, TURNS - 1) as it:
                turn(it, True)
            turn(TURNS - 1, False)

        @block.gpsimd
        def _(pool):
            with pool.Fori(0, FC) as m:
                for j in range(2):
                    pool.wait_ge(w_hi_ready, m * 2 + j + 1)
                    nc.gpsimd.tensor_tensor(w_lo[j][:], w_raw[j][:], w_hi[j][:].bitcast(F32),
                                            ALU.subtract).then_inc(w_lo_ready, 1)

        @block.vector
        def _(v):
            v.sem_inc(f_ready, 4)
            v.sem_inc(acc_done, 2)
            with v.Fori(0, TURNS) as it:
                for b in range(1, DEPTH, 2):
                    v.wait_ge(acc_done, it * DEPTH + b + 3)
                    for n in range(NH):
                        v.wait_ge(silu_ready, it * DEPTH + b + n)
                        v.tensor_tensor(f[:, it * 2 + b // 2, n * HALF:(n + 1) * HALF], banks[2 * b + n], act_g[n][:],
                                        ALU.mult).then_inc(f_ready, 1)


def ffn_out(nc, sem, banks, io, keep):
    psum, f, row = keep["psum"], keep["f"], keep["gate_row"][1]
    T = 4
    with ExitStack() as ctx:
        sb = lambda n, s, d=F32: ctx.enter_context(nc.sbuf_tensor(n, s, d))
        w_raw = [sb(f"u_raw{j}", [P, D]) for j in range(2)]
        w_hi, w_lo = ([sb(f"u_{n}{j}", [P, D], F32R) for j in range(2)] for n in ("hi", "lo"))
        f_hi, f_lo = ([sb(f"uf_{n}{j}", [P, HALF], F32R) for j in range(2)] for n in ("hi", "lo"))
        y = [sb(f"u_y{t}", [P, D]) for t in range(T)]
        x = [sb(f"u_x{t}", [P, D]) for t in range(T)]
        junk = sb("u_junk", [P, D])
        ss = sb("u_ss", [P, T])
        w_in, x_in = [sem(f"fo_w_in{j}") for j in range(2)], sem("fo_x_in")
        w_hi_ready, w_lo_ready, f_hi_ready, f_lo_ready, acc_k, acc_done = (
            sem(f"fo_{n}") for n in ("w_hi", "w_lo", "f_hi", "f_lo", "acc_k", "acc"))
        y_copied, ss_ready, mean_ready, root_ready, out_ready, stored, dve = (
            sem(f"fo_{n}") for n in ("y", "ss", "mean", "root", "out", "stored", "dve"))
        STEPS = NH * FC
        block = ctx.enter_context(nc.Block())

        @block.sync
        def _(sp):
            w_out = io["w_ffn_out"].rearrange("(k p) n -> k p n", p=P)

            def load_x(c):
                for t in range(T):
                    sp.dma_start(x[t][:], io["x_mid"][c * T + t]).then_inc(x_in, 16)

            load_x(0)
            for j in range(2):
                sp.dma_start(w_raw[j][:], w_out[j]).then_inc(w_in[j], 16)
            for c in range(NH):
                with sp.Fori(0, FC // 2 - 1) as it:
                    for j in range(2):
                        sp.wait_ge(w_lo_ready, it * 2 + (j + c * FC + 1))
                        sp.dma_start(w_raw[j][:], w_out[it * 2 + j + 2]).then_inc(w_in[j], 16)
                if c + 1 < NH:
                    for j in range(2):
                        sp.wait_ge(w_lo_ready, c * FC + FC - 1 + j)
                        sp.dma_start(w_raw[j][:], w_out[j]).then_inc(w_in[j], 16)
                for t in range(T):
                    sp.wait_ge(out_ready, c * T + t + 1)
                    sp.dma_start(io["out"][(c * T + t) * P:(c * T + t + 1) * P, :], y[t][:]).then_inc(stored, 16)
                if c + 1 < NH:
                    load_x(c + 1)
            sp.wait_ge(stored, 16 * NH * T)

        @block.tensor
        def _(pe):
            def chunk(step, j, first, last):
                pe.wait_ge(w_lo_ready, step + 1)
                pe.wait_ge(f_lo_ready, step + 1)
                for t in range(T):
                    for n in range(NH):
                        mm = parts_product(pe, banks[2 * t + n],
                                           (f_hi[j][:, t * P:(t + 1) * P], f_lo[j][:, t * P:(t + 1) * P]),
                                           (w_hi[j][:, n * HALF:(n + 1) * HALF], w_lo[j][:, n * HALF:(n + 1) * HALF]),
                                           first, last)
                    if last:
                        mm.then_inc(acc_done, 1)
                if not last:
                    mm.then_inc(acc_k, 1)

            for c in range(NH):
                if c:
                    pe.wait_ge(y_copied, c * T)
                for j in range(2):
                    chunk(c * FC + j, j, j == 0, False)
                with pe.Fori(1, FC // 2 - 1) as it:
                    for j in range(2):
                        chunk(it * 2 + (c * FC + j), j, False, False)
                for j in range(2):
                    chunk(c * FC + FC - 2 + j, j, False, j == 1)

        @block.scalar
        def _(act):
            def cut(step, c, k, j, landed):
                act.wait_ge(w_in[j], landed)
                if c and isinstance(k, int) and k < 2:
                    act.wait_ge(acc_done, c * T)
                act.wait_ge(acc_k, k + (c * (FC - 1) + 1))
                act.activation(w_hi[j][:], w_raw[j][:], ACT.Copy).then_inc(w_hi_ready, 1)
                act.activation(f_hi[j][:], f[:, k, c * HALF:(c + 1) * HALF], ACT.Copy).then_inc(f_hi_ready, 1)

            def copy_out(c):
                for t in range(T):
                    act.wait_ge(acc_done, c * T + t + 1)
                    if c:
                        act.wait_ge(stored, 16 * T * c)
                    act.activation(y[t][:], psum[:, 2 * t * HALF:2 * (t + 1) * HALF], ACT.Copy).then_inc(y_copied, 1)

            def norms(c):
                for t in range(T):
                    n = c * T + t
                    act.wait_ge(y_copied, n + 1)
                    if n:
                        act.wait_ge(ss_ready, n)
                    act.activation(junk[:], y[t][:], ACT.Square, accum_out=ss[:, t:t + 1]).then_inc(ss_ready, 1)
                act.wait_ge(mean_ready, c + 1)
                act.activation(ss[:], ss[:], ACT.Sqrt).then_inc(root_ready, 1)

            act.sem_inc(acc_k, 2)
            for c in range(NH):
                for k in range(2):
                    if c == 0:
                        cut(k, 0, k, k, 16)
                with act.Fori(1, FC // 2) as it:
                    for j in range(2):
                        cut(it * 2 + (c * FC + j), c, it * 2 + j, j, it * 16 + (16 * (c * FC // 2) + 16))
                copy_out(c)
                if c + 1 < NH:
                    for k in range(2):
                        cut((c + 1) * FC + k, c + 1, k, k, 16 * ((c + 1) * FC // 2) + 16)
                norms(c)

        @block.gpsimd
        def _(pool):
            for c in range(NH):
                with pool.Fori(0, FC // 2) as it:
                    for j in range(2):
                        pool.wait_ge(f_hi_ready, it * 2 + (c * FC + j + 1))
                        nc.gpsimd.tensor_tensor(f_lo[j][:], f[:, it * 2 + j, c * HALF:(c + 1) * HALF], f_hi[j][:].bitcast(F32),
                                                ALU.subtract).then_inc(f_lo_ready, 1)

        @block.vector
        def _(v):
            def weight_lo(step, j):
                v.wait_ge(w_hi_ready, step + 1)
                v.tensor_tensor(w_lo[j][:], w_raw[j][:], w_hi[j][:].bitcast(F32), ALU.subtract).then_inc(w_lo_ready, 1)

            ch = Chain(v, dve)
            for k in range(2):
                weight_lo(k, k)
            for c in range(NH):
                with v.Fori(1, FC // 2) as it:
                    for j in range(2):
                        weight_lo(it * 2 + (c * FC + j), j)
                if c + 1 < NH:
                    for k in range(2):
                        weight_lo((c + 1) * FC + k, k)
                v.wait_ge(ss_ready, T * (c + 1))
                v.tensor_scalar(ss[:], ss[:], 1.0 / D, EPS, ALU.mult, ALU.add).then_inc(mean_ready, 1)
                v.wait_ge(root_ready, c + 1)
                ch.link(v.reciprocal(ss[:], ss[:]))
                v.wait_ge(x_in, 16 * T * (c + 1))
                for t in range(T):
                    ch.link(v.scalar_tensor_tensor(out=y[t][:], in0=y[t][:], scalar=ss[:, t:t + 1], in1=row[:], op0=ALU.mult,
                                                   op1=ALU.mult))
                    v.tensor_tensor(y[t][:], y[t][:], x[t][:], ALU.add).then_inc(out_ready, 1)


def tables():
    f = np.float32
    rows = SEQ // GRID_W
    row = np.repeat(np.arange(rows, dtype=f), GRID_W)
    col = np.tile(np.arange(GRID_W, dtype=f), rows)
    n_freq = HD // 4
    inv = (f(ROPE_THETA) ** (-np.arange(n_freq, dtype=f) / f(n_freq))).astype(f)
    ang = np.concatenate([row[:, None] * inv, col[:, None] * inv], axis=-1).astype(f)
    cos, sin = np.cos(ang).astype(f), np.sin(ang).astype(f)
    cos2 = np.repeat(cos, 2, axis=1)
    sin2 = np.stack([-sin, sin], axis=-1).reshape(SEQ, HD)
    turn = lambda a: np.ascontiguousarray(a.reshape(TL, P, HD).transpose(1, 0, 2))
    q, j = np.arange(P)[:, None], np.arange(P)[None, :]
    mask = np.zeros((P, 3, P), f)
    mask[:, 0, :] = np.where(j >= q, 0.0, MASKED)
    mask[:, 2, :] = np.where(j <= q, 0.0, MASKED)
    t = np.arange(SEQ)
    inv_count = np.stack([1.0 / (np.clip(t + w - w // 2, 0, SEQ) - np.clip(t - w // 2, 0, SEQ)) for w in POOL_WINDOWS])
    return {"cosT": turn(cos2), "sinT": turn(sin2), "ident": np.eye(P, dtype=f), "mask": mask.reshape(P, 3 * P),
            "inv_count": inv_count.astype(f)}


def lay_out(x, c, ctx, c_ctx, w_ada, b_ada, norm_g, w_in, da_lambda, da_subln_g, pool_w, pool_scale, wa_sink,
            w_branch, w_out, w_ffn_in, w_ffn_out):
    a = lambda v: np.ascontiguousarray(v)
    w = np.asarray(w_in)[0]
    q0, k0, v0, u0 = 0, 512, 1024, 1536
    qw0, kw0, vw0, g0 = 2048, 2560, 2688, 2816
    groups = [[(q0 + h * P, P), (k0 + h * P, P), (v0 + h * P, P)] for h in range(DA_HEADS)]
    groups += [[(qw0 + 6 * HD, P), (kw0, P), (vw0, P)], [(qw0, GW)]]
    chunks = lambda m: m.reshape(m.shape[0] // P, P, -1).transpose(1, 0, 2)
    w_tok = a(np.stack([chunks(np.concatenate([w[:, s:s + n] for s, n in g], axis=1)) for g in groups]))
    feat = np.concatenate([w[:, u0:u0 + BW], w[:, g0:]], axis=1)
    w_feat = a(feat.reshape(KC, P, -1, P).transpose(2, 1, 0, 3))
    w_br = a(np.asarray(w_branch)[0].reshape(3, BC, P, KC, P).transpose(3, 2, 0, 1, 4))
    w_ff = a(np.asarray(w_ffn_in)[0].reshape(KC, P, 2, FC, P).transpose(3, 2, 1, 0, 4))
    cT = a(np.stack([np.asarray(c)[0], np.asarray(c_ctx)]).reshape(2, KC, P).transpose(2, 0, 1))
    return {
        "x": a(np.asarray(x)[0]), "ctx": a(np.asarray(ctx)[0]), "cT": cT,
        "w_ada": a(np.asarray(w_ada)[0]), "b_adaT": a(np.asarray(b_ada)[0].reshape(6 * KC, P).T), "b_ada": a(b_ada),
        "norm_gT": a(np.asarray(norm_g)[0].reshape(4, KC, P).transpose(2, 0, 1)), "norm_g": a(np.asarray(norm_g)[0]),
        "w_tok": w_tok, "w_feat": w_feat, "da_lambda": a(np.asarray(da_lambda)[0].reshape(1, -1)),
        "sub_g": a(np.asarray(da_subln_g)[0].reshape(P, 1)), "pool_w": a(np.asarray(pool_w)[0].transpose(1, 0, 2)),
        "pool_scaleT": a(np.asarray(pool_scale)[0].reshape(BC, P).T), "wa_sink": a(np.asarray(wa_sink)),
        "w_br": w_br, "w_out": a(np.asarray(w_out)[0]), "w_ff": w_ff, "w_ffn_out": a(np.asarray(w_ffn_out)[0]),
    }


SCRATCH = {"stacks_da": [DA_HEADS, 4, P, TOK], "stacks_wa": [10, P, TOK], "vals": [DA_HEADS + 1, TT, P, P],
           "gates": [3, KC, P, SEQ], "yb": [BC, P, SEQ], "x_mid": [TL, P, D]}


def program(nc, io, upto=99):
    with ExitStack() as ctx:
        taken = []

        def sem(name):
            taken.append(nc.alloc_semaphore(name=name))
            return taken[-1]

        tensor = lambda stack, n, s, d=F32, side="left": stack.enter_context(nc.sbuf_tensor(n, s, d, side=side))
        psum = ctx.enter_context(nc.psum_tensor("psum", [P, 8 * HALF], F32))
        banks = [psum[:, i * HALF:(i + 1) * HALF] for i in range(8)]
        keep = {"psum": psum, "silu_x": tensor(ctx, "silu_x", [P, KC]), "ident": tensor(ctx, "ident", [P, P]),
                "neg_lam": tensor(ctx, "neg_lam", [P, 1]), "sub_g": tensor(ctx, "sub_g_sb", [P, 1]),
                "gate_row": [tensor(ctx, f"gate_row{i}", [P, D]) for i in range(2)],
                "A2": tensor(ctx, "A2", [P, KC]), "B2": tensor(ctx, "B2", [P, KC])}
        with ExitStack() as first:
            keep["h_hi"] = tensor(first, "h_hi", [P, KC, TOK], F32R)
            keep["h_lo"] = tensor(first, "h_lo", [P, KC, TOK], F32R)
            prepare(nc, sem, banks, io, keep)
            if upto >= 2:
                project(nc, sem, banks, io, keep)
            if upto >= 3:
                features(nc, sem, banks, io, keep)
        if upto < 4:
            return
        o_stack = ctx.enter_context(ExitStack())
        keep["o"] = tensor(o_stack, "o", [P, DA_HEADS * TL, P], F32, "right")
        keep["o_ss"] = tensor(o_stack, "o_squares", [P, DA_HEADS * TL], F32, "right")
        diff(nc, sem, banks, io, keep)
        if upto < 5:
            return
        nc.clear_and_free_semaphores(taken)
        nc.all_engine_barrier()
        with ExitStack() as ys, ExitStack() as ms:
            for part in ("hi", "lo"):
                keep[f"y_{part}"] = [tensor(ys, f"y_{part}{i}", [P, BC, SEQ], F32R) for i in range(3)]
            window(nc, sem, banks, io, keep)
            o_stack.close()
            keep["m"] = tensor(ms, "m", [P, KC, SEQ], F32, "right")
            if upto >= 6:
                merge(nc, sem, banks, io, keep)
            ys.close()
            with ExitStack() as h2:
                keep["h2_hi"] = tensor(h2, "h2_hi", [P, KC, SEQ], F32R)
                keep["h2_lo"] = tensor(h2, "h2_lo", [P, KC, SEQ], F32R)
                if upto >= 7:
                    residual(nc, sem, banks, io, keep)
                ms.close()
                keep["f"] = tensor(ctx, "f", [P, FC, SEQ], F32, "right")
                if upto >= 8:
                    ffn_in(nc, sem, banks, io, keep)
        if upto >= 9:
            ffn_out(nc, sem, banks, io, keep)


def kernel(**inputs):
    import concourse.bacc as bacc
    from concourse.bass_utils import run_bass_kernel_spmd

    laid = lay_out(**inputs)
    laid.update(tables())
    nc = bacc.Bacc("TRN2", target_bir_lowering=False, num_devices=1)
    io = {k: nc.dram_tensor(f"in_{k}", a.shape, mybir.dt.from_np(a.dtype), kind="ExternalInput").ap()
          for k, a in laid.items()}
    for k, shape in SCRATCH.items():
        io[k] = nc.dram_tensor(f"{k}_dram", shape, F32, kind="Internal").ap()
    io["out"] = nc.dram_tensor("out", [SEQ, D], F32, kind="ExternalOutput").ap()
    program(nc, io)
    result = run_bass_kernel_spmd(nc, [{f"in_{k}": a for k, a in laid.items()}], core_ids=[0])
    return result.results[0]["out"].reshape(1, SEQ, D)
```

```python
import math
from contextlib import ExitStack

import numpy as np

import concourse.bass as bass
from concourse import mybir

F32 = mybir.dt.float32
F32R = mybir.dt.float32r
BF16 = mybir.dt.bfloat16
ALU = mybir.AluOpType
ACT = mybir.ActivationFunctionType
AX = mybir.AxisListType

P = 128
D = 1024
SEQ = 1024
CTX = 256
TOK = SEQ + CTX
KC = D // P
TL = SEQ // P
TT = TOK // P
HALF = 512
NH = SEQ // HALF
GRID_W = 64
EPS = 1e-6
ROPE_THETA = 10000.0
HD = 64
DA_HEADS = 4
DA_V = 128
WA_HEADS = 8
WA_KV = 2
WA_GROUP = WA_HEADS // WA_KV
BW = 512
BC = BW // P
POOL_WINDOWS = (2, 4, 8, 16)
D_FF = ((8 * D + 3 * 256 - 1) // (3 * 256)) * 256
FC = D_FF // P
LAM_INIT = 0.8 - 0.6 * math.exp(-0.3 * 0)
SCALE = HD ** -0.5
MASKED = -1e30
GW = 3 * P
UNITS = 6


def parts_product(pe, out, stat, mov, first, last):
    (sh, sl), (mh, ml) = stat, mov
    pe.matmul(out, sh, mh, start=first, stop=False)
    pe.matmul(out, sh, ml, start=False, stop=False)
    return pe.matmul(out, sl, mh, start=False, stop=last)


class Chain:

    def __init__(self, eng, sem, base=0):
        self.eng, self.sem, self.base, self.n = eng, sem, base, 0

    def did(self, ins):
        ins.then_inc(self.sem, 1)
        self.n += 1

    def settle(self):
        self.eng.wait_ge(self.sem, self.base + self.n)

    def link(self, ins):
        self.did(ins)
        self.settle()


def prepare(nc, sem, banks, io, keep):
    h_hi, h_lo, ident, neg_lam, sub_g = keep["h_hi"], keep["h_lo"], keep["ident"], keep["neg_lam"], keep["sub_g"]
    AW = 256
    ADA, BUFS = 2 * D // AW, 4
    UN = [(c, k) for c in range(3) for k in range(KC)]
    with ExitStack() as ctx:
        sb = lambda n, s, d=F32: ctx.enter_context(nc.sbuf_tensor(n, s, d))
        xt = sb("xt", [P, TT, D])
        ada = [sb(f"ada{j}", [P, KC, AW]) for j in range(BUFS)]
        junk = sb("junk", [P, D])
        full = sb("full", [P, 4, HALF])
        row = sb("ada_row", [2, 2 * D])
        ROW_BANKS = 2 * D // HALF
        rows = keep["psum"][0:2, 4 * HALF:8 * HALF]
        cond = sb("cond", [P, 2, KC])
        econd = sb("econd", [P, 2, KC])
        silu = sb("silu", [P, KC, 2])
        ada_b = sb("ada_b", [P, 48])
        norm_g = sb("norm_g", [P, 4, KC])
        mod = sb("mod", [P, 2 * KC, 2])
        A = sb("A", [P, KC, 2])
        lamv = sb("lamv", [P, 4, HD])
        lamp = sb("lamp", [P, 2, HD])
        lamd = sb("lamd", [P, 4])
        ss = sb("ss", [P, TT])
        rs = sb("rs", [P, TT])
        small_in, x_in = sem("pr_small_in"), [sem(f"pr_x_in{j}") for j in range(3)]
        ada_in = [sem(f"pr_ada_in{j}") for j in range(BUFS)]
        e_ready, silu_ready, ada_used, ab_ready = sem("pr_e"), sem("pr_silu"), sem("pr_ada_used"), sem("pr_ab")
        row_ready, ada_turned = sem("pr_row"), sem("pr_ada_turned")
        sq_done, mean_ready, rs_ready, xn_ready = sem("pr_sq"), sem("pr_mean"), sem("pr_rs"), sem("pr_xn")
        turned, full_ready, hi_ready, dve = sem("pr_turned"), sem("pr_full"), sem("pr_hi"), sem("pr_dve")
        lo_ready = [sem(f"pr_lo{j}") for j in range(2)]
        lam_dots, lam_exp = sem("pr_lam_dots"), sem("pr_lam_exp")
        CH = [range(0, 4), range(4, 8), range(8, 10)]

        block = ctx.enter_context(nc.Block())

        @block.sync
        def _(sp):
            for dst, src in ((cond, io["cT"]), (ada_b, io["b_adaT"]), (norm_g, io["norm_gT"]), (ident, io["ident"]),
                             (sub_g, io["sub_g"])):
                sp.dma_start(dst[:], src).then_inc(small_in, 16)
            sp.dma_start(lamv[:].rearrange("p a b -> p (a b)"),
                         io["da_lambda"].to_broadcast([P, 4 * HD])).then_inc(small_in, 16)
            xv = io["x"].rearrange("(t p) d -> p t d", p=P)
            cv = io["ctx"].rearrange("(t p) d -> p t d", p=P)
            av = io["w_ada"].rearrange("(k p) n -> p k n", p=P)
            sp.dma_start(xt[:, 0:4, :], xv[:, 0:4, :]).then_inc(x_in[0], 16)
            for j in range(ADA):
                if j >= BUFS:
                    sp.wait_ge(ada_used, j - BUFS + 1)
                sp.dma_start(ada[j % BUFS][:], av[:, :, j * AW:(j + 1) * AW]).then_inc(ada_in[j % BUFS], 16)
                if j == ADA - 3:
                    sp.dma_start(xt[:, 4:8, :], xv[:, 4:8, :]).then_inc(x_in[1], 16)
            sp.dma_start(xt[:, 8:10, :], cv).then_inc(x_in[2], 16)
            for j in range(2):
                sp.dma_start(keep["w_raw"][j][:], io["w_tok"][j]).then_inc(keep["w_in"][j], 16)

        @block.tensor
        def _(pe):
            pe.wait_ge(silu_ready, 1)
            for j in range(ADA):
                pe.wait_ge(ada_in[j % BUFS], 16 * (j // BUFS + 1))
                for k in range(KC):
                    mm = pe.matmul(rows[:, j * AW:(j + 1) * AW], silu[:, k, :], ada[j % BUFS][:, k, :], start=(k == 0),
                                   stop=(k == KC - 1))
                mm.then_inc(ada_used, 1)
            pe.wait_ge(row_ready, ROW_BANKS)
            for n in range(2 * KC):
                mm = pe.transpose(banks[4][:, 2 * n:2 * n + 2], row[:, n * P:(n + 1) * P], ident[0:2, 0:2])
            mm.then_inc(ada_turned, 1)
            for u, (c, k) in enumerate(UN):
                pe.wait_ge(xn_ready, [4, 8, 10][c])
                if u >= 4:
                    pe.wait_ge(full_ready, u - 3)
                for j, t in enumerate(CH[c]):
                    mm = pe.transpose(banks[u % 4][:, j * P:(j + 1) * P], xt[:, t, k * P:(k + 1) * P], ident[:])
                mm.then_inc(turned, 1)

        @block.scalar
        def _(act):
            act.wait_ge(small_in, 96)
            act.activation(econd[:], cond[:], ACT.Exp, scale=-1.0).then_inc(e_ready, 1)
            act.wait_ge(lam_dots, 1)
            act.activation(lamd[:, 2:4], lamd[:, 0:2], ACT.Exp).then_inc(lam_exp, 1)
            for t in range(TT):
                if t in (0, 4, 8):
                    act.wait_ge(x_in[t // 4], 16)
                if t:
                    act.wait_ge(sq_done, t)
                act.activation(junk[:], xt[:, t, :], ACT.Square, accum_out=ss[:, t:t + 1]).then_inc(sq_done, 1)
                if t == CH[t // 4][-1]:
                    act.wait_ge(mean_ready, t // 4 + 1)
                    act.activation(rs[:, t // 4 * 4:t + 1], ss[:, t // 4 * 4:t + 1], ACT.Sqrt).then_inc(rs_ready, 1)
            act.wait_ge(ab_ready, 2)
            for u, (c, k) in enumerate(UN):
                w = len(CH[c]) * P
                act.wait_ge(turned, u + 1)
                if u >= 4:
                    act.wait_ge(lo_ready[u % 2], u // 2 - 1)
                i = 1 if c == 2 else 0
                act.activation(full[:, u % 4, 0:w], banks[u % 4][:, 0:w], ACT.Identity, scale=A[:, k, i:i + 1],
                               bias=mod[:, k, i:i + 1]).then_inc(full_ready, 1)

        def low_part(eng, u, c, k):
            w, t0 = len(CH[c]) * P, CH[c][0] * P
            eng.wait_ge(hi_ready, u + 1)
            eng.tensor_tensor(h_lo[:, k, t0:t0 + w], full[:, u % 4, 0:w], h_hi[:, k, t0:t0 + w].bitcast(F32),
                              ALU.subtract).then_inc(lo_ready[u % 2], 1)

        @block.gpsimd
        def _(pool):
            for u, (c, k) in enumerate(UN):
                if u % 2:
                    low_part(pool, u, c, k)

        @block.vector
        def _(v):
            ch = Chain(v, dve)
            v.wait_ge(small_in, 96)
            v.wait_ge(e_ready, 1)
            ch.link(v.tensor_scalar(econd[:], econd[:], 1.0, None, ALU.add))
            ch.link(v.reciprocal(econd[:], econd[:]))
            v.tensor_tensor(silu[:].rearrange("p k c -> p c k"), cond[:], econd[:], ALU.mult).then_inc(silu_ready, 1)
            ch.link(v.tensor_tensor(keep["silu_x"][:], cond[:, 0, :], econd[:, 0, :], ALU.mult))
            for i in range(2):
                ins = v.tensor_tensor_reduce(out=lamp[:, i, :], in0=lamv[:, 2 * i, :], in1=lamv[:, 2 * i + 1, :],
                                             scale=1.0, scalar=0.0, op0=ALU.mult, op1=ALU.add,
                                             accum_out=lamd[:, i:i + 1])
            ins.then_inc(lam_dots, 1)
            v.wait_ge(lam_exp, 1)
            ch.did(v.scalar_tensor_tensor(out=neg_lam[:], in0=lamd[:, 3:4], scalar=-LAM_INIT, in1=lamd[:, 2:3],
                                          op0=ALU.add, op1=ALU.subtract))
            ch.link(v.tensor_scalar(sub_g[:], sub_g[:], 1.0 - LAM_INIT, None, ALU.mult))
            for c in range(3):
                a, b = CH[c][0], CH[c][-1] + 1
                v.wait_ge(sq_done, b)
                v.tensor_scalar(ss[:, a:b], ss[:, a:b], 1.0 / D, EPS, ALU.mult, ALU.add).then_inc(mean_ready, 1)
                v.wait_ge(rs_ready, c + 1)
                ch.link(v.reciprocal(rs[:, a:b], rs[:, a:b]))
                if c == 2:
                    for j in range(ROW_BANKS):
                        v.wait_ge(ada_used, (j + 1) * HALF // AW)
                        v.tensor_copy(row[:, j * HALF:(j + 1) * HALF], banks[4 + j][0:2, :]).then_inc(row_ready, 1)
                for t in CH[c]:
                    v.tensor_scalar(xt[:, t, :], xt[:, t, :], rs[:, t:t + 1], None, ALU.mult).then_inc(xn_ready, 1)
            v.wait_ge(ada_turned, 1)
            for i in range(2):
                ch.did(v.tensor_tensor(mod[:, :, i], banks[4][:, i:4 * KC:2], ada_b[:, 0:2 * KC], ALU.add))
            ch.settle()
            for i in range(2):
                v.scalar_tensor_tensor(out=A[:, :, i], in0=mod[:, KC:2 * KC, i], scalar=1.0, in1=norm_g[:, 0, :],
                                       op0=ALU.add, op1=ALU.mult).then_inc(ab_ready, 1)
            for u, (c, k) in enumerate(UN):
                w, t0 = len(CH[c]) * P, CH[c][0] * P
                v.wait_ge(full_ready, u + 1)
                v.tensor_copy(h_hi[:, k, t0:t0 + w], full[:, u % 4, 0:w]).then_inc(hi_ready, 1)
                if u % 2 == 0:
                    low_part(v, u, c, k)


def project(nc, sem, banks, io, keep):
    h_hi, h_lo, ident = keep["h_hi"], keep["h_lo"], keep["ident"]
    with ExitStack() as ctx:
        sb = lambda n, s, d=F32: ctx.enter_context(nc.sbuf_tensor(n, s, d))
        w_raw, w_in = keep["w_raw"], keep["w_in"]
        w_hi = [sb(f"w_hi{j}", [P, KC, GW], F32R) for j in range(2)]
        w_lo = [sb(f"w_lo{j}", [P, KC, GW], F32R) for j in range(2)]
        cosT, sinT = sb("cosT", [P, TL, HD]), sb("sinT", [P, TL, HD])
        raw = [sb(f"raw{j}", [P, GW]) for j in range(2)]
        rot = sb("rot", [P, UNITS, HD])
        swp = sb("swp", [P, UNITS, HD])
        cut = [sb(f"cut{j}", [P, UNITS, 2, HD], F32R) for j in range(2)]
        st = keep["st"]
        table_in = sem("pj_table_in")
        w_hi_ready, w_lo_ready = sem("pj_w_hi"), sem("pj_w_lo")
        acc_done, raw_ready, cut_ready = sem("pj_acc"), sem("pj_raw"), sem("pj_cut")
        turned, st_ready, dve = sem("pj_turned"), sem("pj_st"), sem("pj_dve")
        st_out, v_out = keep["st_out"], [sem(f"pj_v_out{j}") for j in range(2)]
        f_hi_ready = sem("pj_f_hi")

        def content(kind, t):
            if kind == "q":
                return 0, 6, False
            return (0, 4, True) if t < TL else (P, 2, True)

        def tiles(kind):
            return TL if kind == "q" else TT

        LOOP_KINDS, LAST_KINDS = ("kv", "kv"), ("kv", "q")
        LAST = 2

        def item(it, j, t):
            return (it * 2 + j) * TT + t

        def uses(it, j, t):
            return (it * 2 + j) * (TT // 2) + t // 2

        keep["st_stored"] = 16 * (uses(LAST, 1, TL) + 1)
        CR = 2
        block = ctx.enter_context(nc.Block())

        @block.sync
        def _(sp):
            sp.dma_start(cosT[:], io["cosT"]).then_inc(table_in, 16)
            sp.dma_start(sinT[:], io["sinT"]).then_inc(table_in, 16)

            def turn(it, kinds, stacks, more):
                for j, kind in enumerate(kinds):
                    if more:
                        sp.wait_ge(w_lo_ready, (it * 2 + j + 1) * KC)
                        sp.dma_start(w_raw[j][:], io["w_tok"][it * 2 + j + 2]).then_inc(w_in[j], 16)
                    for t in range(tiles(kind)):
                        col, units, has_v = content(kind, t)
                        skip = 4 - units if kind == "kv" else 0
                        if has_v:
                            sp.wait_ge(raw_ready, item(it, j, t) + 1 + 4)
                            sp.dma_start(io["vals"][it * 2 + j, t], raw[t % 2][:, 2 * P:GW]).then_inc(v_out[t % 2], 16)
                        sp.wait_ge(st_ready, item(it, j, t) + 1 + CR)
                        sp.dma_start(stacks(j)[skip:skip + units, :, t * P:(t + 1) * P].rearrange("u p n -> p u n"),
                                     st[t % 2][:, 0:units, :].bitcast(F32)).then_inc(st_out[t % 2], 16)

            with sp.Fori(0, LAST) as it:
                turn(it, LOOP_KINDS, lambda j: io["stacks_da"][it * 2 + j], True)
            for j in range(2):
                sp.dma_start(keep["f_raw"][j][:], io["w_feat"][j]).then_inc(keep["f_in"][j], 16)
            turn(LAST, LAST_KINDS, lambda j: io["stacks_wa"][4 * j:4 * j + 4 + 2 * j], False)
            for s in range(2):
                sp.wait_ge(v_out[s], 16 * (uses(LAST, 1, 0) + 1))

        @block.tensor
        def _(pe):
            def accumulate(it, j, t, kind):
                col, units, has_v = content(kind, t)
                bank = banks[(2 * j + t) % 4]
                pe.wait_ge(raw_ready, item(it, j, t) + 1)
                for k in range(KC):
                    if t == 0:
                        pe.wait_ge(w_lo_ready, it * 2 * KC + (j * KC + k + 1))
                    mm = parts_product(pe, bank[:, col:GW], (h_hi[:, k, t * P:(t + 1) * P], h_lo[:, k, t * P:(t + 1) * P]),
                                       (w_hi[j][:, k, col:GW], w_lo[j][:, k, col:GW]), k == 0, k == KC - 1)
                mm.then_inc(acc_done, 1)

            def turn_units(it, j, t, kind):
                col, units, has_v = content(kind, t)
                pe.wait_ge(cut_ready, item(it, j, t) + 1 + CR)
                pe.wait_ge(st_ready, item(it, j, t) + 1)
                for u in range(units):
                    mm = pe.transpose(banks[4 + 2 * (t % 2) + u // 4][:, (u % 4) * P:(u % 4 + 1) * P],
                                      cut[t % 2][:, u, :, :].rearrange("p a d -> p (a d)").bitcast(F32), ident[:])
                mm.then_inc(turned, 1)

            def turn(it, kinds):
                todo = [(j, t, kind) for j, kind in enumerate(kinds) for t in range(tiles(kind))]
                for i, (j, t, kind) in enumerate(todo):
                    accumulate(it, j, t, kind)
                    if i:
                        jj, tt, kk = todo[i - 1]
                        turn_units(it, jj, tt, kk)
                turn_units(it, j, t, kind)

            pe.sem_inc(turned, CR)
            with pe.Fori(0, LAST) as it:
                turn(it, LOOP_KINDS)
            turn(LAST, LAST_KINDS)

        @block.scalar
        def _(act):
            def weight_hi(group, slot, k, landed):
                act.wait_ge(w_in[slot], landed)
                act.activation(w_hi[slot][:, k, :], w_raw[slot][:, k, :], ACT.Copy).then_inc(w_hi_ready, 1)

            def copy_units(it, j, t, kind):
                col, units, has_v = content(kind, t)
                act.wait_ge(turned, item(it, j, t) + 1 + CR)
                act.wait_ge(st_out[t % 2], 16 * uses(it, j, t) + 16)
                b = 4 + 2 * (t % 2)
                n = min(units, 4)
                ins = act.activation(st[t % 2][:, 0:n, :], banks[b][:, 0:n * P].rearrange("p (u n) -> p u n", n=P), ACT.Copy)
                if units > 4:
                    ins = act.activation(st[t % 2][:, 4:units, :],
                                         banks[b + 1][:, 0:(units - 4) * P].rearrange("p (u n) -> p u n", n=P), ACT.Copy)
                ins.then_inc(st_ready, 1)

            def turn(it, kinds, more):
                todo = [(j, t, kind) for j, kind in enumerate(kinds) for t in range(tiles(kind))]
                for i, (j, t, kind) in enumerate(todo):
                    col, units, has_v = content(kind, t)
                    act.wait_ge(acc_done, item(it, j, t) + 1)
                    act.wait_ge(cut_ready, item(it, j, t) + 1)
                    act.wait_ge(v_out[t % 2], 16 * uses(it, j, t if kind == "kv" else 0) + 16)
                    act.activation(raw[t % 2][:, col:GW], banks[(2 * j + t) % 4][:, col:GW], ACT.Copy).then_inc(raw_ready, 1)
                    if (j == 0 or more) and t < KC:
                        weight_hi(it * 2 + j + 1, 1 - j, t, 16 * (it + j + 1))
                    if j == 1 and not more and t < 2:
                        act.wait_ge(keep["f_in"][t], 16)
                        act.activation(keep["f_hi"][t][:], keep["f_raw"][t][:], ACT.Copy).then_inc(f_hi_ready, 1)
                    if i:
                        jj, tt, kk = todo[i - 1]
                        copy_units(it, jj, tt, kk)
                copy_units(it, j, t, kind)

            act.sem_inc(raw_ready, 4)
            act.sem_inc(st_ready, CR)
            for s in range(2):
                act.sem_inc(st_out[s], 16)
                act.sem_inc(v_out[s], 16)
            for k in range(KC):
                weight_hi(0, 0, k, 16)
            with act.Fori(0, LAST) as it:
                turn(it, LOOP_KINDS, True)
            turn(LAST, LAST_KINDS, False)

        def weight_lo(eng, group, slot):
            for k in range(KC):
                eng.wait_ge(w_hi_ready, group * KC + k + 1)
                eng.tensor_tensor(w_lo[slot][:, k, :], w_raw[slot][:, k, :], w_hi[slot][:, k, :].bitcast(F32),
                                  ALU.subtract).then_inc(w_lo_ready, 1)

        @block.gpsimd
        def _(pool):
            pool.wait_ge(w_lo_ready, KC)
            weight_lo(pool, 1, 1)
            with pool.Fori(1, LAST + 1) as it:
                for j in range(2):
                    weight_lo(pool, it * 2 + j, j)
            for j in range(2):
                pool.wait_ge(f_hi_ready, j + 1)
                pool.tensor_tensor(keep["f_lo"][j][:], keep["f_raw"][j][:], keep["f_hi"][j][:].bitcast(F32), ALU.subtract)

        @block.vector
        def _(v):
            def cut_tile(ch, it, j, t, kind):
                col, units, has_v = content(kind, t)
                src, c = raw[t % 2], cut[t % 2]
                v.wait_ge(raw_ready, item(it, j, t) + 1 + 4)
                v.wait_ge(turned, item(it, j, t) + 1)
                x = src[:, col:col + units * HD].rearrange("p (u d) -> p u d", d=HD)
                if t < TL:
                    v.wait_ge(cut_ready, item(it, j, t) + CR)
                    cs = cosT[:, t:t + 1, :].to_broadcast([P, units, HD])
                    sn = sinT[:, t:t + 1, :].to_broadcast([P, units, HD])
                    ch.did(v.tensor_tensor(rot[:, 0:units, :], x, cs, ALU.mult))
                    ch.did(v.tensor_tensor(swp[:, 0:units, 0:HD:2], x[:, :, 1:HD:2], sn[:, :, 0:HD:2], ALU.mult))
                    ch.link(v.tensor_tensor(swp[:, 0:units, 1:HD:2], x[:, :, 0:HD:2], sn[:, :, 1:HD:2], ALU.mult))
                    x = rot[:, 0:units, :]
                    ch.link(v.tensor_tensor(x, x, swp[:, 0:units, :], ALU.add))
                ch.did(v.tensor_copy(c[:, 0:units, 0, :], x))
                ch.settle()
                v.tensor_tensor(c[:, 0:units, 1, :], x, c[:, 0:units, 0, :].bitcast(F32), ALU.subtract)\
                 .then_inc(cut_ready, 1)

            OWN = 2 * (5 * TL + (TT - TL))
            v.sem_inc(cut_ready, CR)
            weight_lo(v, 0, 0)
            v.wait_ge(table_in, 32)

            def turn(it, kinds):
                ch = Chain(v, dve, it * OWN)
                for j, kind in enumerate(kinds):
                    for t in range(tiles(kind)):
                        cut_tile(ch, it, j, t, kind)
                return ch.n

            with v.Fori(0, LAST) as it:
                assert turn(it, LOOP_KINDS) == OWN
            turn(LAST, LAST_KINDS)


def wide_product(pe, outs, stat, movs, first, last):
    sh, sl = stat
    for out, (mh, ml) in zip(outs, movs):
        pe.matmul(out, sh, mh, start=first, stop=False)
        pe.matmul(out, sh, ml, start=False, stop=False)
    for out, (mh, ml) in zip(outs, movs):
        mm = pe.matmul(out, sl, mh, start=False, stop=last)
    return mm


def features(nc, sem, banks, io, keep):
    h_hi, h_lo, psum = keep["h_hi"], keep["h_lo"], keep["psum"]
    silu_x, A2, B2, gate_row = keep["silu_x"], keep["A2"], keep["B2"], keep["gate_row"]
    G = len(POOL_WINDOWS)
    TILES = G + 3 * KC
    TURNS = 3 * KC // 2
    PAD = max(POOL_WINDOWS) // 2
    AC = P
    PIECES = 4 * D // AC
    A_TURNS = PIECES // 4
    with ExitStack() as ctx:
        sb = lambda n, s, d=F32: ctx.enter_context(nc.sbuf_tensor(n, s, d))
        w_raw, w_in = keep["f_raw"], keep["f_in"]
        w_hi, w_lo = keep["f_hi"], keep["f_lo"]
        gst = [sb(f"gst{j}", [P, HALF]) for j in range(2)]
        upad = sb("upad", [P, SEQ + 2 * PAD])
        acc = sb("acc", [P, 4 * D])
        WW = SEQ + 2 * PAD
        win = [acc[:, j * WW:(j + 1) * WW] for j in range(2)]
        inv, yb = acc[:, 2 * WW:2 * WW + SEQ], sb("yb", [P, SEQ])
        pl_hi, pl_lo = sb("pl_hi", [P, SEQ], F32R), sb("pl_lo", [P, SEQ], F32R)
        pw = sb("pw", [P, G, P])
        pw_hi, pw_lo = sb("pw_hi", [P, G, P], F32R), sb("pw_lo", [P, G, P], F32R)
        pscale = sb("pscale", [P, G])
        piece = [sb(f"piece{j}", [P, KC, AC]) for j in range(2)]
        brow, grow = (p[:].rearrange("p k n -> p (k n)") for p in piece)
        ones = sb("ones", [P, P])
        badaT, ngT = sb("badaT", [P, 6 * KC]), sb("ngT", [P, 4, KC])
        m2 = sb("m2", [P, 2 * KC])
        small_in, inv_in, row_in = sem("ft_small_in"), sem("ft_inv_in"), sem("ft_row_in")
        piece_in = [sem(f"ft_piece_in{j}") for j in range(2)]
        w_hi_ready, w_lo_ready, acc_done, taken = sem("ft_w_hi"), sem("ft_w_lo"), sem("ft_acc"), sem("ft_taken")
        gst_ready, gst_out = sem("ft_gst"), [sem(f"ft_gst_out{j}") for j in range(2)]
        upad_clear, u_ready, u_used, pooled, pool_done, yb_ready = (sem(f"ft_{n}") for n in
                                                        ("clear", "u", "u_used", "pooled", "pool_done", "yb"))
        yb_out, piece_used, ada_ready, dve = sem("ft_yb_out"), sem("ft_piece_used"), sem("ft_ada"), sem("ft_dve")
        pw_ready, rows_done, row_used = sem("ft_pw"), sem("ft_rows"), sem("ft_row_used")
        gates = io["gates"].rearrange("i m p n -> (i m) p n")
        block = ctx.enter_context(nc.Block())

        @block.sync
        def _(sp):
            for dst, src in ((pw, io["pool_w"]), (pscale, io["pool_scaleT"]), (badaT, io["b_adaT"]), (ngT, io["norm_gT"])):
                sp.dma_start(dst[:], src).then_inc(small_in, 16)

            def load_w(f, slot):
                sp.wait_ge(w_lo_ready, f - 1)
                sp.dma_start(w_raw[slot][:], io["w_feat"][f]).then_inc(w_in[slot], 16)

            def load_piece(q, slot):
                sp.wait_ge(piece_used, q + 1)
                sp.dma_start(piece[slot][:], io["w_ada"].rearrange("(k p) n -> p k n", p=P)
                             .rearrange("p k (a n) -> a p k n", n=AC)[2 * D // AC + q]).then_inc(piece_in[slot], 16)

            def store_gate(f):
                for n in range(NH):
                    sp.wait_ge(gst_ready, (f - G) * NH + n + 1)
                    sp.dma_start(gates[f - G][:, n * HALF:(n + 1) * HALF], gst[n][:]).then_inc(gst_out[n], 16)

            for g in range(G):
                if g:
                    sp.wait_ge(pooled, g)
                sp.dma_start(inv, io["inv_count"][g:g + 1, :].to_broadcast([P, SEQ])).then_inc(inv_in, 16)
                load_w(g + 2, g % 2)
                if g >= 1:
                    sp.wait_ge(yb_ready, g)
                    sp.dma_start(io["yb"][g - 1], yb[:]).then_inc(yb_out, 16)

            def turn(it, pieces, more):
                for j in range(2):
                    f = it * 2 + G + j
                    if more:
                        load_w(f + 2, j)
                    for q in range(2 * pieces):
                        load_piece((it - 1) * 4 + 2 * j + q, q)
                    store_gate(f)

            load_w(G + 2, 0)
            sp.wait_ge(yb_ready, G)
            sp.dma_start(io["yb"][G - 1], yb[:]).then_inc(yb_out, 16)
            store_gate(G)
            load_w(G + 3, 1)
            store_gate(G + 1)
            with sp.Fori(1, 1 + A_TURNS) as it:
                turn(it, 1, True)
            with sp.Fori(1 + A_TURNS, TURNS - 1) as it:
                turn(it, 0, True)
            load_head(io, sp, 0, keep["head0"], keep["head0_in"])
            sp.wait_ge(ada_ready, 1)
            for i in range(2):
                if i:
                    sp.wait_ge(row_used, 2)
                sp.dma_start(brow, io["b_ada"][0:1, (2 + 3 * i) * D:(3 + 3 * i) * D].to_broadcast([P, D])).then_inc(row_in, 16)
                sp.dma_start(grow, io["norm_g"][1 + 2 * i:2 + 2 * i, :].to_broadcast([P, D])).then_inc(row_in, 16)
            turn(TURNS - 1, 0, False)
            sp.wait_ge(row_used, 3)
            sp.dma_start(io["late_row"], upad[0:1, 0:D]).then_inc(yb_out, 16)
            for j in range(2):
                sp.wait_ge(keep["st_out"][j], keep["st_stored"])
            for n in range(NH):
                sp.wait_ge(gst_out[n], 16 * (3 * KC + 1))
            sp.wait_ge(yb_out, 16 * (G + 1))

        @block.tensor
        def _(pe):
            def tile(f, slot):
                pe.wait_ge(w_lo_ready, f + 1)
                pe.wait_ge(taken, f + 1)
                for k in range(KC):
                    mm = wide_product(pe, [banks[2 * slot + n][:, :] for n in range(NH)],
                                      (w_hi[slot][:, k, :], w_lo[slot][:, k, :]),
                                      [(h_hi[:, k, n * HALF:(n + 1) * HALF], h_lo[:, k, n * HALF:(n + 1) * HALF])
                                       for n in range(NH)], k == 0, k == KC - 1)
                mm.then_inc(acc_done, 1)

            def pool_tile(g):
                pe.wait_ge(pooled, g + 1)
                if g == 0:
                    pe.wait_ge(pw_ready, 1)
                else:
                    pe.wait_ge(yb_ready, g)
                wide_product(pe, [banks[4 + n][:, :] for n in range(NH)], (pw_hi[:, g, :], pw_lo[:, g, :]),
                             [(pl_hi[:, n * HALF:(n + 1) * HALF], pl_lo[:, n * HALF:(n + 1) * HALF])
                              for n in range(NH)], True, True).then_inc(pool_done, 1)

            pe.sem_inc(acc_done, 2)
            for f in range(G):
                tile(f, f % 2)
                if f:
                    pool_tile(f - 1)
            tile(G, 0)
            pool_tile(G - 1)
            tile(G + 1, 1)
            with pe.Fori(1, TURNS - 1) as it:
                for j in range(2):
                    tile(it * 2 + G + j, j)

            def row_sums(i, first):
                for n in range(NH):
                    mm = pe.matmul(banks[first + n], ones[:], acc[:, 3 * i * D + n * HALF:3 * i * D + (n + 1) * HALF],
                                   start=True, stop=True)
                mm.then_inc(rows_done, 1)

            pe.wait_ge(ada_ready, 1)
            for b in range(2 * KC):
                pe.matmul(banks[4][:, b:b + 1], acc[:, D + b * P:D + (b + 1) * P], ones[:, 0:1], start=True, stop=True)
            row_sums(0, 6)
            tile((TURNS - 1) * 2 + G, 0)
            pe.wait_ge(row_used, 1)
            row_sums(1, 4)
            tile((TURNS - 1) * 2 + G + 1, 1)

        @block.scalar
        def _(act):
            def weight_hi(f, slot, landed):
                act.wait_ge(w_in[slot], landed)
                act.wait_ge(acc_done, f + 1)
                act.activation(w_hi[slot][:], w_raw[slot][:], ACT.Copy).then_inc(w_hi_ready, 1)

            def gate(f, slot):
                act.wait_ge(acc_done, f + 3)
                for n in range(NH):
                    act.wait_ge(gst_out[n], 16 * (f - G) + 16)
                    ins = act.activation(gst[n][:], banks[2 * slot + n][:, :], ACT.Sigmoid)
                    ins.then_inc(gst_ready, 1)
                act.wait_ge(gst_ready, (f - G) * NH + NH)
                act.sem_inc(taken, 1)

            act.sem_inc(taken, 2)
            for n in range(NH):
                act.sem_inc(gst_out[n], 16)
            act.wait_ge(small_in, 64)
            act.activation(pw_hi[:], pw[:], ACT.Copy).then_inc(pw_ready, 1)
            act.wait_ge(upad_clear, 1)
            for g in range(G):
                act.wait_ge(acc_done, g + 3)
                if g:
                    act.wait_ge(u_used, g)
                act.activation(upad[:, PAD:PAD + SEQ], psum[:, 2 * HALF * (g % 2):2 * HALF * (g % 2 + 1)],
                               ACT.Copy).then_inc(u_ready, 1)
                act.wait_ge(u_ready, g + 1)
                act.sem_inc(taken, 1)
                weight_hi(g + 2, g % 2, 16 * ((g + 2) // 2 + 1))

            def turn(it, more):
                for j in range(2):
                    f = it * 2 + G + j
                    gate(f, j)
                    if more:
                        weight_hi(f + 2, j, 16 * (it + G // 2 + 2))

            with act.Fori(0, TURNS - 1) as it:
                turn(it, True)
            turn(TURNS - 1, False)

        def weight_lo(eng, f, slot):
            eng.wait_ge(w_hi_ready, f + 1)
            eng.tensor_tensor(w_lo[slot][:], w_raw[slot][:], w_hi[slot][:].bitcast(F32), ALU.subtract).then_inc(w_lo_ready, 1)

        @block.gpsimd
        def _(pool):
            with pool.Fori(1, TILES // 2) as it:
                for j in range(2):
                    weight_lo(pool, it * 2 + j, j)

        @block.vector
        def _(v):
            v.sem_inc(w_hi_ready, 2)
            v.sem_inc(w_lo_ready, 2)
            ch = Chain(v, dve)
            ch.did(v.memset(upad[:, 0:PAD], 0.0))
            ch.did(v.memset(upad[:, PAD + SEQ:], 0.0))
            ch.link(v.memset(ones[:], 1.0))
            v.sem_inc(upad_clear, 1)
            v.sem_inc(piece_used, 2)
            v.wait_ge(pw_ready, 1)
            v.tensor_tensor(pw_lo[:], pw[:], pw_hi[:].bitcast(F32), ALU.subtract).then_inc(pw_ready, 1)

            def branch(g):
                v.wait_ge(pool_done, g + 1)
                if g:
                    v.wait_ge(yb_out, 16 * g)
                v.tensor_scalar(yb[:], psum[:, 4 * HALF:6 * HALF], pscale[:, g:g + 1], None, ALU.mult).then_inc(yb_ready, 1)

            for g, w in enumerate(POOL_WINDOWS):
                v.wait_ge(u_ready, g + 1)
                src, width, step, i = upad, SEQ + 2 * PAD, 1, 0
                while step < w:
                    dst = win[i]
                    ch.link(v.tensor_tensor(dst[:, 0:width - step], src[:, 0:width - step], src[:, step:width], ALU.add))
                    src, width, step, i = dst, width - step, 2 * step, 1 - i
                other = win[i]
                v.wait_ge(inv_in, 16 * (g + 1))
                ch.link(v.tensor_tensor(other[:, 0:SEQ], src[:, PAD - w // 2:PAD - w // 2 + SEQ], inv, ALU.mult))
                ch.link(v.tensor_tensor(other[:, 0:SEQ], other[:, 0:SEQ], upad[:, PAD:PAD + SEQ], ALU.subtract))
                v.sem_inc(u_used, 1)
                if g:
                    branch(g - 1)
                ch.link(v.tensor_copy(pl_hi[:], other[:, 0:SEQ]))
                v.tensor_tensor(pl_lo[:], other[:, 0:SEQ], pl_hi[:].bitcast(F32), ALU.subtract).then_inc(pooled, 1)
                v.wait_ge(pooled, g + 1)
            branch(G - 1)

            n0 = ch.n
            with v.Fori(0, A_TURNS) as it:
                own = Chain(v, dve, it * (4 * (KC - 1)) + n0)
                for q in range(4):
                    out = acc[:].rearrange("p (a n) -> p a n", n=AC)[:, it * 4 + q, :]
                    v.wait_ge(piece_in[q % 2], it * 32 + 16 * (q // 2) + 16)
                    own.link(v.tensor_scalar(out, piece[q % 2][:, 0, :], silu_x[:, 0:1], None, ALU.mult))
                    for k in range(1, KC):
                        ins = v.scalar_tensor_tensor(out=out, in0=piece[q % 2][:, k, :], scalar=silu_x[:, k:k + 1], in1=out,
                                                     op0=ALU.mult, op1=ALU.add)
                        if k < KC - 1:
                            own.link(ins)
                    ins.then_inc(piece_used, 1)
                assert own.n == 4 * (KC - 1)
            v.wait_ge(piece_used, PIECES + 2)
            v.sem_inc(ada_ready, 1)
            v.wait_ge(rows_done, 1)
            fin = Chain(v, dve, n0 + A_TURNS * 4 * (KC - 1))
            fin.link(v.tensor_tensor(m2[:], banks[4][:, 0:2 * KC], badaT[:, 3 * KC:5 * KC], ALU.add))
            v.sem_inc(row_used, 1)
            fin.did(v.tensor_copy(B2[:], m2[:, 0:KC]))
            fin.did(v.scalar_tensor_tensor(out=A2[:], in0=m2[:, KC:2 * KC], scalar=1.0, in1=ngT[:, 2, :], op0=ALU.add,
                                           op1=ALU.mult))
            for i in range(2):
                v.wait_ge(rows_done, i + 1)
                v.wait_ge(row_in, 32 * (i + 1))
                out = (gate_row[:], upad[:, 0:D])[i]
                fin.link(v.tensor_tensor(out, psum[:, (6 - 2 * i) * HALF:(8 - 2 * i) * HALF], brow, ALU.add))
                v.tensor_tensor(out, out, grow, ALU.mult).then_inc(row_used, 1)


def load_head(io, sp, h, buffers, landed):
    q, k, ks, val = buffers
    src = io["stacks_da"][h]
    for dst, s in ((q[:], src[0:2, :, 0:SEQ]), (k[:], src[2:4])):
        sp.dma_start(dst.bitcast(F32), s.rearrange("s p n -> p s n")).then_inc(landed, 16)
    for a, b in ((0, HD), (HD, 0)):
        sp.dma_start(ks[a:a + HD].bitcast(F32), src[2:4, b:b + HD].rearrange("s p n -> p s n")).then_inc(landed, 16)
    sp.dma_start(val[:], io["vals"][h].rearrange("t p n -> p t n")).then_inc(landed, 16)


def window_buffers(keep):
    q, k, ks, val = keep["head0"]
    return (q, ks), k[:, 0, :], k[:, 1, :]


def load_window_qk(io, sp, kv, buffers, landed):
    qs, k_st, k_sw = buffers
    k = io["stacks_wa"][2 + kv]
    for dst, a, b in ((k_st, 0, 0), (k_st, HD, HD), (k_sw, 0, HD), (k_sw, HD, 0)):
        for d0, s0, w in ((0, SEQ, CTX), (CTX, 0, SEQ)):
            sp.dma_start(dst[a:a + HD, d0:d0 + w].bitcast(F32), k[b:b + HD, s0:s0 + w]).then_inc(landed, 16)
    for n in range(WA_GROUP):
        h = kv * WA_GROUP + n
        src = io["stacks_wa"][h - 6 if h >= 6 else h + 4]
        sp.dma_start(qs[n // 2][:, n % 2, 0:SEQ].bitcast(F32), src[:, 0:SEQ]).then_inc(landed, 16)



def diff(nc, sem, banks, io, keep):
    psum, ident, neg_lam, o, ss = keep["psum"], keep["ident"], keep["neg_lam"], keep["o"], keep["o_ss"]
    TILES = 2 * TL
    LAG_TURN, LAG_AV = 2, 3
    COLS = [(0, HALF), (HALF, HALF), (2 * HALF, TOK - 2 * HALF)]
    with ExitStack() as ctx:
        sb = lambda n, s, d=F32: ctx.enter_context(nc.sbuf_tensor(n, s, d))
        heads = [keep["head0"], (sb("q_st1", [P, 2, SEQ], F32R), sb("k_st1", [P, 2, TOK], F32R), sb("k_sw1", [P, 2, TOK], F32R),
                                 sb("val1", [P, TT, P]))]
        q_st, k_st, k_sw, val = zip(*heads)
        e = [[sb(f"e{b}{s}", [P, TOK]) for s in range(2)] for b in range(2)]
        a = [sb(f"a{b}", [P, TOK]) for b in range(2)]
        at = [sb(f"at{b}", [P, TT, P]) for b in range(2)]
        junk = sb("junk_d", [P, P])
        mx = sb("mx", [P, 2])
        neg_m = sb("neg_m", [P, 2, 2])
        sums = sb("sums", [P, 2, 2])
        rec = sb("rec", [P, 4, 2])
        c1 = sb("c1", [P, 2])
        head_in = [keep["head0_in"], sem("da_head_in1")]
        sc_done, neg_ready, exp_done = ([sem(f"da_{n}{s}") for s in range(2)] for n in ("sc", "neg", "exp"))
        a_ready, av_done, o_ready, sq_done, dve = sem("da_a"), sem("da_av"), sem("da_o"), sem("da_sq"), sem("da_dve")
        turned, free = ([sem(f"da_{n}{b}") for b in range(2)] for n in ("turned", "free"))

        RING = ("last", "low", "high")
        KEYS = {"low": range(0, 4), "high": range(4, 8), "last": range(8, TT)}
        STEPS = TILES + LAG_AV

        USES = (3 * TILES + 2) // 2

        def slot(it, i, what):
            n = 3 * (i - LAG_TURN) + RING.index(what)
            return n % 2, it * USES + n // 2

        block = ctx.enter_context(nc.Block())

        @block.sync
        def _(sp):
            load_head(io, sp, 1, heads[1], head_in[1])
            for j in range(2):
                sp.wait_ge(av_done, TL * (j + 1))
                load_head(io, sp, 2 + j, heads[j], head_in[j])
            sp.wait_ge(av_done, TL * 3)
            load_window_qk(io, sp, 0, window_buffers(keep), keep["qk_in"])

        @block.tensor
        def _(pe):
            def use(it, i, what):
                b, used = slot(it, i, what)
                pe.wait_ge(free[b], used + 1)
                return b, banks[6 + b]

            def scores(it, i):
                j, t = i // TL, i % TL
                if t == 0:
                    pe.wait_ge(head_in[j], 80 * it + 80)
                for s in range(2):
                    pe.wait_ge(exp_done[s], it * TILES + i + 1)
                    q = q_st[j][:, s, t * P:(t + 1) * P]
                    for c, (c0, w) in enumerate(COLS):
                        out = banks[3 * s + c][:, 0:w]
                        pe.matmul(out, q, k_st[j][:, s, c0:c0 + w], start=True, stop=False)
                        mm = pe.matmul(out, q, k_sw[j][:, s, c0:c0 + w], start=False, stop=True)
                    mm.then_inc(sc_done[s], 1)

            def turn(it, t, i, what):
                b, bank = use(it, i, what)
                for n, k in enumerate(KEYS[what]):
                    mm = pe.transpose(bank[:, n * P:(n + 1) * P], a[t % 2][:, k * P:(k + 1) * P], ident[:])
                return b, mm

            def products(t, bank):
                for k in range(TT):
                    mm = pe.matmul(bank[:, 2 * P:3 * P], at[t % 2][:, k, :], val[t // TL][:, k, :], start=(k == 0), stop=(k == TT - 1))
                return mm

            with pe.Fori(0, 2) as it:
                for i in range(STEPS):
                    t = i - LAG_TURN
                    if i < TILES:
                        scores(it, i)
                    if t >= 0:
                        if t < TILES:
                            pe.wait_ge(a_ready, it * TILES + t + 3)
                            b, mm = turn(it, t, i, "last")
                        else:
                            b, bank = use(it, i, "last")
                        if t >= 1:
                            for what in ("low", "high"):
                                bb, used = slot(it, i - 1, what)
                                pe.wait_ge(free[bb], used + 2)
                            mm = products(t - 1, banks[6 + b])
                            mm.then_inc(av_done, 1)
                            pe.wait_ge(av_done, it * TILES + t)
                            pe.sem_inc(turned[b], 1)
                        else:
                            mm.then_inc(turned[b], 1)
                    if 0 <= t < TILES:
                        for what in ("low", "high"):
                            b, mm = turn(it, t, i, what)
                            mm.then_inc(turned[b], 1)
                pe.sem_inc(turned[slot(it, STEPS - 1, "low")[0]], 1)

        @block.scalar
        def _(act):
            def exp(it, i, s):
                N = it * TILES + i
                act.wait_ge(neg_ready[s], N + 1)
                act.wait_ge(sc_done[s], N + 1)
                act.wait_ge(a_ready, N + 1)
                act.activation(e[i % 2][s][:], psum[:, 3 * s * HALF:3 * s * HALF + TOK], ACT.Exp, scale=SCALE,
                               bias=neg_m[:, i % 2, s:s + 1], accum_out=sums[:, i % 2, s:s + 1]).then_inc(exp_done[s], 1)

            def copy_out(it, i, what):
                b, used = slot(it, i, what)
                act.wait_ge(turned[b], used + 1)
                tiles, t = KEYS[what], i - LAG_TURN
                act.activation(at[t % 2][:, tiles[0]:tiles[-1] + 1, :],
                               banks[6 + b].rearrange("p (k n) -> p k n", n=P), ACT.Copy).then_inc(free[b], 1)

            def copy_last(it, i):
                b, used = slot(it, i, "last")
                t = i - LAG_TURN
                act.wait_ge(turned[b], used + 1)
                if t >= 1:
                    act.activation(o[:, bass.ds(it * TILES + (t - 1), 1), :].rearrange("p a n -> p (a n)"),
                                   banks[6 + b][:, 2 * P:3 * P], ACT.Copy, scale=rec[:, (t - 1) % 4, 0:1]).then_inc(o_ready, 1)
                if t < TILES:
                    act.activation(at[t % 2][:, 8:TT, :], banks[6 + b][:, 0:2 * P].rearrange("p (k n) -> p k n", n=P), ACT.Copy)\
                       .then_inc(free[b], 1)
                else:
                    act.wait_ge(o_ready, it * TILES + t)
                    act.sem_inc(free[b], 1)

            def square(it, t):
                col = it * TILES + t
                act.wait_ge(o_ready, it * TILES + t + 1)
                act.wait_ge(sq_done, it * TILES + t + 1)
                act.activation(junk[:], o[:, bass.ds(col, 1), :].rearrange("p a n -> p (a n)"), ACT.Square,
                               accum_out=ss[:, bass.ds(col, 1)]).then_inc(sq_done, 1)

            act.sem_inc(sq_done, 1)
            for s in range(2):
                act.sem_inc(exp_done[s], 1)
            with act.Fori(0, 2) as it:
                for i in range(STEPS):
                    if i < TILES:
                        exp(it, i, 0)
                    if i >= LAG_TURN:
                        copy_last(it, i)
                    if i < TILES:
                        exp(it, i, 1)
                    if LAG_TURN <= i < TILES + LAG_TURN:
                        copy_out(it, i, "low")
                        copy_out(it, i, "high")
                    if i >= LAG_AV:
                        square(it, i - LAG_AV)
                act.sem_inc(free[slot(it, STEPS - 1, "low")[0]], 1)

        @block.vector
        def _(v):
            def maximum(ch, it, i, s):
                v.wait_ge(sc_done[s], it * TILES + i + 1)
                ch.link(v.tensor_reduce(mx[:, s:s + 1], psum[:, 3 * s * HALF:3 * s * HALF + TOK], AX.X, ALU.max))
                v.tensor_scalar(neg_m[:, i % 2, s:s + 1], mx[:, s:s + 1], -SCALE, None, ALU.mult).then_inc(neg_ready[s], 1)

            def reciprocals(ch, it, i):
                for s in range(2):
                    v.wait_ge(exp_done[s], it * TILES + i + 2)
                ch.link(v.reciprocal(rec[:, i % 4, :], sums[:, i % 2, :]))
                ch.link(v.tensor_scalar(c1[:, i % 2:i % 2 + 1], rec[:, i % 4, 1:2], sums[:, i % 2, 0:1], neg_lam[:, 0:1],
                                        ALU.mult, ALU.mult))

            def combine(it, t):
                if t >= 2:
                    b, used = slot(it, t - 2 + LAG_TURN, "high")
                    v.wait_ge(turned[b], used + 1)
                v.scalar_tensor_tensor(out=a[t % 2][:], in0=e[t % 2][1][:], scalar=c1[:, t % 2:t % 2 + 1],
                                       in1=e[t % 2][0][:], op0=ALU.mult, op1=ALU.add).then_inc(a_ready, 1)

            for b in range(2):
                v.sem_inc(free[b], 1)
            v.sem_inc(a_ready, 2)
            OWN = 4 * TILES
            with v.Fori(0, 2) as it:
                ch = Chain(v, dve, it * OWN)
                for i in range(STEPS):
                    if i < TILES:
                        maximum(ch, it, i, 0)
                        maximum(ch, it, i, 1)
                    if 1 <= i < TILES + 1:
                        combine(it, i - 1)
                    if i < TILES:
                        reciprocals(ch, it, i)
                assert ch.n == OWN


def window(nc, sem, banks, io, keep):
    psum, ident, y_hi, y_lo = keep["psum"], keep["ident"], keep["y_hi"], keep["y_lo"]
    o_da, ss, sub_g = keep["o"], keep["o_ss"], keep["sub_g"]
    UN = 2 * TL
    BAND = 3 * P
    KEYS = CTX + BAND
    GROUPS = 4
    DA_STEPS = (7, 10, 13, 16)
    with ExitStack() as ctx:
        sb = lambda n, s, d=F32: ctx.enter_context(nc.sbuf_tensor(n, s, d))
        q_st, k_st, k_sw = window_buffers(keep)
        val = sb("wval", [P, TT, HD])
        e = [[sb(f"we{b}{s}", [P, KEYS]) for s in range(2)] for b in range(2)]
        pt = [sb(f"wpt{b}", [P, 2, KEYS // P, P]) for b in range(2)]
        o = [sb(f"wo{b}", [P, 2, HD]) for b in range(2)]
        ident_r, mask_r = sb("ident_r", [P, P], F32R), sb("mask_r", [P, BAND], F32R)
        sink, nsink = sb("sink", [P, WA_HEADS]), sb("nsink", [P, WA_HEADS])
        mx, neg_m, sums, es, rec = (sb("wmx", [P, 2]), sb("wneg_m", [P, 2, 2]), sb("wsums", [P, 2, 2]), sb("wes", [P, 2, 2]),
                                    sb("wrec", [P, 4, 2]))
        y_in = [sb(f"y_in{j}", [P, SEQ]) for j in range(2)]
        on = [sb(f"on{j}", [P, 4, P]) for j in range(2)]
        mask = on[1][:, 0:3, :].rearrange("p a n -> p (a n)")
        const_in, qk_in, v_in, y_landed = sem("wa_const_in"), keep["qk_in"], sem("wa_v_in"), [sem(f"wa_y_in{j}") for j in range(2)]
        const_ready, yb_hi_ready, yb_lo_ready = sem("wa_const"), sem("wa_yb_hi"), sem("wa_yb_lo")
        ss_ready, root_ready, rms_ready, on_ready, ya_hi_ready = (
            sem(f"wa_{n}") for n in ("ss", "root", "rms", "on", "ya_hi"))
        sc_done, neg_ready, exp_done = ([sem(f"wa_{n}{s}") for s in range(2)] for n in ("sc", "neg", "exp"))
        es_in_ready, es_ready, o_ready, yc_hi_ready, dve = (sem(f"wa_{n}") for n in ("es_in", "es", "o", "yc_hi", "dve"))
        turned, free = ([sem(f"wa_{n}{b}") for b in range(4)] for n in ("turned", "free"))

        def tiles_of(u):
            blk = u // 2
            return [0, 1] + [2 + b for b in range(max(blk - 1, 0), min(blk + 2, TL))]

        def squares(u):
            todo = [(s, k) for s in range(2) for k in range(len(tiles_of(u)))]
            return [todo[n:n + 4] for n in range(0, len(todo), 4)]

        STEPS = UN + 3
        ring = {}
        for i in range(STEPS):
            if 0 <= i - 2 < UN:
                ring["av", i - 2, 0] = len(ring)
            if 0 <= i - 1 < UN:
                for part in range(len(squares(i - 1))):
                    ring["turn", i - 1, part] = len(ring)
            if 0 <= i - 3 < UN:
                ring["out", i - 3, 0] = len(ring)
            if i in DA_STEPS:
                ring["da", DA_STEPS.index(i), 0] = len(ring)
        assert len(ring) % 4 == 0
        PER_BANK = len(ring) // 4

        def slot(kv, what, u, part=0):
            n = ring[what, u, part]
            return n % 4, kv * PER_BANK + n // 4

        def ya_part(part, kv, g):
            return part[0][:, bass.ds(kv * 2 + g // NH, 1), g % NH * HALF:(g % NH + 1) * HALF].rearrange("p a q -> p (a q)")

        block = ctx.enter_context(nc.Block())

        @block.sync
        def _(sp):
            def load_v(kv):
                v = io["vals"][DA_HEADS].rearrange("t p (g d) -> g p t d", g=WA_KV)[kv]
                sp.dma_start(val[:, 2:TT, :], v[:, 0:TL, :]).then_inc(v_in, 16)
                sp.dma_start(val[:, 0:2, :], v[:, TL:TT, :]).then_inc(v_in, 16)

            sp.dma_start(mask, io["mask"]).then_inc(const_in, 16)
            sp.dma_start(sink[:], io["wa_sink"].to_broadcast([P, WA_HEADS])).then_inc(const_in, 16)
            load_v(0)
            for j in range(2):
                sp.dma_start(keep["b_raw"][j][:], io["w_br"][j]).then_inc(keep["b_in"][j], 16)
            for n in range(BC):
                if n >= 2:
                    sp.wait_ge(yb_lo_ready, n - 1)
                sp.dma_start(y_in[n % 2][:], io["yb"][n]).then_inc(y_landed[n % 2], 16)
            for s in range(2):
                sp.wait_ge(sc_done[s], UN)
            load_window_qk(io, sp, 1, (q_st, k_st, k_sw), qk_in)
            b, used = slot(0, "av", UN - 1)
            sp.wait_ge(turned[b], used + 1)
            load_v(1)

        QK_DMAS, V_DMAS = 16 * (8 + WA_GROUP), 16 * 2

        @block.tensor
        def _(pe):
            def use(kv, what, u, part=0):
                b, used = slot(kv, what, u, part)
                pe.wait_ge(free[b], used + 1)
                return b, banks[4 + b]

            def scores(kv, u):
                blk, pair = u // 2, u % 2
                if u == 0:
                    pe.wait_ge(qk_in, QK_DMAS * kv + QK_DMAS)
                band = tiles_of(u)[2]
                width = (len(tiles_of(u)) - 2) * P
                for s in range(2):
                    pe.wait_ge(exp_done[s], kv * UN + u + 1)
                    q = q_st[pair][:, s, blk * P:(blk + 1) * P]
                    pe.matmul(banks[2 * s][:, CTX:HALF], q, k_st[:, 0:CTX], start=True, stop=False)
                    pe.matmul(banks[2 * s][:, CTX:HALF], q, k_sw[:, 0:CTX], start=False, stop=True)
                    out, at = banks[2 * s + 1][:, 0:width], slice(band * P, band * P + width)
                    pe.matmul(out, q, k_st[:, at], start=True, stop=False)
                    pe.matmul(out, q, k_sw[:, at], start=False, stop=False)
                    m0 = (band - 2 - (blk - 1)) * P
                    mm = pe.matmul(out, ident_r[:], mask_r[:, m0:m0 + width], start=False, stop=True)
                    mm.then_inc(sc_done[s], 1)

            def turn(kv, u):
                for s in range(2):
                    pe.wait_ge(exp_done[s], kv * UN + u + 2)
                for part, todo in enumerate(squares(u)):
                    b, bank = use(kv, "turn", u, part)
                    for n, (s, k) in enumerate(todo):
                        mm = pe.transpose(bank[:, n * P:(n + 1) * P], e[u % 2][s][:, k * P:(k + 1) * P], ident[:])
                    mm.then_inc(turned[b], 1)

            def products(kv, u):
                if u == 0:
                    pe.wait_ge(v_in, V_DMAS * kv + V_DMAS)
                for part in range(len(squares(u))):
                    b, used = slot(kv, "turn", u, part)
                    pe.wait_ge(free[b], used + 2)
                b, bank = use(kv, "av", u)
                tiles = tiles_of(u)
                for s in range(2):
                    for n, k in enumerate(tiles):
                        mm = pe.matmul(bank[:, s * HD:(s + 1) * HD], pt[u % 2][:, s, n, :], val[:, k, :], start=(n == 0),
                                       stop=(n == len(tiles) - 1))
                mm.then_inc(turned[b], 1)

            def out(kv, u):
                pe.wait_ge(o_ready, kv * UN + u + 1)
                b, bank = use(kv, "out", u)
                pe.transpose(bank[:, 0:P], o[u % 2][:].rearrange("p s d -> p (s d)"), ident[:]).then_inc(turned[b], 1)

            def turn_da(kv, g):
                pe.wait_ge(on_ready, kv * GROUPS + g + 1)
                b, bank = use(kv, "da", g)
                for n in range(4):
                    mm = pe.transpose(bank[:, n * P:(n + 1) * P], on[g % 2][:, n, :], ident[:])
                mm.then_inc(turned[b], 1)

            pe.wait_ge(const_ready, 2)
            with pe.Fori(0, WA_KV) as kv:
                for i in range(STEPS):
                    if i < UN:
                        scores(kv, i)
                    if 0 <= i - 2 < UN:
                        products(kv, i - 2)
                    if 0 <= i - 1 < UN:
                        turn(kv, i - 1)
                    if 0 <= i - 3 < UN:
                        out(kv, i - 3)
                    if i in DA_STEPS:
                        turn_da(kv, DA_STEPS.index(i))

        @block.scalar
        def _(act):
            def exp(kv, u, s):
                N = kv * UN + u
                keys = len(tiles_of(u)) * P
                act.wait_ge(neg_ready[s], N + 1)
                act.wait_ge(sc_done[s], N + 1)
                if u >= 2:
                    b, used = slot(kv, "turn", u - 2, len(squares(u - 2)) - 1)
                    act.wait_ge(turned[b], used + 1)
                act.activation(e[u % 2][s][:, 0:keys], psum[:, 2 * s * HALF + CTX:2 * s * HALF + CTX + keys], ACT.Exp, scale=SCALE,
                               bias=neg_m[:, u % 2, s:s + 1], accum_out=sums[:, u % 2, s:s + 1]).then_inc(exp_done[s], 1)

            def sinks(kv, u):
                act.wait_ge(es_in_ready, kv * UN + u + 1)
                act.activation(es[:, u % 2, :], es[:, u % 2, :], ACT.Exp).then_inc(es_ready, 1)

            def copy_out(kv, u):
                b, used = slot(kv, "turn", u, 0)
                act.wait_ge(turned[b], used + 1)
                act.activation(pt[u % 2][:, 0, 0:4, :], banks[4 + b].rearrange("p (k n) -> p k n", n=P), ACT.Copy)\
                   .then_inc(free[b], 1)

            def output_hi(kv, u):
                b, used = slot(kv, "out", u)
                act.wait_ge(turned[b], used + 1)
                dst = y_hi[2][:, bass.ds(kv * 2 + u % 2, 1), u // 2 * P:(u // 2 + 1) * P].rearrange("p a q -> p (a q)")
                act.activation(dst, banks[4 + b][:, 0:P], ACT.Copy).then_inc(yc_hi_ready, 1)

            act.wait_ge(ss_ready, 1)
            act.activation(ss[:], ss[:], ACT.Sqrt).then_inc(root_ready, 1)
            act.wait_ge(const_in, 32)
            act.activation(mask_r[:], mask, ACT.Copy).then_inc(const_ready, 1)
            act.activation(ident_r[:], ident[:], ACT.Copy).then_inc(const_ready, 1)
            for s in range(2):
                act.sem_inc(exp_done[s], 1)

            def da_hi(kv, g):
                b, used = slot(kv, "da", g)
                act.wait_ge(turned[b], used + 1)
                act.activation(ya_part(y_hi, kv, g), banks[4 + b], ACT.Copy, scale=sub_g[:, 0:1]).then_inc(ya_hi_ready, 1)

            with act.Fori(0, WA_KV) as kv:
                for i in range(STEPS):
                    if i < UN:
                        exp(kv, i, 0)
                        exp(kv, i, 1)
                    if 0 <= i - 1 < UN:
                        copy_out(kv, i - 1)
                    if i < UN:
                        sinks(kv, i)
                    if 0 <= i - 3 < UN:
                        output_hi(kv, i - 3)
                    if i in DA_STEPS:
                        da_hi(kv, DA_STEPS.index(i))

        @block.gpsimd
        def _(pool):
            for n in range(BC):
                pool.wait_ge(y_landed[n % 2], 16 * (n // 2 + 1))
                nc.gpsimd.tensor_copy(y_hi[1][:, n, :], y_in[n % 2][:]).then_inc(yb_hi_ready, 1)
                pool.wait_ge(yb_hi_ready, n + 1)
                nc.gpsimd.tensor_tensor(y_lo[1][:, n, :], y_in[n % 2][:], y_hi[1][:, n, :].bitcast(F32),
                                        ALU.subtract).then_inc(yb_lo_ready, 1)
            pool.wait_ge(rms_ready, 1)
            pool.wait_ge(const_ready, 2)
            with pool.Fori(0, WA_KV) as kv:
                for g in range(GROUPS):
                    pool.wait_ge(ya_hi_ready, kv * GROUPS + g + 1)
                    col = kv * (4 * GROUPS) + 4 * g
                    nc.gpsimd.tensor_tensor(on[g % 2][:], o_da[:, bass.ds(col, 4), :],
                                            ss[:, bass.ds(col, 4)].unsqueeze(2).to_broadcast([P, 4, P]), ALU.mult)\
                      .then_inc(on_ready, 1)

        @block.vector
        def _(v):
            def maximum(ch, kv, u, s):
                keys = len(tiles_of(u)) * P
                v.wait_ge(sc_done[s], kv * UN + u + 1)
                ch.link(v.tensor_reduce(mx[:, s:s + 1], psum[:, 2 * s * HALF + CTX:2 * s * HALF + CTX + keys], AX.X, ALU.max))
                v.tensor_scalar(neg_m[:, u % 2, s:s + 1], mx[:, s:s + 1], -SCALE,
                                nsink[:, bass.ds(kv * WA_GROUP + 2 * (u % 2) + s, 1)], ALU.mult, ALU.min)\
                 .then_inc(neg_ready[s], 1)

            def sinks(kv, u):
                for s in range(2):
                    v.wait_ge(neg_ready[s], kv * UN + u + 1)
                v.tensor_tensor(es[:, u % 2, :], neg_m[:, u % 2, :], sink[:, bass.ds(kv * WA_GROUP + 2 * (u % 2), 2)], ALU.add)\
                 .then_inc(es_in_ready, 1)

            def reciprocals(ch, kv, u):
                for s in range(2):
                    v.wait_ge(exp_done[s], kv * UN + u + 2)
                v.wait_ge(es_ready, kv * UN + u + 1)
                ch.link(v.tensor_tensor(sums[:, u % 2, :], sums[:, u % 2, :], es[:, u % 2, :], ALU.add))
                ch.link(v.reciprocal(rec[:, u % 4, :], sums[:, u % 2, :]))

            def output(kv, u):
                b, used = slot(kv, "av", u)
                v.wait_ge(turned[b], used + 1)
                v.tensor_tensor(o[u % 2][:], banks[4 + b][:, 0:P].rearrange("p (s d) -> p s d", s=2),
                                rec[:, u % 4, :].unsqueeze(2).to_broadcast([P, 2, HD]), ALU.mult).then_inc(o_ready, 1)
                v.wait_ge(o_ready, kv * UN + u + 1)
                v.sem_inc(free[b], 1)

            def copy_out(kv, u, part):
                b, used = slot(kv, "turn", u, part)
                v.wait_ge(turned[b], used + 1)
                for n0, s, k0, cnt in split_runs(squares(u)[part]):
                    ins = v.tensor_copy(pt[u % 2][:, s, k0:k0 + cnt, :],
                                        banks[4 + b][:, n0 * P:(n0 + cnt) * P].rearrange("p (k n) -> p k n", n=P))
                ins.then_inc(free[b], 1)

            def output_lo(kv, u):
                b, used = slot(kv, "out", u)
                v.wait_ge(yc_hi_ready, kv * UN + u + 1)
                at = (slice(None), bass.ds(kv * 2 + u % 2, 1), slice(u // 2 * P, (u // 2 + 1) * P))
                v.tensor_tensor(y_lo[2][at].rearrange("p a q -> p (a q)"), banks[4 + b][:, 0:P],
                                y_hi[2][at].rearrange("p a q -> p (a q)").bitcast(F32), ALU.subtract).then_inc(free[b], 1)

            def da_lo(kv, g):
                b, used = slot(kv, "da", g)
                v.wait_ge(ya_hi_ready, kv * GROUPS + g + 3)
                v.scalar_tensor_tensor(out=ya_part(y_lo, kv, g), in0=banks[4 + b], scalar=sub_g[:, 0:1],
                                       in1=ya_part(y_hi, kv, g).bitcast(F32), op0=ALU.mult, op1=ALU.subtract).then_inc(free[b], 1)

            ch = Chain(v, dve)
            v.tensor_scalar(ss[:], ss[:], 1.0 / DA_V, EPS, ALU.mult, ALU.add).then_inc(ss_ready, 1)
            v.wait_ge(root_ready, 1)
            v.reciprocal(ss[:], ss[:]).then_inc(rms_ready, 1)
            v.sem_inc(ya_hi_ready, 2)
            v.wait_ge(const_in, 32)
            ch.link(v.tensor_scalar(nsink[:], sink[:], -1.0, None, ALU.mult))
            for b in range(4):
                v.sem_inc(free[b], 1)
            OWN = 4 * UN
            with v.Fori(0, WA_KV) as kv:
                ch = Chain(v, dve, kv * OWN + 1)
                for i in range(STEPS):
                    if i < UN:
                        maximum(ch, kv, i, 0)
                        maximum(ch, kv, i, 1)
                        sinks(kv, i)
                    if 0 <= i - 2 < UN:
                        output(kv, i - 2)
                    if 0 <= i - 1 < UN:
                        for part in range(1, len(squares(i - 1))):
                            copy_out(kv, i - 1, part)
                    if 0 <= i - 3 < UN:
                        output_lo(kv, i - 3)
                    if i in DA_STEPS:
                        da_lo(kv, DA_STEPS.index(i))
                    if i < UN:
                        reciprocals(ch, kv, i)
                assert ch.n == OWN


def split_runs(todo):
    runs = []
    for n, (s, k) in enumerate(todo):
        if runs and runs[-1][1] == s:
            runs[-1][3] += 1
        else:
            runs.append([n, s, k, 1])
    return runs


def merge(nc, sem, banks, io, keep):
    y_hi, y_lo, m = keep["y_hi"], keep["y_lo"], keep["m"]
    psum = keep["psum"]
    WN = 3 * BC * P
    with ExitStack() as ctx:
        sb = lambda n, s, d=F32: ctx.enter_context(nc.sbuf_tensor(n, s, d))
        w_raw, w_in = keep["b_raw"], keep["b_in"]
        w_hi = [sb(f"b_hi{j}", [P, 3, BC, P], F32R) for j in range(2)]
        w_lo = [sb(f"b_lo{j}", [P, 3, BC, P], F32R) for j in range(2)]
        g = [sb(f"b_g{j}", [P, 3, SEQ]) for j in range(2)]
        tmp = sb("b_tmp", [P, SEQ])
        g_in = [sem(f"mg_g_in{j}") for j in range(2)]
        w_hi_ready, w_lo_ready, acc_done, m_ready, taken, dve = (sem(f"mg_{n}") for n in
                                                                ("w_hi", "w_lo", "acc", "m", "taken", "dve"))
        gates = io["gates"].rearrange("i m p n -> m p i n")
        TURNS = KC // 2
        block = ctx.enter_context(nc.Block())

        @block.sync
        def _(sp):
            for j in range(2):
                sp.dma_start(g[j][:], gates[j]).then_inc(g_in[j], 16)
            with sp.Fori(0, TURNS - 1) as it:
                for j in range(2):
                    sp.wait_ge(w_lo_ready, it * 2 + j + 1)
                    sp.wait_ge(m_ready, it * 2 + j + 1)
                    sp.dma_start(w_raw[j][:], io["w_br"][it * 2 + j + 2]).then_inc(w_in[j], 16)
                    sp.dma_start(g[j][:], gates[it * 2 + j + 2]).then_inc(g_in[j], 16)
            for j in range(2):
                sp.dma_start(keep["stage"][j][:], io["w_out"][j * P:(j + 1) * P, :]).then_inc(keep["o_in"][j], 16)

        @block.tensor
        def _(pe):
            def tile(t, j, phase):
                pe.wait_ge(w_lo_ready, t + 1)
                for i in range(3):
                    r = (3 * phase + i) % 4
                    pe.wait_ge(taken, t * 3 + i + 1)
                    for k in range(BC):
                        mm = wide_product(pe, [banks[2 * r + n] for n in range(NH)],
                                          (w_hi[j][:, i, k, :], w_lo[j][:, i, k, :]),
                                          [(y_hi[i][:, k, n * HALF:(n + 1) * HALF], y_lo[i][:, k, n * HALF:(n + 1) * HALF])
                                           for n in range(NH)], k == 0, k == BC - 1)
                    mm.then_inc(acc_done, 1)

            with pe.Fori(0, TURNS // 2) as it:
                for q in range(4):
                    tile(it * 4 + q, q % 2, q)

        @block.scalar
        def _(act):
            with act.Fori(0, TURNS) as it:
                for j in range(2):
                    act.wait_ge(w_in[j], it * 16 + 16)
                    act.wait_ge(acc_done, (it * 2 + j) * 3 + 1)
                    act.activation(w_hi[j][:], w_raw[j][:], ACT.Copy).then_inc(w_hi_ready, 1)

        def weight_lo(eng, t, j):
            eng.wait_ge(w_hi_ready, t + 1)
            eng.tensor_tensor(w_lo[j][:], w_raw[j][:], w_hi[j][:].bitcast(F32), ALU.subtract).then_inc(w_lo_ready, 1)

        @block.gpsimd
        def _(pool):
            pool.wait_ge(w_lo_ready, 2)
            with pool.Fori(1, TURNS) as it:
                for j in range(2):
                    weight_lo(pool, it * 2 + j, j)

        @block.vector
        def _(v):
            v.sem_inc(taken, 4)
            v.sem_inc(acc_done, 7)
            for j in range(2):
                weight_lo(v, j, j)
            OWN = 4
            with v.Fori(0, TURNS // 2) as it:
                ch = Chain(v, dve, it * OWN)
                for q in range(4):
                    t = it * 4 + q
                    out = m[:, t, :]
                    v.wait_ge(g_in[q % 2], (it * 2 + q // 2) * 16 + 16)
                    for i in range(3):
                        r = (3 * q + i) % 4
                        v.wait_ge(acc_done, t * 3 + i + 8)
                        ins = v.tensor_tensor(out if i == 0 else tmp[:], psum[:, 2 * r * HALF:2 * (r + 1) * HALF],
                                              g[q % 2][:, i, :], ALU.mult)
                        ins.then_inc(taken, 1)
                        v.wait_ge(taken, t * 3 + i + 5)
                        if i == 1:
                            ch.link(v.tensor_tensor(out, out, tmp[:], ALU.add))
                        if i == 2:
                            v.tensor_tensor(out, out, tmp[:], ALU.add).then_inc(m_ready, 1)
                            v.wait_ge(m_ready, t + 1)
                assert ch.n == OWN


def residual(nc, sem, banks, io, keep):
    psum, ident, m, h_hi, h_lo = keep["psum"], keep["ident"], keep["m"], keep["h2_hi"], keep["h2_lo"]
    A2, B2, row = keep["A2"], keep["B2"], keep["gate_row"]
    RAW = 4
    with ExitStack() as ctx:
        sb = lambda n, s, d=F32: ctx.enter_context(nc.sbuf_tensor(n, s, d))
        w_in = keep["o_in"] + [sem(f"rs_w_in{j}") for j in (2, 3)]
        w_hi, w_lo = sb("o_hi", [P, KC, D], F32R), sb("o_lo", [P, KC, D], F32R)
        m_hi, m_lo = keep["cut_hi"], keep["cut_lo"]
        x = [sb(f"o_x{j}", [P, D]) for j in range(2)]
        junk, xn = sb("o_junk", [P, D], BF16), sb("o_xn", [P, D])
        full = sb("o_full", [P, KC, P])
        w_raw = [w[:] for w in keep["stage"]] + [xn[:], full[:].rearrange("p k q -> p (k q)")]
        ss, rs = sb("o_ss", [P, 2, 2]), sb("o_rs", [P, 2, 2])
        x_in, x_out = ([sem(f"rs_{n}{j}") for j in range(2)] for n in ("x_in", "x_out"))
        w_hi_ready, w_lo_ready, m_hi_ready, m_lo_ready = (sem(f"rs_{n}") for n in ("w_hi", "w_lo", "m_hi", "m_lo"))
        acc_done, ss_ready, mean_ready, root_ready, taken = (sem(f"rs_{n}") for n in ("acc", "ss", "mean", "root", "taken"))
        x_ready, xn_ready, turned, full_ready, h_ready, dve = (sem(f"rs_{n}") for n in ("x", "xn", "turned", "full", "h", "dve"))
        block = ctx.enter_context(nc.Block())

        @block.sync
        def _(sp):
            for k in range(2, KC):
                if k >= RAW:
                    sp.wait_ge(w_lo_ready, k - RAW + 1)
                sp.dma_start(w_raw[k % RAW], io["w_out"][k * P:(k + 1) * P, :]).then_inc(w_in[k % RAW], 16)
            for j in range(2):
                sp.wait_ge(w_lo_ready, KC - RAW + 1 + j)
                sp.dma_start(w_raw[j].rearrange("p (k c) -> p k c", c=P), io["w_ff"][0, j]).then_inc(keep["i_in"][j], 16)
            for t in range(TL):
                if t >= 2:
                    sp.wait_ge(x_out[t % 2], 16 * (t // 2))
                    sp.wait_ge(xn_ready, t - 1)
                sp.dma_start(x[t % 2][:], io["x"][t * P:(t + 1) * P, :]).then_inc(x_in[t % 2], 16)
                if t:
                    sp.wait_ge(x_ready, t)
                    sp.dma_start(io["x_mid"][t - 1], x[(t - 1) % 2][:]).then_inc(x_out[(t - 1) % 2], 16)
            sp.wait_ge(x_ready, TL)
            sp.dma_start(io["x_mid"][TL - 1], x[(TL - 1) % 2][:]).then_inc(x_out[(TL - 1) % 2], 16)
            for j in range(2):
                sp.wait_ge(x_out[j], 16 * TL // 2)

        def turned_x(t, k):
            return banks[4 + 2 * (t % 2) + k // 4][:, (k % 4) * P:(k % 4 + 1) * P]

        @block.tensor
        def _(pe):
            def turn(t):
                pe.wait_ge(xn_ready, t + 1)
                if t >= 2:
                    pe.wait_ge(full_ready, KC * (t - 1))
                for k in range(KC):
                    mm = pe.transpose(turned_x(t, k), xn[:, k * P:(k + 1) * P], ident[:])
                mm.then_inc(turned, 1)

            for t in range(TL):
                pe.wait_ge(m_lo_ready, t + 1)
                if t >= 2:
                    pe.wait_ge(taken, t - 1)
                for k in range(KC):
                    if t == 0:
                        pe.wait_ge(w_lo_ready, k + 1)
                    for n in range(NH):
                        mm = parts_product(pe, banks[2 * (t % 2) + n], (m_hi[t % 2][:, k, :], m_lo[t % 2][:, k, :]),
                                           (w_hi[:, k, n * HALF:(n + 1) * HALF], w_lo[:, k, n * HALF:(n + 1) * HALF]),
                                           k == 0, k == KC - 1)
                mm.then_inc(acc_done, 1)
                if t:
                    turn(t - 1)
            turn(TL - 1)

        @block.scalar
        def _(act):
            def cut_m(t):
                if t >= 2:
                    act.wait_ge(acc_done, t - 1)
                act.activation(m_hi[t % 2][:], m[:, :, t * P:(t + 1) * P], ACT.Copy).then_inc(m_hi_ready, 1)

            def cut_ff(j):
                act.wait_ge(acc_done, TL - 1 + j)
                act.wait_ge(keep["i_in"][j], 16)
                act.activation(m_hi[j][:], w_raw[j].rearrange("p (k c) -> p k c", c=P), ACT.Copy).then_inc(m_hi_ready, 1)

            def modulate(t):
                act.wait_ge(turned, t + 1)
                if t:
                    act.wait_ge(h_ready, t)
                for k in range(KC if t < TL - 1 else KC // 2):
                    act.activation(full[:, k, :], turned_x(t, k), ACT.Identity, scale=A2[:, k:k + 1],
                                   bias=B2[:, k:k + 1]).then_inc(full_ready, 1)

            for k in range(KC):
                act.wait_ge(w_in[k % RAW], 16 * (k // RAW + 1))
                act.activation(w_hi[:, k, :], w_raw[k % RAW], ACT.Copy).then_inc(w_hi_ready, 1)
            cut_m(1)
            for t in range(TL):
                acc = psum[:, 2 * (t % 2) * HALF:2 * (t % 2 + 1) * HALF]
                act.wait_ge(acc_done, t + 1)
                if t:
                    act.wait_ge(ss_ready, 2 * t)
                act.activation(junk[:], acc, ACT.Square, accum_out=ss[:, t % 2, 0:1]).then_inc(ss_ready, 1)
                act.wait_ge(mean_ready, 2 * t + 1)
                act.activation(rs[:, t % 2, 0:1], ss[:, t % 2, 0:1], ACT.Sqrt).then_inc(root_ready, 1)
                if t + 2 < TL:
                    cut_m(t + 2)
                elif t + 2 == TL:
                    cut_ff(0)
                if t:
                    modulate(t - 1)
                act.wait_ge(x_ready, t + 1)
                act.wait_ge(ss_ready, 2 * t + 1)
                act.activation(junk[:], x[t % 2][:], ACT.Square, accum_out=ss[:, t % 2, 1:2]).then_inc(ss_ready, 1)
                act.wait_ge(mean_ready, 2 * t + 2)
                act.activation(rs[:, t % 2, 1:2], ss[:, t % 2, 1:2], ACT.Sqrt).then_inc(root_ready, 1)
            cut_ff(1)
            modulate(TL - 1)

        @block.gpsimd
        def _(pool):
            def cut_m(t):
                pool.wait_ge(m_hi_ready, t + 1)
                nc.gpsimd.tensor_tensor(m_lo[t % 2][:], m[:, :, t * P:(t + 1) * P], m_hi[t % 2][:].bitcast(F32),
                                        ALU.subtract).then_inc(m_lo_ready, 1)
            pool.wait_ge(m_lo_ready, 1)
            for t in range(1, TL):
                cut_m(t)
            for j in range(2):
                pool.wait_ge(m_hi_ready, TL + j + 1)
                nc.gpsimd.tensor_tensor(m_lo[j][:], w_raw[j].rearrange("p (k c) -> p k c", c=P), m_hi[j][:].bitcast(F32),
                                        ALU.subtract).then_inc(m_lo_ready, 1)

        @block.vector
        def _(v):
            ch = Chain(v, dve)

            def h_parts(t):
                v.wait_ge(full_ready, KC * (t + 1))
                at = (slice(None), slice(None), slice(t * P, (t + 1) * P))
                ch.link(v.tensor_copy(h_hi[at], full[:]))
                v.tensor_tensor(h_lo[at], full[:], h_hi[at].bitcast(F32), ALU.subtract).then_inc(h_ready, 1)

            v.tensor_copy(m_hi[0][:], m[:, :, 0:P]).then_inc(m_hi_ready, 1)
            v.wait_ge(m_hi_ready, 1)
            v.tensor_tensor(m_lo[0][:], m[:, :, 0:P], m_hi[0][:].bitcast(F32), ALU.subtract).then_inc(m_lo_ready, 1)
            for k in range(KC):
                v.wait_ge(w_hi_ready, k + 1)
                v.tensor_tensor(w_lo[:, k, :], w_raw[k % RAW], w_hi[:, k, :].bitcast(F32), ALU.subtract).then_inc(w_lo_ready, 1)
            for t in range(TL):
                acc = psum[:, 2 * (t % 2) * HALF:2 * (t % 2 + 1) * HALF]
                root = lambda i: rs[:, t % 2, i:i + 1]
                v.wait_ge(ss_ready, 2 * t + 1)
                v.tensor_scalar(ss[:, t % 2, 0:1], ss[:, t % 2, 0:1], 1.0 / D, EPS, ALU.mult, ALU.add).then_inc(mean_ready, 1)
                v.wait_ge(root_ready, 2 * t + 1)
                ch.link(v.reciprocal(root(0), root(0)))
                if t:
                    v.wait_ge(turned, t)
                ch.link(v.scalar_tensor_tensor(out=xn[:], in0=acc, scalar=root(0), in1=row[:], op0=ALU.mult, op1=ALU.mult))
                v.sem_inc(taken, 1)
                v.wait_ge(x_in[t % 2], 16 * (t // 2 + 1))
                v.tensor_tensor(x[t % 2][:], x[t % 2][:], xn[:], ALU.add).then_inc(x_ready, 1)
                v.wait_ge(ss_ready, 2 * t + 2)
                v.tensor_scalar(ss[:, t % 2, 1:2], ss[:, t % 2, 1:2], 1.0 / D, EPS, ALU.mult, ALU.add).then_inc(mean_ready, 1)
                v.wait_ge(root_ready, 2 * t + 2)
                ch.link(v.reciprocal(root(1), root(1)))
                v.wait_ge(x_ready, t + 1)
                v.tensor_scalar(xn[:], x[t % 2][:], root(1), None, ALU.mult).then_inc(xn_ready, 1)
                if t:
                    h_parts(t - 1)
            v.wait_ge(turned, TL)
            v.wait_ge(h_ready, TL - 1)
            for k in range(KC // 2, KC):
                v.tensor_scalar(full[:, k, :], turned_x(TL - 1, k), A2[:, k:k + 1], B2[:, k:k + 1], ALU.mult,
                                ALU.add).then_inc(full_ready, 1)
            h_parts(TL - 1)


def ffn_in(nc, sem, banks, io, keep):
    psum, h_hi, h_lo, f = keep["psum"], keep["h2_hi"], keep["h2_lo"], keep["f"]
    DEPTH = 4
    TURNS = 2 * FC // DEPTH
    with ExitStack() as ctx:
        sb = lambda n, s, d=F32: ctx.enter_context(nc.sbuf_tensor(n, s, d))
        w_raw = [w[:].rearrange("p (k c) -> p k c", c=P) for w in keep["stage"]]
        w_hi, w_lo = keep["cut_hi"], keep["cut_lo"]
        act_g = [sb(f"i_act{j}", [P, HALF]) for j in range(2)]
        w_in = keep["i_in"]
        w_hi_ready, w_lo_ready, acc_done, silu_ready, f_ready = (sem(f"fi_{n}") for n in ("w_hi", "w_lo", "acc", "silu", "f"))
        w_ff = io["w_ff"]
        block = ctx.enter_context(nc.Block())

        @block.sync
        def _(sp):
            with sp.Fori(1, FC) as m:
                for j in range(2):
                    sp.wait_ge(w_lo_ready, m * 2 + j - 1)
                    sp.dma_start(w_raw[j], w_ff[m, j]).then_inc(w_in[j], 16)
            for j in range(2):
                sp.wait_ge(w_lo_ready, 2 * FC - 1 + j)
                sp.dma_start(keep["stage"][j][:], io["w_ffn_out"][j * P:(j + 1) * P, :]).then_inc(keep["u_in"][j], 16)

        @block.tensor
        def _(pe):
            with pe.Fori(0, TURNS) as it:
                for b in range(DEPTH):
                    pe.wait_ge(w_lo_ready, it * DEPTH + b + 1)
                    if b % 2 == 0:
                        pe.wait_ge(f_ready, it * DEPTH + b + 1)
                    for k in range(KC):
                        mm = wide_product(pe, [banks[2 * b + n] for n in range(NH)],
                                          (w_hi[b % 2][:, k, :], w_lo[b % 2][:, k, :]),
                                          [(h_hi[:, k, n * HALF:(n + 1) * HALF], h_lo[:, k, n * HALF:(n + 1) * HALF])
                                           for n in range(NH)], k == 0, k == KC - 1)
                    mm.then_inc(acc_done, 1)

        @block.scalar
        def _(act):
            def weight_hi(b, slot, landed):
                act.wait_ge(w_in[slot], landed)
                act.wait_ge(acc_done, b + 1)
                act.activation(w_hi[slot][:], w_raw[slot], ACT.Copy).then_inc(w_hi_ready, 1)

            def silu(it, b):
                act.wait_ge(acc_done, it * DEPTH + b + 3)
                for n in range(NH):
                    act.wait_ge(f_ready, it * DEPTH + b + n + 3)
                    act.activation(act_g[n][:], banks[2 * b + n], ACT.Silu).then_inc(silu_ready, 1)

            def turn(it, more):
                for b in range(DEPTH):
                    if b % 2 == 0:
                        silu(it, b)
                    if b < 2 or more:
                        weight_hi(it * DEPTH + b + 2, b % 2, (it * 2 + b // 2 + 1) * 16 + 16)

            with act.Fori(0, TURNS - 1) as it:
                turn(it, True)
            turn(TURNS - 1, False)

        def weight_lo(eng, b, slot):
            eng.wait_ge(w_hi_ready, b + 1)
            eng.tensor_tensor(w_lo[slot][:], w_raw[slot], w_hi[slot][:].bitcast(F32), ALU.subtract).then_inc(w_lo_ready, 1)

        @block.gpsimd
        def _(pool):
            with pool.Fori(1, FC) as m:
                for j in range(2):
                    weight_lo(pool, m * 2 + j, j)

        @block.vector
        def _(v):
            v.sem_inc(w_hi_ready, 2)
            v.sem_inc(w_lo_ready, 2)
            v.sem_inc(f_ready, 4)
            v.sem_inc(acc_done, 2)
            with v.Fori(0, TURNS) as it:
                for b in range(1, DEPTH, 2):
                    v.wait_ge(acc_done, it * DEPTH + b + 3)
                    for n in range(NH):
                        v.wait_ge(silu_ready, it * DEPTH + b + n)
                        v.tensor_tensor(f[:, it * 2 + b // 2, n * HALF:(n + 1) * HALF], banks[2 * b + n], act_g[n][:],
                                        ALU.mult).then_inc(f_ready, 1)


def ffn_out(nc, sem, banks, io, keep):
    psum, f, w_raw, w_in = keep["psum"], keep["f"], keep["stage"], keep["u_in"]
    T = 4
    BUFS = 4
    HEAD = 2
    LOOP = (FC - 4 - HEAD) // BUFS
    with ExitStack() as ctx:
        sb = lambda n, s, d=F32: ctx.enter_context(nc.sbuf_tensor(n, s, d))
        w_hi, w_lo = ([sb(f"u_{n}{j}", [P, D], F32R) for j in range(BUFS)] for n in ("hi", "lo"))
        f_hi, f_lo = ([sb(f"uf_{n}{j}", [P, HALF], F32R) for j in range(BUFS)] for n in ("hi", "lo"))
        y = [sb(f"u_y{t}", [P, D]) for t in range(T)]
        x = [sb(f"u_x{t}", [P, D]) for t in range(T)]
        row = sb("late_row", [P, D])
        junk = sb("u_junk", [P, D], BF16)
        ss = sb("u_ss", [P, 2 * T])
        x_in, row_in = [sem(f"fo_x_in{t}") for t in range(T)], sem("fo_row_in")
        w_hi_ready, w_lo_ready, f_hi_ready, f_lo_ready, acc_k, acc_done = (
            sem(f"fo_{n}") for n in ("w_hi", "w_lo", "f_hi", "f_lo", "acc_k", "acc"))
        ss_ready, mean_ready, root_ready, y_ready, out_ready, stored, dve = (
            sem(f"fo_{n}") for n in ("ss", "mean", "root", "y", "out", "stored", "dve"))
        block = ctx.enter_context(nc.Block())

        def halves(eng, step, between):
            for c in range(NH):
                for k in range(HEAD):
                    step(c, k, k)
                if c:
                    between(c - 1)
                with eng.Fori(0, LOOP) as it:
                    for q in range(BUFS):
                        step(c, it * BUFS + (HEAD + q), HEAD + q)
                for k in range(HEAD + LOOP * BUFS, FC):
                    step(c, k, k)
            between(NH - 1)

        def place(c, k, q):
            return k + c * FC, (q + c * FC) % BUFS

        @block.sync
        def _(sp):
            sp.dma_start(row[:], io["late_row"].to_broadcast([P, D])).then_inc(row_in, 16)

            def load_x(c, t):
                if c:
                    sp.wait_ge(out_ready, (c - 1) * T + t + 1)
                sp.dma_start(x[t][:], io["x_mid"][c * T + t]).then_inc(x_in[t], 16)

            def load_w(c, k, q):
                j = (q + c * FC) % 2
                sp.wait_ge(w_lo_ready, k + (c * FC + 1))
                sp.dma_start(w_raw[j][:], w_out[k + 2 if q < FC - 2 else k + 2 - FC]).then_inc(w_in[j], 16)

            def store(c):
                for t in range(T):
                    sp.wait_ge(out_ready, c * T + t + 1)
                    sp.dma_start(io["out"][(c * T + t) * P:(c * T + t + 1) * P, :], y[t][:]).then_inc(stored, 16)
                    if c + 1 < NH:
                        load_x(c + 1, t)

            w_out = io["w_ffn_out"].rearrange("(k p) n -> k p n", p=P)
            for t in range(T):
                load_x(0, t)
            with sp.Fori(0, (FC - 2) // 2) as it:
                for q in range(2):
                    load_w(0, it * 2 + q, q)
            for k in range(FC - 2, FC):
                load_w(0, k, k)
            for k in range(4):
                load_w(1, k, k)
            store(0)
            with sp.Fori(2, (FC - 2) // 2) as it:
                for q in range(2):
                    load_w(1, it * 2 + q, q)
            store(1)
            sp.wait_ge(stored, 16 * NH * T)

        @block.tensor
        def _(pe):
            def tile(c, q, t, j):
                for n in range(NH):
                    mm = parts_product(pe, banks[2 * t + n],
                                       (f_hi[j][:, t * P:(t + 1) * P], f_lo[j][:, t * P:(t + 1) * P]),
                                       (w_hi[j][:, n * HALF:(n + 1) * HALF], w_lo[j][:, n * HALF:(n + 1) * HALF]),
                                       q == 0, q == FC - 1)
                return mm

            def step(c, k, q):
                s, j = place(c, k, q)
                if q == FC - 1:
                    return
                pe.wait_ge(w_lo_ready, s + 1)
                pe.wait_ge(f_lo_ready, s + 1)
                if q == FC - 2:
                    pe.wait_ge(w_lo_ready, s + 2)
                    pe.wait_ge(f_lo_ready, s + 2)
                    for t in range(T):
                        tile(c, q, t, j)
                        tile(c, q + 1, t, (j + 1) % BUFS).then_inc(acc_done, 1)
                    pe.wait_ge(acc_done, (c + 1) * T)
                    pe.sem_inc(acc_k, 2)
                    return
                for t in range(T):
                    if c and q == 0:
                        pe.wait_ge(y_ready, (c - 1) * T + t + 1)
                    mm = tile(c, q, t, j)
                mm.then_inc(acc_k, 1)

            halves(pe, step, lambda c: None)

        @block.scalar
        def _(act):
            def cut(c, k, q):
                s, j = place(c, k, q)
                S = q + c * FC
                act.wait_ge(w_in[S % 2], (s - S) * 8 + 16 * (S // 2 + 1))
                act.wait_ge(acc_k, s + 1)
                act.activation(w_hi[j][:], w_raw[S % 2][:], ACT.Copy).then_inc(w_hi_ready, 1)
                act.activation(f_hi[j][:], f[:, k, c * HALF:(c + 1) * HALF], ACT.Copy).then_inc(f_hi_ready, 1)

            def norms(c):
                for t in range(T):
                    n = c * T + t
                    act.wait_ge(acc_done, n + 1)
                    if n:
                        act.wait_ge(ss_ready, n)
                    act.activation(junk[:], psum[:, 2 * t * HALF:2 * (t + 1) * HALF], ACT.Square,
                                   accum_out=ss[:, n:n + 1]).then_inc(ss_ready, 1)
                    act.wait_ge(mean_ready, n + 1)
                    act.activation(ss[:, n:n + 1], ss[:, n:n + 1], ACT.Sqrt).then_inc(root_ready, 1)

            act.sem_inc(acc_k, BUFS)
            halves(act, cut, norms)

        @block.gpsimd
        def _(pool):
            def cut(c, k, q):
                s, j = place(c, k, q)
                pool.wait_ge(f_hi_ready, s + 1)
                nc.gpsimd.tensor_tensor(f_lo[j][:], f[:, k, c * HALF:(c + 1) * HALF], f_hi[j][:].bitcast(F32),
                                        ALU.subtract).then_inc(f_lo_ready, 1)

            def add(c):
                for t in range(T):
                    n = c * T + t
                    pool.wait_ge(y_ready, n + 1)
                    pool.wait_ge(x_in[t], 16 * (c + 1))
                    nc.gpsimd.tensor_tensor(y[t][:], y[t][:], x[t][:], ALU.add).then_inc(out_ready, 1)

            halves(pool, cut, add)

        @block.vector
        def _(v):
            def cut(c, k, q):
                s, j = place(c, k, q)
                v.wait_ge(w_hi_ready, s + 1)
                v.tensor_tensor(w_lo[j][:], w_raw[(q + c * FC) % 2][:], w_hi[j][:].bitcast(F32), ALU.subtract)\
                 .then_inc(w_lo_ready, 1)

            ch = Chain(v, dve)

            def scale(c):
                v.wait_ge(row_in, 16)
                for t in range(T):
                    n = c * T + t
                    one = ss[:, n:n + 1]
                    v.wait_ge(ss_ready, n + 1)
                    v.tensor_scalar(one, one, 1.0 / D, EPS, ALU.mult, ALU.add).then_inc(mean_ready, 1)
                    v.wait_ge(root_ready, n + 1)
                    ch.link(v.reciprocal(one, one))
                    if c:
                        v.wait_ge(stored, 16 * T * c)
                    v.scalar_tensor_tensor(out=y[t][:], in0=psum[:, 2 * t * HALF:2 * (t + 1) * HALF], scalar=one, in1=row[:],
                                           op0=ALU.mult, op1=ALU.mult).then_inc(y_ready, 1)

            halves(v, cut, scale)


def tables():
    f = np.float32
    rows = SEQ // GRID_W
    row = np.repeat(np.arange(rows, dtype=f), GRID_W)
    col = np.tile(np.arange(GRID_W, dtype=f), rows)
    n_freq = HD // 4
    inv = (f(ROPE_THETA) ** (-np.arange(n_freq, dtype=f) / f(n_freq))).astype(f)
    ang = np.concatenate([row[:, None] * inv, col[:, None] * inv], axis=-1).astype(f)
    cos, sin = np.cos(ang).astype(f), np.sin(ang).astype(f)
    cos2 = np.repeat(cos, 2, axis=1)
    sin2 = np.stack([-sin, sin], axis=-1).reshape(SEQ, HD)
    turn = lambda a: np.ascontiguousarray(a.reshape(TL, P, HD).transpose(1, 0, 2))
    q, j = np.arange(P)[:, None], np.arange(P)[None, :]
    mask = np.zeros((P, 3, P), f)
    mask[:, 0, :] = np.where(j >= q, 0.0, MASKED)
    mask[:, 2, :] = np.where(j <= q, 0.0, MASKED)
    t = np.arange(SEQ)
    inv_count = np.stack([1.0 / (np.clip(t + w - w // 2, 0, SEQ) - np.clip(t - w // 2, 0, SEQ)) for w in POOL_WINDOWS])
    return {"cosT": turn(cos2), "sinT": turn(sin2), "ident": np.eye(P, dtype=f), "mask": mask.reshape(P, 3 * P),
            "inv_count": inv_count.astype(f)}


def lay_out(x, c, ctx, c_ctx, w_ada, b_ada, norm_g, w_in, da_lambda, da_subln_g, pool_w, pool_scale, wa_sink,
            w_branch, w_out, w_ffn_in, w_ffn_out):
    a = lambda v: np.ascontiguousarray(v)
    w = np.asarray(w_in)[0]
    q0, k0, v0, u0 = 0, 512, 1024, 1536
    qw0, kw0, vw0, g0 = 2048, 2560, 2688, 2816
    groups = [[(q0 + h * P, P), (k0 + h * P, P), (v0 + h * P, P)] for h in range(DA_HEADS)]
    groups += [[(qw0 + 6 * HD, P), (kw0, P), (vw0, P)], [(qw0, GW)]]
    chunks = lambda m: m.reshape(m.shape[0] // P, P, -1).transpose(1, 0, 2)
    w_tok = a(np.stack([chunks(np.concatenate([w[:, s:s + n] for s, n in g], axis=1)) for g in groups]))
    feat = np.concatenate([w[:, u0:u0 + BW], w[:, g0:]], axis=1)
    w_feat = a(feat.reshape(KC, P, -1, P).transpose(2, 1, 0, 3))
    w_br = a(np.asarray(w_branch)[0].reshape(3, BC, P, KC, P).transpose(3, 2, 0, 1, 4))
    w_ff = a(np.asarray(w_ffn_in)[0].reshape(KC, P, 2, FC, P).transpose(3, 2, 1, 0, 4))
    cT = a(np.stack([np.asarray(c)[0], np.asarray(c_ctx)]).reshape(2, KC, P).transpose(2, 0, 1))
    return {
        "x": a(np.asarray(x)[0]), "ctx": a(np.asarray(ctx)[0]), "cT": cT,
        "w_ada": a(np.asarray(w_ada)[0]), "b_adaT": a(np.asarray(b_ada)[0].reshape(6 * KC, P).T), "b_ada": a(b_ada),
        "norm_gT": a(np.asarray(norm_g)[0].reshape(4, KC, P).transpose(2, 0, 1)), "norm_g": a(np.asarray(norm_g)[0]),
        "w_tok": w_tok, "w_feat": w_feat, "da_lambda": a(np.asarray(da_lambda)[0].reshape(1, -1)),
        "sub_g": a(np.asarray(da_subln_g)[0].reshape(P, 1)), "pool_w": a(np.asarray(pool_w)[0].transpose(1, 0, 2)),
        "pool_scaleT": a(np.asarray(pool_scale)[0].reshape(BC, P).T), "wa_sink": a(np.asarray(wa_sink)),
        "w_br": w_br, "w_out": a(np.asarray(w_out)[0]), "w_ff": w_ff, "w_ffn_out": a(np.asarray(w_ffn_out)[0]),
    }


SCRATCH = {"stacks_da": [DA_HEADS, 4, P, TOK], "stacks_wa": [10, P, TOK], "vals": [DA_HEADS + 1, TT, P, P],
           "gates": [3, KC, P, SEQ], "yb": [BC, P, SEQ], "x_mid": [TL, P, D], "late_row": [1, D]}


def program(nc, io, upto=99):
    with ExitStack() as ctx:
        lasting = lambda name: ctx.enter_context(nc.semaphore(name))
        taken = []

        def sem(name):
            taken.append(nc.alloc_semaphore(name=name))
            return taken[-1]

        tensor = lambda stack, n, s, d=F32, side="left": stack.enter_context(nc.sbuf_tensor(n, s, d, side=side))
        psum = ctx.enter_context(nc.psum_tensor("psum", [P, 8 * HALF], F32))
        banks = [psum[:, i * HALF:(i + 1) * HALF] for i in range(8)]
        keep = {"psum": psum, "silu_x": tensor(ctx, "silu_x", [P, KC]), "ident": tensor(ctx, "ident", [P, P]),
                "neg_lam": tensor(ctx, "neg_lam", [P, 1]), "sub_g": tensor(ctx, "sub_g_sb", [P, 1]),
                "gate_row": tensor(ctx, "gate_row", [P, D]),
                "A2": tensor(ctx, "A2", [P, KC]), "B2": tensor(ctx, "B2", [P, KC])}
        with ExitStack() as first:
            keep["h_hi"] = tensor(first, "h_hi", [P, KC, TOK], F32R)
            keep["h_lo"] = tensor(first, "h_lo", [P, KC, TOK], F32R)
            with ExitStack() as pj:
                keep["w_raw"] = [tensor(pj, f"w_raw{j}", [P, KC, GW], F32, "right") for j in range(2)]
                keep["w_in"] = [sem(f"pj_w_in{j}") for j in range(2)]
                prepare(nc, sem, banks, io, keep)
                keep["f_raw"] = [tensor(first, f"f_raw{j}", [P, KC, P]) for j in range(2)]
                keep["f_in"] = [sem(f"ft_w_in{j}") for j in range(2)]
                for n in ("f_hi", "f_lo"):
                    keep[n] = [tensor(first, f"{n}{j}", [P, KC, P], F32R) for j in range(2)]
                keep["st"] = [tensor(first, f"st{j}", [P, UNITS, P], F32R) for j in range(2)]
                keep["st_out"] = [sem(f"pj_st_out{j}") for j in range(2)]
                if upto >= 2:
                    project(nc, sem, banks, io, keep)
            attention = ctx.enter_context(ExitStack())
            keep["head0"] = [tensor(attention, n, shape, d, "right") for n, shape, d in
                             (("q_st0", [P, 2, SEQ], F32R), ("k_st0", [P, 2, TOK], F32R), ("k_sw0", [P, 2, TOK], F32R),
                              ("val0", [P, TT, P], F32))]
            keep["head0_in"], keep["qk_in"] = lasting("da_head_in0"), lasting("wa_qk_in")
            if upto >= 3:
                features(nc, sem, banks, io, keep)
        if upto < 4:
            return
        keep["o"] = tensor(attention, "o", [P, DA_HEADS * TL, P], F32, "right")
        keep["o_ss"] = tensor(attention, "o_squares", [P, DA_HEADS * TL], F32, "right")
        diff(nc, sem, banks, io, keep)
        if upto < 5:
            return
        nc.clear_and_free_semaphores(taken)
        nc.all_engine_barrier()
        keep["stage"] = [tensor(ctx, f"stage{j}", [P, D]) for j in range(2)]
        for n in ("b_in", "o_in", "i_in", "u_in"):
            keep[n] = [sem(f"{n}{j}") for j in range(2)]
        with ExitStack() as ys, ExitStack() as ms:
            keep["b_raw"] = [tensor(ys, f"b_raw{j}", [P, 3, BC, P]) for j in range(2)]
            for part in ("hi", "lo"):
                keep[f"y_{part}"] = [tensor(ys, f"y_{part}{i}", [P, BC, SEQ], F32R) for i in range(3)]
            window(nc, sem, banks, io, keep)
            attention.close()
            keep["m"] = tensor(ms, "m", [P, KC, SEQ], F32, "right")
            if upto >= 6:
                merge(nc, sem, banks, io, keep)
            ys.close()
            with ExitStack() as h2:
                keep["h2_hi"] = tensor(h2, "h2_hi", [P, KC, SEQ], F32R)
                keep["h2_lo"] = tensor(h2, "h2_lo", [P, KC, SEQ], F32R)
                for n in ("cut_hi", "cut_lo"):
                    keep[n] = [tensor(h2, f"{n}{j}", [P, KC, P], F32R) for j in range(2)]
                if upto >= 7:
                    residual(nc, sem, banks, io, keep)
                ms.close()
                keep["f"] = tensor(ctx, "f", [P, FC, SEQ], F32, "right")
                if upto >= 8:
                    ffn_in(nc, sem, banks, io, keep)
        if upto >= 9:
            ffn_out(nc, sem, banks, io, keep)


def kernel(**inputs):
    import concourse.bacc as bacc
    from concourse.bass_utils import run_bass_kernel_spmd

    laid = lay_out(**inputs)
    laid.update(tables())
    nc = bacc.Bacc("TRN2", target_bir_lowering=False, num_devices=1)
    io = {k: nc.dram_tensor(f"in_{k}", a.shape, mybir.dt.from_np(a.dtype), kind="ExternalInput").ap()
          for k, a in laid.items()}
    for k, shape in SCRATCH.items():
        io[k] = nc.dram_tensor(f"{k}_dram", shape, F32, kind="Internal").ap()
    io["out"] = nc.dram_tensor("out", [SEQ, D], F32, kind="ExternalOutput").ap()
    program(nc, io)
    result = run_bass_kernel_spmd(nc, [{f"in_{k}": a for k, a in laid.items()}], core_ids=[0])
    return result.results[0]["out"].reshape(1, SEQ, D)
```
